# Optimizing a Trainium2 kernel written in Bass

```python
import jax, jax.numpy as jnp
from jax import lax
import numpy as np

D_MODEL = 1024
BATCH = 1
SEQ = 1024
DEPTH = 1

D_MIX = D_MODEL
D_CONV = D_MIX // 2
CONV_GROUPS = 8
CONV_WIDTH = 31
D_HGRN = D_MIX - D_CONV
HGRN_HEADS = 4
HGRN_HEAD_DIM = D_HGRN // HGRN_HEADS
HGRN_CHUNK = 64
D_IN = 2 * D_CONV + 4 * D_HGRN
PEER_HEADS = 8
PEER_KEY_DIM = 256
PEER_N_KEYS = 128
PEER_N_EXPERTS = PEER_N_KEYS * PEER_N_KEYS
PEER_TOPK = 16
PEER_BLOCK = 128
EPS = 1e-6

kernel_name = "hybrid_conv_hgrn2_peer_block"

def rmsnorm(x, g):
    xf = x.astype(jnp.float32)
    xf = xf * lax.rsqrt(jnp.mean(xf * xf, axis=-1, keepdims=True) + EPS)
    return (xf * g.astype(jnp.float32)).astype(x.dtype)

def conformer_conv(a, gate, conv_w, conv_b, norm_g, norm_b):
    bsz, s, _ = a.shape
    h = a * jax.nn.sigmoid(gate)
    h = lax.conv_general_dilated(
        h, conv_w[:, None, :].astype(h.dtype), window_strides=(1,),
        padding=[(CONV_WIDTH - 1, 0)],
        dimension_numbers=('NWC', 'WIO', 'NWC'),
        feature_group_count=D_CONV) + conv_b.astype(h.dtype)
    hf = h.astype(jnp.float32).reshape(bsz, s, CONV_GROUPS, D_CONV // CONV_GROUPS)
    mu = jnp.mean(hf, axis=-1, keepdims=True)
    var = jnp.mean(jnp.square(hf - mu), axis=-1, keepdims=True)
    hf = ((hf - mu) * lax.rsqrt(var + EPS)).reshape(bsz, s, D_CONV)
    hf = hf * norm_g.astype(jnp.float32) + norm_b.astype(jnp.float32)
    return jax.nn.silu(hf).astype(a.dtype)

def _hgrn2_chunk(state, inp):
    q, k, v, log_f = inp
    b = jnp.cumsum(log_f, axis=2)
    inter = jnp.einsum('bhtk,bhkv->bhtv', q * jnp.exp(b), state)
    tri = jnp.tril(jnp.ones((HGRN_CHUNK, HGRN_CHUNK), dtype=bool))
    diff = b[:, :, :, None, :] - b[:, :, None, :, :]
    decay = jnp.exp(jnp.where(tri[:, :, None], diff, -jnp.inf))
    scores = jnp.einsum('bhtk,bhsk,bhtsk->bhts', q, k, decay)
    intra = jnp.einsum('bhts,bhsv->bhtv', scores, v)
    b_last = b[:, :, -1, :]
    state = (jnp.exp(b_last)[..., None] * state
             + jnp.einsum('bhsk,bhsv->bhkv', k * jnp.exp(b_last[:, :, None, :] - b), v))
    return state, inter + intra

def hgrn2(q_in, f_in, i_in, g_in, lb, norm_g):
    bsz, s, _ = q_in.shape
    shp = (bsz, s, HGRN_HEADS, HGRN_HEAD_DIM)
    lbh = lb.reshape(HGRN_HEADS, HGRN_HEAD_DIM)
    z = f_in.astype(jnp.float32).reshape(shp)
    f = lbh + (1.0 - lbh) * jax.nn.sigmoid(z)
    log_f = jnp.log(f)
    k = (1.0 - lbh) * jax.nn.sigmoid(-z)
    q = jax.nn.silu(q_in.astype(jnp.float32)).reshape(shp)
    v = i_in.astype(jnp.float32).reshape(shp)
    nc = s // HGRN_CHUNK

    def to_chunks(t):
        return t.reshape(bsz, nc, HGRN_CHUNK, HGRN_HEADS, HGRN_HEAD_DIM).transpose(1, 0, 3, 2, 4)

    state0 = jnp.zeros((bsz, HGRN_HEADS, HGRN_HEAD_DIM, HGRN_HEAD_DIM), jnp.float32)
    _, o = lax.scan(_hgrn2_chunk, state0,
                    (to_chunks(q), to_chunks(k), to_chunks(v), to_chunks(log_f)))
    o = o.transpose(1, 0, 3, 2, 4).reshape(shp)
    o = o * lax.rsqrt(jnp.mean(o * o, axis=-1, keepdims=True) + EPS)
    o = o.reshape(bsz, s, D_HGRN) * norm_g.astype(jnp.float32)
    o = o * jax.nn.silu(g_in.astype(jnp.float32))
    return o.astype(q_in.dtype)

def peer(xn, w_query, sub_keys, u_tab, v_tab):
    bsz, s, d = xn.shape
    xt = xn.reshape(-1, d)
    t = xt.shape[0]
    q = (xt @ w_query).reshape(t, PEER_HEADS, 2, PEER_KEY_DIM // 2)
    sc = jnp.einsum('thpd,hpnd->thpn', q, sub_keys).astype(jnp.float32)
    s1, i1 = lax.top_k(sc[:, :, 0], PEER_TOPK)
    s2, i2 = lax.top_k(sc[:, :, 1], PEER_TOPK)
    cand = (s1[..., :, None] + s2[..., None, :]).reshape(t, PEER_HEADS, PEER_TOPK * PEER_TOPK)
    top_s, ci = lax.top_k(cand, PEER_TOPK)
    experts = (jnp.take_along_axis(i1, ci // PEER_TOPK, axis=-1) * PEER_N_KEYS
               + jnp.take_along_axis(i2, ci % PEER_TOPK, axis=-1))
    gate = jax.nn.softmax(top_s, axis=-1).astype(xn.dtype)
    nb = t // PEER_BLOCK

    def block(args):
        xb, eb, gb = args
        u = u_tab[eb]
        act = jax.nn.gelu(jnp.einsum('thkd,td->thk', u, xb), approximate=False)
        return jnp.einsum('thk,thkd->td', gb * act, v_tab[eb])

    y = lax.map(block, (xt.reshape(nb, PEER_BLOCK, d),
                        experts.reshape(nb, PEER_BLOCK, PEER_HEADS, PEER_TOPK),
                        gate.reshape(nb, PEER_BLOCK, PEER_HEADS, PEER_TOPK)))
    return y.reshape(bsz, s, d)

def setup_inputs(seed: int = 0) -> dict:
    key = jax.random.key(seed)
    ks = jax.random.split(key, 16)
    f32 = jnp.float32
    nrm = lambda k, shp, sc: jax.random.normal(k, shp, f32) * sc
    return {
        "x": jax.random.normal(ks[0], (BATCH, SEQ, D_MODEL), f32),
        "norm_mix_g": 1.0 + nrm(ks[1], (DEPTH, D_MODEL), 0.02),
        "w_in": nrm(ks[2], (DEPTH, D_MODEL, D_IN), D_MODEL ** -0.5),
        "conv_w": nrm(ks[3], (DEPTH, CONV_WIDTH, D_CONV), CONV_WIDTH ** -0.5),
        "conv_b": nrm(ks[4], (DEPTH, D_CONV), 0.02),
        "conv_norm_g": 1.0 + nrm(ks[5], (DEPTH, D_CONV), 0.02),
        "conv_norm_b": nrm(ks[6], (DEPTH, D_CONV), 0.02),
        "hgrn_lb_logits": nrm(ks[7], (DEPTH + 1, D_HGRN), 0.1),
        "hgrn_norm_g": 1.0 + nrm(ks[8], (DEPTH, D_HGRN), 0.02),
        "w_out": nrm(ks[9], (DEPTH, D_MIX, D_MODEL), D_MIX ** -0.5),
        "norm_ffn_g": 1.0 + nrm(ks[10], (DEPTH, D_MODEL), 0.02),
        "peer_w_query": nrm(ks[11], (DEPTH, D_MODEL, PEER_HEADS * PEER_KEY_DIM), D_MODEL ** -0.5),
        "peer_sub_keys": nrm(ks[12], (DEPTH, PEER_HEADS, 2, PEER_N_KEYS, PEER_KEY_DIM // 2),
                             (PEER_KEY_DIM // 2) ** -0.5),
        "peer_u": nrm(ks[13], (DEPTH, PEER_N_EXPERTS, D_MODEL), D_MODEL ** -0.5),
        "peer_v": nrm(ks[14], (DEPTH, PEER_N_EXPERTS, D_MODEL), 0.5),
        "final_norm_g": 1.0 + nrm(ks[15], (D_MODEL,), 0.02),
    }

def reference(x, norm_mix_g, w_in, conv_w, conv_b, conv_norm_g, conv_norm_b, hgrn_lb_logits,
              hgrn_norm_g, w_out, norm_ffn_g, peer_w_query, peer_sub_keys, peer_u, peer_v,
              final_norm_g):
    lb_all = jnp.cumsum(jax.nn.softmax(hgrn_lb_logits.astype(jnp.float32), axis=0), axis=0)
    splits = [D_CONV, 2 * D_CONV, 2 * D_CONV + D_HGRN, 2 * D_CONV + 2 * D_HGRN,
              2 * D_CONV + 3 * D_HGRN]
    h = x
    for l in range(DEPTH):
        xn = rmsnorm(h, norm_mix_g[l])
        proj = xn @ w_in[l]
        a, a_gate, qh, fh, ih, gh = jnp.split(proj, splits, axis=-1)
        y_conv = conformer_conv(a, a_gate, conv_w[l], conv_b[l], conv_norm_g[l], conv_norm_b[l])
        y_hgrn = hgrn2(qh, fh, ih, gh, lb_all[l], hgrn_norm_g[l])
        h = h + jnp.concatenate([y_conv, y_hgrn], axis=-1) @ w_out[l]
        h = h + peer(rmsnorm(h, norm_ffn_g[l]), peer_w_query[l], peer_sub_keys[l],
                     peer_u[l], peer_v[l])
    return rmsnorm(h, final_norm_g)


_drawn_inputs = setup_inputs


def setup_inputs(seed=0):
    import zlib

    import numpy as np

    out = dict(_drawn_inputs(seed))
    spreads = {}
    factors = {}
    for name, (base, spread) in spreads.items():
        noise = np.random.default_rng([zlib.crc32(name.encode()), seed]).standard_normal(out[name].shape)
        drawn = base * np.exp(spread * noise) if base else spread * noise
        out[name] = __import__('jax').numpy.asarray(drawn.astype(out[name].dtype))
    for name, factor in factors.items():
        out[name] = (out[name] * factor).astype(out[name].dtype)
    return out
```

```python
from contextlib import ExitStack

import concourse.bass as bass
from concourse import mybir
from concourse.bass import ds

P = 128
T = 1024
D = 1024
TB = T // P
KC = D // P
HALF = 512
NH = T // HALF
CG = 4
TAPS = 31
PAD = TAPS - 1
GROUP = 64
CHUNK = 64
LEVELS = 6
HEADS = 8
HP = 2 * HEADS
NK = 128
TOPK = 16
SEL = HEADS * TOPK
GT = 32
CPG = 4
GROUPS = NK // CPG
EPS = 1e-6
BASE = 1
NEG = -3.0e38

ALU = mybir.AluOpType
ACT = mybir.ActivationFunctionType
F32 = mybir.dt.float32
BF16 = mybir.dt.bfloat16
U32 = mybir.dt.uint32
I32 = mybir.dt.int32
AX = mybir.AxisListType

PAR = {}
_at = 0
for _name, _n in (("mix_g", KC), ("ffn_g", KC), ("conv_w", CG * TAPS), ("conv_b", CG), ("conv_g", CG),
                  ("conv_nb", CG), ("hgrn_g", CG), ("lb0", CG), ("lb1", CG)):
    PAR[_name] = (_at, _at + _n)
    _at += _n
NPAR = _at


def begin(eng, counters):
    for c in counters:
        eng.sem_inc(c, BASE)


def norm_and_transpose(nc, sems, label, src, load, scaled, small, psum, ident, gain, dst, src_gate):
    loaded = [sems(f"{label}_x{t}") for t in range(TB)] if load is not None else None
    sq_done = sems(f"{label}_sq")
    ms_done = sems(f"{label}_ms")
    rms_done = sems(f"{label}_rms")
    rstd_done = sems(f"{label}_rstd")
    scaled_done = sems(f"{label}_scaled")
    tp_done = sems(f"{label}_tp")
    out_a = sems(f"{label}_out_a")
    out_v = sems(f"{label}_out_v")
    ss, ms, rms, rstd = (small[:, TB * i:TB * (i + 1)] for i in range(4))

    block = nc.Block()
    with block as blk:
        @blk.sync
        def _(sp):
            if load is not None:
                for t in range(TB):
                    sp.dma_start(src[:, t, :], load[t * P:(t + 1) * P, :]).then_inc(loaded[t], 16)

        @blk.scalar
        def _(act):
            for t in range(TB):
                if load is not None:
                    act.wait_ge(loaded[t], 16)
                act.activation(scaled[:, t, :], src[:, t, :], ACT.Square,
                               accum_out=ss[:, t:t + 1]).then_inc(sq_done, 1)
            act.wait_ge(ms_done, 1)
            act.activation(rms, ms, ACT.Sqrt).then_inc(rms_done, 1)
            for k in range(KC):
                act.wait_ge(tp_done, 2 * k + 1)
                act.activation(dst[:, k, 0:HALF], psum[:, (2 * k) % 4, :], ACT.Copy,
                               scale=gain[:, k:k + 1]).then_inc(out_a, 1)

        @blk.vector
        def _(dve):
            dve.wait_ge(sq_done, TB)
            dve.tensor_scalar(ms, ss, 1.0 / D, EPS, ALU.mult, ALU.add).then_inc(ms_done, 1)
            dve.wait_ge(rms_done, 1)
            dve.reciprocal(rstd, rms).then_inc(rstd_done, 1)
            dve.wait_ge(rstd_done, 1)
            for t in range(TB):
                dve.tensor_scalar(scaled[:, t, :], src[:, t, :], rstd[:, t:t + 1], None,
                                  ALU.mult).then_inc(scaled_done, 1)
            for k in range(KC):
                dve.wait_ge(tp_done, 2 * k + 2)
                dve.tensor_scalar(dst[:, k, HALF:T], psum[:, (2 * k + 1) % 4, :], gain[:, k:k + 1], None,
                                  ALU.mult).then_inc(out_v, 1)

        @blk.tensor
        def _(pe):
            for k in range(KC):
                for h, evacuated in ((0, out_a), (1, out_v)):
                    if k == 0:
                        pe.wait_ge(scaled_done, 4 * h + 4)
                    if k >= 2:
                        pe.wait_ge(evacuated, k - 1)
                    for j in range(4):
                        t = 4 * h + j
                        last = pe.transpose(psum[:, (2 * k + h) % 4, j * P:(j + 1) * P],
                                            scaled[:, t, k * P:(k + 1) * P], ident)
                    last.then_inc(tp_done, 1)


def hybrid_block(nc, x, const_f, const_b, const_m, params, w_stream, w_v, w_out, w_q, keys, u_t, v_t,
                 final_g, out, gates):
    top = ExitStack()
    with top:
        def sb(ctx, name, shape, dt):
            return ctx.enter_context(nc.sbuf_tensor(name, shape, dt))

        def sems(name):
            return top.enter_context(nc.semaphore(name))

        psum = top.enter_context(nc.psum_tensor("psum", [P, 8, HALF], F32))
        cf = sb(top, "cf", [P, 3 * P + TOPK], F32)
        ident, group_mean, head_mean = cf[:, 0:P], cf[:, P:2 * P], cf[:, 2 * P:3 * P]
        iota16 = cf[:, 3 * P:3 * P + TOPK]
        cb = sb(top, "cb", [P, P + T], BF16)
        iota128, restart = cb[:, 0:P], cb[:, P:P + T]
        par = sb(top, "par", [P, NPAR], F32)
        small = sb(top, "small", [P, 4 * TB], F32)
        lbs = sb(top, "lbs", [P, 8 * CG], F32)
        region_y = sb(top, "region_y", [P, 8, T], F32)
        region_x = sb(top, "region_x", [P, 8, T], F32)

        def param(name):
            return par[:, PAR[name][0]:PAR[name][1]]

        const_in = sems("const_in")
        small_in = sems("small_in")
        with nc.Block() as blk:
            @blk.sync
            def _(sp):
                sp.dma_start(cf[:, :], const_f).then_inc(const_in, 16)
                sp.dma_start(par[:, :], params).then_inc(const_in, 16)
                sp.wait_ge(const_in, 32)

            @blk.gpsimd
            def _(pool):
                pool.dma_start(cb[:, :], const_b).then_inc(small_in, 16)
                pool.wait_ge(small_in, 16)

        with ExitStack() as ctx:
            xin = sb(ctx, "xin", [P, TB, D], F32)
            scaled = sb(ctx, "scaled1", [P, TB, D], F32)
            norm_and_transpose(nc, sems, "n1", xin, x, scaled, small, psum, ident, param("mix_g"),
                               region_x, None)

        with ExitStack() as ctx:
            mixer(nc, ctx, sb, sems, psum, region_x, region_y, ident, group_mean, head_mean, restart, const_m,
                  param, lbs, w_stream, w_v)

        with ExitStack() as ctx:
            project_out(nc, ctx, sb, sems, psum, region_y, region_x, x, w_out)

        h_acc = region_x
        xh = region_y[:, 0:4, :].bitcast(BF16).rearrange("p a (b n) -> p (a b) n", b=2)
        xl = region_y[:, 4:8, :].bitcast(BF16).rearrange("p a (b n) -> p (a b) n", b=2)
        with ExitStack() as ctx:
            scores = sb(ctx, "scores", [P, TB, HP, NK], F32)
            with ExitStack() as inner:
                xn2 = sb(inner, "xn2", [P, KC, T], F32)
                scaled = scores[:, 0:4, :, :].rearrange("p a b n -> p (a b n)").rearrange(
                    "p (t n) -> p t n", t=TB)
                norm_and_transpose(nc, sems, "n2", h_acc, None, scaled, small, psum, ident,
                                   param("ffn_g"), xn2, None)
                queries(nc, inner, sb, sems, psum, xn2, xh, xl, w_q, keys, scores)
            with ExitStack() as inner:
                sel_t = sb(inner, "sel_t", [P, 3, T], F32)
                with ExitStack() as tk:
                    top_experts(nc, tk, sb, sems, psum, scores, ident, iota16, sel_t)
                with ExitStack() as gk:
                    dense_gates(nc, gk, sb, sems, psum, sel_t, iota128, gates)
        with ExitStack() as ctx:
            experts(nc, ctx, sb, sems, psum, xh, xl, h_acc, u_t, v_t, gates)
        with ExitStack() as ctx:
            final_norm(nc, ctx, sb, sems, h_acc, small, final_g, out)


def mixer(nc, ctx, sb, sems, psum, xn, y, ident, group_mean, head_mean, restart, const_m, param, lbs,
          w_stream, w_v):
    W_SLOTS = 2
    wr = sb(ctx, "w_ring", [P, W_SLOTS, D], F32)
    logf = sb(ctx, "logf", [P, CG, T], F32)
    key = sb(ctx, "key", [P, CG, T], F32)
    glu = sb(ctx, "glu", [P, CG, PAD + T], F32)
    qry = sb(ctx, "qry", [P, CG, T], F32)
    gte = sb(ctx, "gte", [P, CG, T], F32)
    val = sb(ctx, "val", [P, TB, HALF], F32)
    cm = sb(ctx, "cm", [P, (LEVELS + 1) * P], I32)
    wv = y[:, 4:8, :].rearrange("p a (b n) -> p (a b) n", b=2)
    lb, omlb = lbs[:, 0:CG], lbs[:, CG:2 * CG]
    tmp = [lbs[:, (2 + i) * CG:(3 + i) * CG] for i in range(6)]

    w_in = [sems(f"w_in{s}") for s in range(W_SLOTS)]
    wv_in = sems("wv_in")
    masks_in = sems("masks_in")
    proj = [sems(f"proj{b}") for b in range(4)]
    proj_out = [sems(f"proj_out{b}") for b in range(4)]
    val_mm = sems("val_mm")
    val_ok = sems("val_ok")
    pad_ok = sems("pad_ok")
    lb_step = sems("lb_step")
    lb_exp = sems("lb_exp")
    f_ok = sems("f_ok")
    ln_ok = sems("ln_ok")
    glu_ok = sems("glu_ok")
    conv = sems("conv")
    F_PAIRS, GATE_PAIRS, A_PAIRS, Q_PAIRS, G_PAIRS = (0, 2), (2, 4), (4, 6), (6, 8), (8, 10)

    with nc.Block() as blk:
        @blk.sync
        def _(sp):
            sp.dma_start(wv, w_v).then_inc(wv_in, 16)
            sp.dma_start(cm[:, :], const_m).then_inc(masks_in, 16)
            with sp.Fori(0, G_PAIRS[1]) as pair:
                for s in range(W_SLOTS):
                    sp.wait_ge(proj[2 * s + 1], BASE + pair)
                    sp.dma_start(wr[:, s, :], w_stream[ds(pair * W_SLOTS + s, 1), :, :].rearrange(
                        "a p n -> (a p) n")).then_inc(w_in[s], 16)
            sp.wait_ge(masks_in, 16)

        @blk.tensor
        def _(pe):
            begin(pe, [*proj, val_mm])
            def pairs(first, end):
                with pe.Fori(first, end) as pair:
                    for s in range(W_SLOTS):
                        pe.wait_ge(w_in[s], 16 * pair + 16)
                        for h in range(NH):
                            b = 2 * s + h
                            pe.wait_ge(proj_out[b], BASE + pair)
                            for k in range(KC):
                                last = pe.matmul(psum[:, b, :], wr[:, s, k * P:(k + 1) * P],
                                                 xn[:, k, h * HALF:(h + 1) * HALF],
                                                 start=(k == 0), stop=(k == KC - 1))
                            last.then_inc(proj[b], 1)

            pairs(F_PAIRS[0], A_PAIRS[1])
            pe.wait_ge(wv_in, 16)
            for t in range(TB):
                if t >= 4:
                    pe.wait_ge(val_ok, BASE + t - 3)
                for k in range(KC):
                    last = pe.matmul(psum[:, 4 + t % 4, :], xn[:, k, t * P:(t + 1) * P], wv[:, k, :],
                                     start=(k == 0), stop=(k == KC - 1))
                last.then_inc(val_mm, 1)
            pairs(Q_PAIRS[0], G_PAIRS[1])

        @blk.scalar
        def _(act):
            begin(act, [*proj_out, val_ok, lb_exp, ln_ok])
            act.wait_ge(lb_step, BASE + 3)
            act.activation(tmp[2], tmp[1], ACT.Exp)
            act.activation(tmp[3], tmp[4], ACT.Exp).then_inc(lb_exp, 1)

            def each(pairs, base, body):
                with act.Fori(*pairs) as pair:
                    for s in range(W_SLOTS):
                        for h in range(NH):
                            b = 2 * s + h
                            act.wait_ge(proj[b], BASE + pair + 1)
                            body(psum[:, b, :], pair * W_SLOTS + (s - W_SLOTS * base), h).then_inc(proj_out[b], 1)

            def forget(ps, c, h):
                act.activation(logf[:, ds(c, 1), h * HALF:(h + 1) * HALF], ps, ACT.Sigmoid)
                return act.activation(key[:, ds(c, 1), h * HALF:(h + 1) * HALF], ps, ACT.Sigmoid, scale=-1.0)

            def gate(ps, c, h):
                return act.activation(glu[:, ds(c, 1), PAD + h * HALF:PAD + (h + 1) * HALF], ps, ACT.Sigmoid)

            def silu_to(buf):
                return lambda ps, c, h: act.activation(buf[:, ds(c, 1), h * HALF:(h + 1) * HALF], ps, ACT.Silu)

            each(F_PAIRS, F_PAIRS[0], forget)
            each(GATE_PAIRS, GATE_PAIRS[0], gate)
            for c in range(CG):
                act.wait_ge(f_ok, BASE + 2 * c + 1)
                act.activation(logf[:, c, :], logf[:, c, :], ACT.Ln).then_inc(ln_ok, 1)
            for t in range(TB):
                act.wait_ge(val_mm, BASE + t + 1)
                act.activation(val[:, t, :], psum[:, 4 + t % 4, :], ACT.Copy).then_inc(val_ok, 1)
            each(Q_PAIRS, Q_PAIRS[0], silu_to(qry))
            each(G_PAIRS, G_PAIRS[0], silu_to(gte))

        @blk.gpsimd
        def _(pool):
            begin(pool, [pad_ok, f_ok])
            pool.memset(glu[:, :, 0:PAD], 0.0).then_inc(pad_ok, 1)
            pool.wait_ge(lb_step, BASE + 7)
            for b in range(4):
                pool.wait_ge(proj_out[b], BASE + F_PAIRS[1])
            for c in range(CG):
                pool.tensor_scalar(logf[:, c, :], logf[:, c, :], omlb[:, c:c + 1], lb[:, c:c + 1],
                                   ALU.mult, ALU.add).then_inc(f_ok, 1)
                pool.tensor_scalar(key[:, c, :], key[:, c, :], omlb[:, c:c + 1], 1.0,
                                   ALU.mult, ALU.mult).then_inc(f_ok, 1)

        @blk.vector
        def _(dve):
            begin(dve, [lb_step, conv])
            l0, l1 = param("lb0"), param("lb1")
            dve.tensor_tensor(tmp[0], l0, l1, ALU.max).then_inc(lb_step, 1)
            dve.wait_ge(lb_step, BASE + 1)
            dve.tensor_tensor(tmp[1], l0, tmp[0], ALU.subtract).then_inc(lb_step, 1)
            dve.tensor_tensor(tmp[4], l1, tmp[0], ALU.subtract).then_inc(lb_step, 1)
            dve.wait_ge(lb_exp, BASE + 1)
            dve.tensor_tensor(tmp[5], tmp[2], tmp[3], ALU.add).then_inc(lb_step, 1)
            dve.wait_ge(lb_step, BASE + 4)
            dve.reciprocal(tmp[0], tmp[5]).then_inc(lb_step, 1)
            dve.wait_ge(lb_step, BASE + 5)
            dve.tensor_tensor(lb, tmp[2], tmp[0], ALU.mult).then_inc(lb_step, 1)
            dve.tensor_tensor(omlb, tmp[3], tmp[0], ALU.mult).then_inc(lb_step, 1)
            for b in range(4):
                dve.wait_ge(proj_out[b], BASE + GATE_PAIRS[1])
            with dve.Fori(*A_PAIRS) as pair:
                for s in range(W_SLOTS):
                    for h in range(NH):
                        b = 2 * s + h
                        dve.wait_ge(proj[b], BASE + pair + 1)
                        at = glu[:, ds(pair * W_SLOTS + (s - W_SLOTS * A_PAIRS[0]), 1),
                                 PAD + h * HALF:PAD + (h + 1) * HALF].rearrange("p a n -> p (a n)")
                        dve.tensor_tensor(at, at, psum[:, b, :], ALU.mult).then_inc(proj_out[b], 1)
            for c in range(CG):
                dve.wait_ge(ln_ok, BASE + c + 1)
                dve.tensor_tensor_scan(logf[:, c, :], restart, logf[:, c, :], 0.0, ALU.mult, ALU.add)
            dve.wait_ge(pad_ok, BASE + 1)
            for b in range(4):
                dve.wait_ge(proj_out[b], BASE + A_PAIRS[1])
            cw, cbias = param("conv_w"), param("conv_b")
            for c in range(CG):
                dve.tensor_scalar(y[:, c, :], glu[:, c, 0:T], cw[:, c * TAPS:c * TAPS + 1], cbias[:, c:c + 1],
                                  ALU.mult, ALU.add).then_inc(conv, 1)
            with dve.Fori(1, TAPS) as tap:
                for c in range(CG):
                    dve.wait_ge(conv, BASE + CG * tap + (c + 1 - CG))
                    dve.scalar_tensor_tensor(out=y[:, c, :], in0=glu[:, c, ds(tap, T)],
                                             scalar=cw[:, ds(tap + c * TAPS, 1)], in1=y[:, c, :],
                                             op0=ALU.mult, op1=ALU.add).then_inc(conv, 1)

    used = [0]

    def carve(n):
        flat = xn[:, :, :].rearrange("p a n -> p (a n)")
        used[0] += n
        return flat[:, used[0] - n:used[0]]

    lev = [carve(CG * P).rearrange("p (h t) -> p h t", h=CG) for _ in range(LEVELS)]
    k_end = carve(CG * P).rearrange("p (h t) -> p h t", h=CG)
    q_beg = carve(CG * P).rearrange("p (h t) -> p h t", h=CG)
    k_blk = carve(CG * P).rearrange("p (h t) -> p h t", h=CG)
    v_blk = carve(CG * P).rearrange("p (h t) -> p h t", h=CG)
    att = carve(CG * P).rearrange("p (h t) -> p h t", h=CG)
    k_end_t = carve(CG * P).rearrange("p (h t) -> p h t", h=CG)
    state = [carve(CG * P).rearrange("p (h t) -> p h t", h=CG) for _ in range(2)]
    decay = carve(3 * CG).rearrange("p (h c) -> p h c", h=CG)

    LV = LEVELS
    init = sems("hg_init")
    x_sub, x_exp, k_mul, q_mul = sems("x_sub"), sems("x_exp"), sems("k_mul"), sems("q_mul")
    sc_mm, sc_ok = sems("sc_mm"), sems("sc_ok")
    kt_mm, kt_ok = sems("kt_mm"), sems("kt_ok")
    u_mm, s_ok, o_mm, o_ok = sems("u_mm"), sems("s_ok"), sems("o_mm"), sems("o_ok")

    def bank(i):
        return psum[:, i, :].rearrange("p (h t) -> p h t", h=CG)

    def seg(ap, n):
        return ap.rearrange("p h (s i) -> p h s i", i=n)

    with nc.Block() as blk:
        @blk.vector
        def _(dve):
            begin(dve, [init, x_sub, q_mul, sc_ok, s_ok])
            dve.memset(att, 0.0)
            dve.memset(state[0], 0.0).then_inc(init, 1)
            dve.wait_ge(init, BASE + 1)
            with dve.Fori(0, TB) as n:
                b_blk = logf[:, :, ds(n * P, P)]
                q_blk = qry[:, :, ds(n * P, P)]
                dve.wait_ge(sc_mm, BASE + n * (LV + 1))
                for l in range(LV):
                    hs = CHUNK >> (l + 1)
                    for hh in range(CG):
                        bs = b_blk[:, hh, :].rearrange("p (s i) -> p s i", i=2 * hs)
                        ref = bs[:, :, hs - 1:hs].to_broadcast([P, P // (2 * hs), 2 * hs])
                        last = dve.tensor_tensor(lev[l][:, hh, :].rearrange("p (s i) -> p s i", i=2 * hs),
                                                 bs, ref, ALU.subtract)
                    last.then_inc(x_sub, 1)
                dve.wait_ge(kt_mm, BASE + n)
                bs = seg(b_blk, CHUNK)
                dve.tensor_tensor(seg(k_end, CHUNK), bs,
                                  bs[:, :, :, CHUNK - 1:CHUNK].to_broadcast([P, CG, P // CHUNK, CHUNK]),
                                  ALU.subtract).then_inc(x_sub, 1)
                for l in range(LV):
                    hs = CHUNK >> (l + 1)
                    dve.wait_ge(x_exp, BASE + n * (LV + 3) + (l + 1))
                    a = seg(lev[l], 2 * hs)[:, :, :, hs:2 * hs]
                    dve.tensor_tensor(a, a, seg(q_blk, 2 * hs)[:, :, :, hs:2 * hs], ALU.mult).then_inc(q_mul, 1)
                dve.wait_ge(x_exp, BASE + n * (LV + 3) + (LV + 2))
                dve.tensor_tensor(q_beg, q_beg, q_blk, ALU.mult).then_inc(q_mul, 1)
                dve.wait_ge(o_mm, BASE + 2 * n)
                for l in range(LV + 1):
                    dve.wait_ge(sc_mm, BASE + n * (LV + 1) + (l + 1))
                    dve.wait_ge(sc_ok, BASE + n * (LV + 1) + l)
                    dve.memset(decay[:, 0:1, 2:3], 0.0)
                    mask = cm[:, l * P:(l + 1) * P].rearrange("p (a t) -> p a t", a=1).to_broadcast([P, CG, P])
                    dve.copy_predicated(att, mask, bank(l % 2)).then_inc(sc_ok, 1)
                for c in range(2):
                    dve.wait_ge(u_mm, BASE + 2 * n + (c + 1))
                    dve.wait_ge(s_ok, BASE + 2 * n + c)
                    if c == 0:
                        dve.wait_ge(x_exp, BASE + n * (LV + 3) + (LV + 3))
                    else:
                        dve.wait_ge(o_mm, BASE + 2 * n + 1)
                    for hh in range(CG):
                        last = dve.scalar_tensor_tensor(out=state[1 - c][:, hh, :], in0=state[c][:, hh, :],
                                                        scalar=decay[:, hh, c:c + 1], in1=bank(3 + c)[:, hh, :],
                                                        op0=ALU.mult, op1=ALU.add)
                    last.then_inc(s_ok, 1)

        @blk.scalar
        def _(act):
            begin(act, [x_exp, kt_ok, o_ok])
            with act.Fori(0, TB) as n:
                b_blk = logf[:, :, ds(n * P, P)]
                for l in range(LV):
                    hs = CHUNK >> (l + 1)
                    act.wait_ge(x_sub, BASE + n * (LV + 1) + (l + 1))
                    a = seg(lev[l], 2 * hs)
                    act.activation(a[:, :, :, 0:hs], a[:, :, :, 0:hs], ACT.Exp, scale=-1.0)
                    act.activation(a[:, :, :, hs:2 * hs], a[:, :, :, hs:2 * hs], ACT.Exp).then_inc(x_exp, 1)
                act.wait_ge(x_sub, BASE + n * (LV + 1) + (LV + 1))
                act.activation(k_end, k_end, ACT.Exp, scale=-1.0).then_inc(x_exp, 1)
                act.wait_ge(o_mm, BASE + 2 * n)
                act.activation(q_beg, b_blk, ACT.Exp).then_inc(x_exp, 1)
                act.wait_ge(s_ok, BASE + 2 * n)
                act.activation(decay[:, :, 0:2], seg(b_blk, CHUNK)[:, :, :, CHUNK - 1], ACT.Exp).then_inc(x_exp, 1)
                act.wait_ge(kt_mm, BASE + n + 1)
                act.wait_ge(u_mm, BASE + 2 * n)
                act.activation(k_end_t, bank(2), ACT.Copy).then_inc(kt_ok, 1)
                act.wait_ge(o_mm, BASE + 2 * n + 2)
                act.activation(y[:, 4:8, ds(n * P, P)], bank(5), ACT.Copy).then_inc(o_ok, 1)

        @blk.gpsimd
        def _(pool):
            begin(pool, [k_mul])
            with pool.Fori(0, TB) as n:
                kb = key[:, :, ds(n * P, P)]
                pool.wait_ge(o_mm, BASE + 2 * n)
                pool.tensor_copy(v_blk, val[:, ds(n, 1), :].rearrange("p a (h t) -> p (a h) t", h=CG))
                pool.tensor_copy(k_blk, kb).then_inc(k_mul, 1)
                pool.wait_ge(k_mul, BASE + n * (LV + 2) + 1)
                for l in range(LV):
                    hs = CHUNK >> (l + 1)
                    pool.wait_ge(x_exp, BASE + n * (LV + 3) + (l + 1))
                    a = seg(lev[l], 2 * hs)[:, :, :, 0:hs]
                    pool.tensor_tensor(a, a, seg(k_blk, 2 * hs)[:, :, :, 0:hs], ALU.mult).then_inc(k_mul, 1)
                pool.wait_ge(x_exp, BASE + n * (LV + 3) + (LV + 1))
                pool.tensor_tensor(k_end, k_end, k_blk, ALU.mult).then_inc(k_mul, 1)

        @blk.tensor
        def _(pe):
            begin(pe, [sc_mm, kt_mm, u_mm, o_mm])
            pe.wait_ge(init, BASE + 1)
            with pe.Fori(0, TB) as n:
                q_blk = qry[:, :, ds(n * P, P)]
                for l in range(LV + 1):
                    if l < LV:
                        pe.wait_ge(q_mul, BASE + n * (LV + 1) + (l + 1))
                        pe.wait_ge(k_mul, BASE + n * (LV + 2) + (l + 2))
                    pe.wait_ge(sc_ok, BASE + n * (LV + 1) + max(l - 1, 0))
                    for hh in range(CG):
                        if l < LV:
                            last = pe.matmul(bank(l % 2)[:, hh, :], lev[l][:, hh, :], lev[l][:, hh, :],
                                             start=True, stop=True)
                        else:
                            last = pe.matmul(bank(l % 2)[:, hh, :], k_blk[:, hh, :], q_blk[:, hh, :],
                                             start=True, stop=True)
                    last.then_inc(sc_mm, 1)
                pe.wait_ge(k_mul, BASE + n * (LV + 2) + (LV + 2))
                pe.wait_ge(kt_ok, BASE + n)
                for hh in range(CG):
                    last = pe.transpose(bank(2)[:, hh, :], k_end[:, hh, :], ident)
                last.then_inc(kt_mm, 1)
                pe.wait_ge(kt_ok, BASE + n + 1)
                pe.wait_ge(s_ok, BASE + 2 * n)
                for c in range(2):
                    r = slice(c * CHUNK, (c + 1) * CHUNK)
                    for hh in range(CG):
                        last = pe.matmul(bank(3 + c)[:, hh, :], k_end_t[r, hh, :], v_blk[r, hh, :],
                                         start=True, stop=True)
                    last.then_inc(u_mm, 1)
                pe.wait_ge(sc_ok, BASE + n * (LV + 1) + (LV + 1))
                pe.wait_ge(o_ok, BASE + n)
                for hh in range(CG):
                    pe.matmul(bank(5)[:, hh, :], v_blk[:, hh, :], att[:, hh, :], start=(hh == 0), stop=False,
                              skip_group_check=True)
                pe.wait_ge(q_mul, BASE + n * (LV + 1) + (LV + 1))
                for c in range(2):
                    pe.wait_ge(s_ok, BASE + 2 * n + c)
                    for hh in range(CG):
                        last = pe.matmul(bank(5)[:, hh, c * CHUNK:(c + 1) * CHUNK], state[c][:, hh, :],
                                         q_beg[:, hh, c * CHUNK:(c + 1) * CHUNK], start=False,
                                         stop=(c == 1), skip_group_check=True)
                    last.then_inc(o_mm, 1)

    rt = xn[:, :, :].rearrange("p a (b n) -> p (a b) n", b=2)
    yt = y[:, :, :].rearrange("p a (b n) -> p (a b) n", b=2)
    N = 2 * 2 * CG
    CV = 2 * CG
    mean_mm, mean_ok, sq_ok, ms_mm = sems("cn_mean_mm"), sems("cn_mean_ok"), sems("cn_sq"), sems("cn_ms_mm")
    ms_ok, rt_ok, rc_ok, ya_ok = sems("cn_ms_ok"), sems("cn_rt"), sems("cn_rc"), sems("cn_ya")
    mix_done = sems("mix_done")

    with nc.Block() as blk:
        @blk.tensor
        def _(pe):
            begin(pe, [mean_mm, ms_mm])
            with pe.Fori(0, CV // 4) as i:
                for j in range(4):
                    pe.wait_ge(mean_ok, BASE + 4 * i)
                    pe.matmul(psum[:, j, :], group_mean, yt[:, ds(4 * i + j, 1), :].rearrange("p a n -> p (a n)"),
                              start=True, stop=True).then_inc(mean_mm, 1)
            with pe.Fori(0, N // 4) as i:
                for j in range(4):
                    pe.wait_ge(sq_ok, BASE + 4 * i + j + 1)
                    pe.wait_ge(ms_ok, BASE + 4 * i)
                    sq = rt[:, ds(4 * i + j, 1), :].rearrange("p a n -> p (a n)")
                    pe.matmul(psum[:, j, :], group_mean, sq, start=True, stop=True)
                    pe.matmul(psum[:, 4 + j, :], head_mean, sq, start=True, stop=True).then_inc(ms_mm, 1)

        @blk.scalar
        def _(act):
            begin(act, [sq_ok, rt_ok])
            with act.Fori(0, N) as i:
                act.wait_ge(mean_ok, BASE + CV)
                act.activation(rt[:, ds(i, 1), :], yt[:, ds(i, 1), :], ACT.Square).then_inc(sq_ok, 1)
            with act.Fori(0, N) as i:
                act.wait_ge(ms_ok, BASE + i + 1)
                act.activation(rt[:, ds(i, 1), :], rt[:, ds(i, 1), :], ACT.Sqrt).then_inc(rt_ok, 1)
            g, b = param("conv_g"), param("conv_nb")
            for c in range(CG):
                act.wait_ge(ya_ok, BASE + 2 * c + 2)
                act.activation(y[:, c, :], y[:, c, :], ACT.Silu, scale=g[:, c:c + 1],
                               bias=b[:, c:c + 1]).then_inc(mix_done, 1)

        @blk.vector
        def _(dve):
            begin(dve, [mean_ok, ms_ok, rc_ok, ya_ok])
            with dve.Fori(0, CV // 4) as i:
                for j in range(4):
                    dve.wait_ge(mean_mm, BASE + 4 * i + j + 1)
                    a = yt[:, ds(4 * i + j, 1), :].rearrange("p a n -> p (a n)")
                    dve.tensor_tensor(a, a, psum[:, j, :], ALU.subtract).then_inc(mean_ok, 1)
            for first, base in ((0, 0), (CV // 4, 4)):
                with dve.Fori(first, first + CV // 4) as i:
                    for j in range(4):
                        dve.wait_ge(ms_mm, BASE + 4 * i + j + 1)
                        dve.tensor_scalar(rt[:, ds(4 * i + j, 1), :].rearrange("p a n -> p (a n)"),
                                          psum[:, base + j, :], EPS, None, ALU.add).then_inc(ms_ok, 1)
            with dve.Fori(0, N) as i:
                dve.wait_ge(rt_ok, BASE + i + 1)
                a = rt[:, ds(i, 1), :]
                dve.reciprocal(a, a).then_inc(rc_ok, 1)
            with dve.Fori(0, N) as i:
                dve.wait_ge(rc_ok, BASE + i + 1)
                a = yt[:, ds(i, 1), :]
                dve.tensor_tensor(a, a, rt[:, ds(i, 1), :], ALU.mult).then_inc(ya_ok, 1)
            g = param("hgrn_g")
            for c in range(CG):
                dve.wait_ge(ya_ok, BASE + CV + 2 * c + 2)
                dve.scalar_tensor_tensor(out=y[:, CG + c, :], in0=y[:, CG + c, :], scalar=g[:, c:c + 1],
                                         in1=gte[:, c, :], op0=ALU.mult, op1=ALU.mult)


def project_out(nc, ctx, sb, sems, psum, y, h_acc, x, w_out):
    wo = sb(ctx, "wo", [P, KC, D], F32)
    wo_in, x_in, o_mm, h_ok = sems("wo_in"), sems("x_in"), sems("wo_mm"), sems("h_ok")
    with nc.Block() as blk:
        @blk.sync
        def _(sp):
            sp.dma_start(wo[:, :, :], w_out.rearrange("(k p) n -> p k n", p=P)).then_inc(wo_in, 16)
            sp.dma_start(h_acc[:, :, :], x.rearrange("(t p) n -> p t n", p=P)).then_inc(x_in, 16)

        @blk.tensor
        def _(pe):
            pe.wait_ge(wo_in, 16)
            for i in range(2 * TB):
                t, h = i // 2, i % 2
                if i >= 8:
                    pe.wait_ge(h_ok, i - 7)
                for k in range(KC):
                    last = pe.matmul(psum[:, i % 8, :], y[:, k, t * P:(t + 1) * P],
                                     wo[:, k, h * HALF:(h + 1) * HALF], start=(k == 0), stop=(k == KC - 1))
                last.then_inc(o_mm, 1)

        @blk.vector
        def _(dve):
            dve.wait_ge(x_in, 16)
            for i in range(2 * TB):
                t, h = i // 2, i % 2
                dve.wait_ge(o_mm, i + 1)
                a = h_acc[:, t, h * HALF:(h + 1) * HALF]
                dve.tensor_tensor(a, a, psum[:, i % 8, :], ALU.add).then_inc(h_ok, 1)


def queries(nc, ctx, sb, sems, psum, xn2, xh, xl, w_q, keys, scores):
    wr = sb(ctx, "wq_ring", [P, 2, D], F32)
    qt = sb(ctx, "qt", [P, 2, T], F32)
    kt = sb(ctx, "kt", [P, HP, NK], F32)
    k_in = sems("keys_in")
    w_in = [sems(f"wq_in{s}") for s in range(2)]
    q_mm = [sems(f"q_mm{b}") for b in range(4)]
    q_ok = [sems(f"q_ok{b}") for b in range(4)]
    s_mm = [sems(f"s_mm{b}") for b in range(4)]
    s_ok = [sems(f"s_ok{b}") for b in range(4)]
    hi_ok = sems("xh_ok")
    lo_ok = sems("xl_ok")
    with nc.Block() as blk:
        @blk.sync
        def _(sp):
            sp.dma_start(kt[:, :, :], keys).then_inc(k_in, 16)
            with sp.Fori(0, HP // 2) as pair:
                for s in range(2):
                    sp.wait_ge(q_mm[2 * s + 1], BASE + pair)
                    sp.dma_start(wr[:, s, :], w_q[ds(pair * 2 + s, 1), :, :].rearrange(
                        "a p n -> (a p) n")).then_inc(w_in[s], 16)

        @blk.tensor
        def _(pe):
            begin(pe, [*q_mm, *s_mm])
            pe.wait_ge(k_in, 16)
            with pe.Fori(0, HP // 2) as pair:
                for s in range(2):
                    pe.wait_ge(w_in[s], 16 * pair + 16)
                    for h in range(NH):
                        b = 2 * s + h
                        pe.wait_ge(q_ok[b], BASE + pair)
                        for k in range(KC):
                            last = pe.matmul(psum[:, b, :], wr[:, s, k * P:(k + 1) * P],
                                             xn2[:, k, h * HALF:(h + 1) * HALF],
                                             start=(k == 0), stop=(k == KC - 1))
                        last.then_inc(q_mm[b], 1)
                for s in range(2):
                    for h in range(NH):
                        b = 2 * s + h
                        pe.wait_ge(q_ok[b], BASE + pair + 1)
                        pe.wait_ge(s_ok[b], BASE + pair)
                        for j in range(4):
                            last = pe.matmul(psum[:, 4 + b, j * P:(j + 1) * P],
                                             qt[:, s, h * HALF + j * P:h * HALF + (j + 1) * P],
                                             kt[:, ds(2 * pair + s, 1), :].rearrange("p a n -> p (a n)"),
                                             start=True, stop=True)
                        last.then_inc(s_mm[b], 1)

        @blk.scalar
        def _(act):
            begin(act, [*q_ok, hi_ok])
            with act.Fori(0, HP // 2) as pair:
                for b in range(4):
                    act.wait_ge(q_mm[b], BASE + pair + 1)
                    act.wait_ge(s_mm[b], BASE + pair)
                    act.activation(qt[:, b // 2, (b % 2) * HALF:(b % 2 + 1) * HALF], psum[:, b, :],
                                   ACT.Copy).then_inc(q_ok[b], 1)
            for k in range(KC):
                act.activation(xh[:, k, :], xn2[:, k, :], ACT.Copy).then_inc(hi_ok, 1)

        @blk.gpsimd
        def _(pool):
            for k in range(KC):
                pool.wait_ge(hi_ok, BASE + k + 1)
                pool.tensor_tensor(xl[:, k, :], xn2[:, k, :], xh[:, k, :], ALU.subtract).then_inc(lo_ok, 1)

        @blk.vector
        def _(dve):
            begin(dve, s_ok)
            with dve.Fori(0, HP // 2) as pair:
                for s in range(2):
                    for h in range(NH):
                        b = 2 * s + h
                        dve.wait_ge(s_mm[b], BASE + pair + 1)
                        dve.tensor_copy(scores[:, 4 * h:4 * h + 4, ds(2 * pair + s, 1), :].rearrange(
                            "p t a n -> p t (a n)"),
                            psum[:, 4 + b, :].rearrange("p (t n) -> p t n", t=4)).then_inc(s_ok[b], 1)


def top_experts(nc, ctx, sb, sems, psum, scores, ident, iota16, sel_t):
    sc = sb(ctx, "tk_sc", [P, HP, NK], F32)
    rest = sb(ctx, "tk_rest", [P, HP, NK], F32)
    best = sb(ctx, "tk_best", [P, HP, TOPK], F32)
    bidx = sb(ctx, "tk_bidx", [P, HP, TOPK], U32)
    bidf = sb(ctx, "tk_bidf", [P, HP, TOPK], F32)
    cand = sb(ctx, "tk_cand", [P, HEADS, TOPK * TOPK], F32)
    crest = sb(ctx, "tk_crest", [P, HEADS, TOPK * TOPK], F32)
    tops = sb(ctx, "tk_tops", [P, HEADS, TOPK], F32)
    ci = sb(ctx, "tk_ci", [P, HEADS, TOPK], U32)
    cab = sb(ctx, "tk_cab", [P, 2, SEL], U32)
    cabf = sb(ctx, "tk_cabf", [P, 2, SEL], F32)
    hit = sb(ctx, "tk_hit", [P, 2, SEL, TOPK], F32)
    sel = sb(ctx, "tk_sel", [P, 3, SEL], F32)
    ex = sb(ctx, "tk_ex", [P, HEADS, TOPK], F32)
    es = sb(ctx, "tk_es", [P, 2, HEADS], F32)

    sc_in, step, e_ok = sems("tk_in"), sems("tk_step"), sems("tk_e_ok")
    picked, found = sems("tk_picked"), sems("tk_found")
    tp, tp_ok = sems("tk_tp"), sems("tk_tp_ok")
    spare = sb(ctx, "tk_spare", [P, 2], F32)
    STEPS = 16
    EXP_IN = 12

    with nc.Block() as blk:
        @blk.scalar
        def _(act):
            begin(act, [sc_in, e_ok, tp_ok])
            with act.Fori(0, TB) as n:
                act.wait_ge(step, BASE + STEPS * n + 0)
                act.activation(sc[:, :, :], scores[:, ds(n, 1), :, :].rearrange("p a h n -> p (a h) n"),
                               ACT.Copy).then_inc(sc_in, 1)
                act.wait_ge(step, BASE + STEPS * n + EXP_IN)
                act.activation(ex[:, :, :], ex[:, :, :], ACT.Exp).then_inc(e_ok, 1)
                act.wait_ge(tp, BASE + n + 1)
                act.activation(sel_t[:, :, ds(n * P, P)], psum[:, 0, 0:3 * P].rearrange("p (a t) -> p a t", a=3),
                               ACT.Copy).then_inc(tp_ok, 1)

        @blk.vector
        def _(dve):
            begin(dve, [step, picked])
            with dve.Fori(0, TB) as n:
                done = [0]

                def then(ins):
                    done[0] += 1
                    ins.then_inc(step, 1)
                    dve.wait_ge(step, BASE + STEPS * n + done[0])
                    dve.memset(spare[:, 0:1], 0.0)

                dve.wait_ge(sc_in, BASE + n + 1)
                dve.memset(spare[:, 1:2], 0.0)
                for h in range(HP):
                    last = dve.max(best[:, h, 0:8], sc[:, h, :])
                then(last)
                for h in range(HP):
                    dve.match_replace(rest[:, h, :], best[:, h, 0:8], sc[:, h, :], NEG)
                    last = dve.max_index(bidx[:, h, 0:8], best[:, h, 0:8], sc[:, h, :])
                then(last)
                for h in range(HP):
                    last = dve.max(best[:, h, 8:16], rest[:, h, :])
                then(last)
                for h in range(HP):
                    last = dve.max_index(bidx[:, h, 8:16], best[:, h, 8:16], rest[:, h, :])
                then(last)
                two = best[:, :, :].rearrange("p (h a) k -> p h a k", a=2)
                a = two[:, :, 0:1, :].rearrange("p h a k -> p h k a").to_broadcast([P, HEADS, TOPK, TOPK])
                b = two[:, :, 1:2, :].to_broadcast([P, HEADS, TOPK, TOPK])
                dve.tensor_copy(bidf[:, :, :], bidx[:, :, :])
                then(dve.tensor_tensor(cand[:, :, :].rearrange("p h (a b) -> p h a b", a=TOPK), a, b, ALU.add))
                for h in range(HEADS):
                    last = dve.max(tops[:, h, 0:8], cand[:, h, :])
                then(last)
                for h in range(HEADS):
                    dve.match_replace(crest[:, h, :], tops[:, h, 0:8], cand[:, h, :], NEG)
                    last = dve.max_index(ci[:, h, 0:8], tops[:, h, 0:8], cand[:, h, :])
                then(last)
                for h in range(HEADS):
                    last = dve.max(tops[:, h, 8:16], crest[:, h, :])
                then(last)
                for h in range(HEADS):
                    last = dve.max_index(ci[:, h, 8:16], tops[:, h, 8:16], crest[:, h, :])
                then(last)
                cflat = ci[:, :, :].rearrange("p h k -> p (h k)")
                dve.tensor_scalar(cab[:, 0, :], cflat, 4, None, ALU.logical_shift_right)
                then(dve.tensor_scalar(cab[:, 1, :], cflat, TOPK - 1, None, ALU.bitwise_and))
                then(dve.tensor_copy(cabf[:, :, :], cab[:, :, :]))
                for i in range(2):
                    rank = cabf[:, i, :].rearrange("p (k a) -> p k a", a=1).to_broadcast([P, SEL, TOPK])
                    last = dve.tensor_tensor(hit[:, i, :, :], rank, iota16.rearrange(
                        "p (a k) -> p a k", a=1).to_broadcast([P, SEL, TOPK]), ALU.is_equal)
                last.then_inc(picked, 1)
                then(dve.tensor_tensor(ex[:, :, :], tops[:, :, :],
                                       tops[:, :, 0:1].to_broadcast([P, HEADS, TOPK]), ALU.subtract))
                assert done[0] == EXP_IN
                dve.wait_ge(e_ok, BASE + n + 1)
                then(dve.reduce_sum(es[:, 0, :], ex[:, :, :], AX.X))
                then(dve.reciprocal(es[:, 1, :], es[:, 0, :]))
                dve.wait_ge(tp, BASE + n)
                then(dve.tensor_tensor(sel[:, 2, :].rearrange("p (h k) -> p h k", h=HEADS), ex[:, :, :],
                                       es[:, 1, :].rearrange("p (h a) -> p h a", a=1).to_broadcast(
                                           [P, HEADS, TOPK]), ALU.mult))
                dve.wait_ge(found, BASE + n + 1)
                then(dve.reduce_sum(sel[:, 0:2, :], hit[:, :, :, :], AX.X))
                assert done[0] == STEPS

        @blk.gpsimd
        def _(pool):
            begin(pool, [found])
            with pool.Fori(0, TB) as n:
                pool.wait_ge(picked, BASE + n + 1)
                for i in range(2):
                    for h in range(HEADS):
                        idx = bidf[:, 2 * h + i:2 * h + i + 1, :].to_broadcast([P, TOPK, TOPK])
                        a = hit[:, i, h * TOPK:(h + 1) * TOPK, :]
                        last = pool.tensor_tensor(a, a, idx, ALU.mult)
                last.then_inc(found, 1)

        @blk.tensor
        def _(pe):
            begin(pe, [tp])
            with pe.Fori(0, TB) as n:
                pe.wait_ge(step, BASE + STEPS * n + STEPS)
                pe.wait_ge(tp_ok, BASE + n)
                for i in range(3):
                    last = pe.transpose(psum[:, 0, i * P:(i + 1) * P], sel[:, i, :], ident)
                last.then_inc(tp, 1)


def dense_gates(nc, ctx, sb, sems, psum, sel_t, iota128, gates):
    RING = 2
    NB = 4
    hot = sb(ctx, "hot", [P, RING, 4, 3, P], BF16)
    glo = sb(ctx, "glo", [P, T], F32)
    ghi = sb(ctx, "ghi", [P, T], BF16)
    tile = sb(ctx, "g_tile", [P, 2, NK, GT], F32)
    Q = GT // 4
    pre, hot_ok, g_mm, g_ok = sems("g_pre"), sems("hot_ok"), sems("g_mm"), sems("g_ok")
    g_st = [sems(f"g_st{i}") for i in range(2)]
    free = [sems(f"g_free{i}") for i in range(2)]
    with nc.Block() as blk:
        @blk.vector
        def _(dve):
            begin(dve, [pre, hot_ok])
            dve.tensor_copy(ghi[:, :], sel_t[:, 2, :]).then_inc(pre, 1)
            dve.wait_ge(pre, BASE + 1)
            dve.tensor_tensor(glo[:, :], sel_t[:, 2, :], ghi[:, :], ALU.subtract).then_inc(pre, 1)
            dve.wait_ge(pre, BASE + 2)
            with dve.Fori(0, T // (4 * RING)) as i:
                for r in range(RING):
                    dve.wait_ge(g_mm, BASE + RING * i)
                    for j in range(4):
                        t = i * (4 * RING) + (4 * r + j)
                        i1 = sel_t[:, 0, ds(t, 1)]
                        i2 = sel_t[:, 1, ds(t, 1)]
                        dve.tensor_scalar(hot[:, r, j, 0, :], iota128, i1, None, ALU.is_equal)
                        dve.tensor_scalar(hot[:, r, j, 1, :], iota128, i2, sel_t[:, 2, ds(t, 1)],
                                          ALU.is_equal, ALU.mult)
                        last = dve.tensor_scalar(hot[:, r, j, 2, :], iota128, i2, glo[:, ds(t, 1)],
                                                 ALU.is_equal, ALU.mult)
                    last.then_inc(hot_ok, 1)

        @blk.tensor
        def _(pe):
            begin(pe, [g_mm])
            with pe.Fori(0, T // (4 * NB)) as i:
                for b in range(NB):
                    pe.wait_ge(hot_ok, BASE + NB * i + b + 1)
                    pe.wait_ge(g_ok, BASE + NB * i)
                    r = b % RING
                    for j in range(4):
                        for part in (1, 2):
                            last = pe.matmul(psum[:, b, j * P:(j + 1) * P], hot[:, r, j, 0, :],
                                             hot[:, r, j, part, :], start=(part == 1), stop=(part == 2))
                    last.then_inc(g_mm, 1)

        @blk.scalar
        def _(act):
            begin(act, [g_ok])
            with act.Fori(0, T // (2 * GT)) as i:
                for u in range(2):
                    act.wait_ge(free[u], BASE + i)
                    for q in range(Q):
                        b = q % NB
                        act.wait_ge(g_mm, BASE + 2 * Q * i + u * Q + q + 1)
                        act.activation(tile[:, u, :, 4 * q:4 * q + 4].rearrange("p c t -> p t c"),
                                       psum[:, b, :].rearrange("p (t c) -> p t c", t=4),
                                       ACT.Copy).then_inc(g_ok, 1)

        @blk.sync
        def _(sp):
            begin(sp, free)
            with sp.Fori(0, T // (2 * GT)) as i:
                for u in range(2):
                    sp.wait_ge(g_ok, BASE + 2 * Q * i + (u + 1) * Q)
                    sp.dma_start(gates[ds(2 * i + u, 1), :, :].rearrange("a p n -> (a p) n"),
                                 tile[:, u, :, :].rearrange("p c t -> p (c t)")).then_inc(g_st[u], 16)
                    sp.wait_ge(g_st[u], 16 * i + 16)
                    sp.sem_inc(free[u], 1)


def experts(nc, ctx, sb, sems, psum, xh, xl, h_acc, u_t, v_t, gates):
    uf = sb(ctx, "uf", [P, 2, D], F32)
    vf = sb(ctx, "vf", [P, 2, D], F32)
    uh = sb(ctx, "uh", [P, CPG, D], BF16)
    ul = sb(ctx, "ul", [P, CPG, D], BF16)
    vh = sb(ctx, "vh", [P, 2, CPG, D], BF16)
    vl = sb(ctx, "vl", [P, 2, CPG, D], BF16)
    gt = sb(ctx, "gt", [P, 2, T // GT, CPG, GT], F32)
    ge = sb(ctx, "ge", [P, 4, HALF], F32)
    wh = sb(ctx, "wh", [P, 2, CPG, T], BF16)
    wl = sb(ctx, "wl", [P, 2, CPG, T], BF16)
    AB = 4
    U = 2 * CPG
    O = 2 * TB

    u_in = [sems(f"u_in{s}") for s in range(2)]
    v_in = [sems(f"v_in{s}") for s in range(2)]
    g_in = [sems(f"gt_in{s}") for s in range(2)]
    u_hi, u_lo, v_hi, v_lo = sems("u_hi"), sems("u_lo"), sems("v_hi"), sems("v_lo")
    a_mm, a_ge, a_w, a_hi, a_lo = sems("a_mm"), sems("a_ge"), sems("a_w"), sems("a_hi"), sems("a_lo")
    y_mm, y_ok = sems("y_mm"), sems("y_ok")
    FREE_STAGE, FREE_GE, FREE_W, FREE_Y, FREE_BANK = 2, 4, U, O, 4

    def slots(eng, slot):
        slot(0, 0)
        with eng.Fori(0, GROUPS // 2 - 1) as i:
            slot(2 * i + 1, 1)
            slot(2 * i + 2, 0)
        slot(GROUPS - 1, 1)

    def is_last(g):
        return isinstance(g, int) and g == GROUPS - 1

    def is_first(g):
        return isinstance(g, int) and g == 0

    with nc.Block() as blk:
        @blk.sync
        def _(sp):
            def load_gates(g, par):
                sp.wait_ge(a_w, g * U)
                sp.dma_start(gt[:, par, :, :, :].rearrange("p b c t -> p b (c t)"),
                             gates.rearrange("b p (g n) -> g p b n", g=GROUPS)[ds(g, 1), :, :, :].rearrange(
                                 "g p b n -> (g p) b n")).then_inc(g_in[par], 16)

            def load(stage, table, arrived, split, g, c):
                sp.wait_ge(split, g * CPG + (c + 1))
                sp.dma_start(stage[:, c % 2, :], table[ds(g * CPG + c, 1), :, :].rearrange(
                    "a p n -> (a p) n")).then_inc(arrived[c % 2], 16)

            def slot(g, par):
                if not is_last(g):
                    load_gates(g + 1, 1 - par)
                for c in range(CPG):
                    load(vf, v_t, v_in, v_lo, g, c)
                    if not is_last(g):
                        load(uf, u_t, u_in, u_lo, g + 1, c)

            load_gates(0, 0)
            for c in range(CPG):
                load(uf, u_t, u_in, u_lo, 0, c)
            slots(sp, slot)

        @blk.tensor
        def _(pe):
            def activations(g):
                for c in range(CPG):
                    pe.wait_ge(u_hi, g * CPG + (c + 1))
                    pe.wait_ge(u_lo, g * CPG + (c + 1) + FREE_STAGE)
                    for h in range(NH):
                        k = 2 * c + h
                        pe.wait_ge(a_ge, g * U + (k + 1))
                        cols = slice(h * HALF, (h + 1) * HALF)
                        for n in range(KC):
                            row = slice(n * P, (n + 1) * P)
                            a = psum[:, k % AB, :]
                            pe.matmul(a, uh[:, c, row], xh[:, n, cols], start=(n == 0), stop=False)
                            pe.matmul(a, uh[:, c, row], xl[:, n, cols], start=False, stop=False)
                            last = pe.matmul(a, ul[:, c, row], xh[:, n, cols], start=False, stop=(n == KC - 1))
                        last.then_inc(a_mm, 1)

            def outputs(g, par):
                pe.wait_ge(v_hi, g * CPG + CPG)
                pe.wait_ge(v_lo, g * CPG + (CPG + FREE_STAGE))
                pe.wait_ge(a_hi, g * U + U)
                pe.wait_ge(a_lo, g * U + (U + FREE_GE))
                for o in range(O):
                    rows, cols = slice((o // 2) * P, (o // 2 + 1) * P), slice((o % 2) * HALF, (o % 2 + 1) * HALF)
                    pe.wait_ge(y_ok, g * O + (o + 1))
                    for c in range(CPG):
                        a = psum[:, AB + o % 4, :]
                        pe.matmul(a, wh[:, par, c, rows], vh[:, par, c, cols], start=(c == 0), stop=False)
                        pe.matmul(a, wh[:, par, c, rows], vl[:, par, c, cols], start=False, stop=False)
                        last = pe.matmul(a, wl[:, par, c, rows], vh[:, par, c, cols], start=False,
                                         stop=(c == CPG - 1))
                    last.then_inc(y_mm, 1)

            pe.nop().then_inc(y_mm, FREE_Y)

            def slot(g, par):
                activations(g)
                if not is_first(g):
                    outputs(g - 1, 1 - par)

            slots(pe, slot)
            outputs(GROUPS - 1, 1)

        @blk.scalar
        def _(act):
            def split(stage, high, arrived, done, g, c):
                act.wait_ge(arrived[c % 2], g * (8 * CPG) + (16 * (c // 2) + 16))
                act.activation(high, stage[:, c % 2, :], ACT.Copy).then_inc(done, 1)

            def slot(g, par):
                for c in range(CPG):
                    for h in range(NH):
                        k = 2 * c + h
                        act.wait_ge(a_mm, g * U + (k + 1))
                        act.wait_ge(a_lo, g * U + (k + 1))
                        act.activation(ge[:, k % 4, :], psum[:, k % AB, :], ACT.Gelu).then_inc(a_ge, 1)
                        act.wait_ge(a_w, g * U + (k + 1 + FREE_W))
                        act.wait_ge(y_mm, g * O)
                        act.activation(wh[:, par, c, h * HALF:(h + 1) * HALF], ge[:, k % 4, :],
                                       ACT.Copy).then_inc(a_hi, 1)
                    split(vf, vh[:, par, c, :], v_in, v_hi, g, c)
                    if not is_last(g):
                        split(uf, uh[:, c, :], u_in, u_hi, g + 1, c)

            act.wait_ge(a_ge, FREE_GE)
            for c in range(CPG):
                split(uf, uh[:, c, :], u_in, u_hi, 0, c)
            slots(act, slot)

        @blk.gpsimd
        def _(pool):
            def low(stage, high, lo, highs, done, g, c):
                pool.wait_ge(highs, g * CPG + (c + 1))
                pool.tensor_tensor(lo, stage[:, c % 2, :], high, ALU.subtract).then_inc(done, 1)

            def slot(g, par):
                for c in range(CPG):
                    for h in range(NH):
                        k = 2 * c + h
                        pool.wait_ge(a_hi, g * U + (k + 1))
                        pool.tensor_tensor(wl[:, par, c, h * HALF:(h + 1) * HALF], ge[:, k % 4, :],
                                           wh[:, par, c, h * HALF:(h + 1) * HALF],
                                           ALU.subtract).then_inc(a_lo, 1)
                    low(vf, vh[:, par, c, :], vl[:, par, c, :], v_hi, v_lo, g, c)
                    if not is_last(g):
                        low(uf, uh[:, c, :], ul[:, c, :], u_hi, u_lo, g + 1, c)

            pool.engine_nop().then_inc(u_lo, FREE_STAGE)
            pool.engine_nop().then_inc(v_lo, FREE_STAGE)
            pool.engine_nop().then_inc(a_lo, FREE_GE)
            for c in range(CPG):
                low(uf, uh[:, c, :], ul[:, c, :], u_hi, u_lo, 0, c)
            slots(pool, slot)

        @blk.vector
        def _(dve):
            def weigh(g, par):
                dve.wait_ge(g_in[par], (g - par) * 8 + 16)
                for c in range(CPG):
                    for h in range(NH):
                        k = 2 * c + h
                        dve.wait_ge(a_ge, g * U + (k + 1 + FREE_GE))
                        nb = HALF // GT
                        a = ge[:, k % 4, :].rearrange("p (b t) -> p b t", t=GT)
                        dve.tensor_tensor(a, a, gt[:, par, h * nb:(h + 1) * nb, c, :], ALU.mult).then_inc(a_w, 1)

            def add(g):
                for o in range(O):
                    dve.wait_ge(y_mm, g * O + (o + 1 + FREE_Y))
                    dve.wait_ge(y_ok, g * O + o)
                    a = h_acc[:, o // 2, (o % 2) * HALF:(o % 2 + 1) * HALF]
                    dve.tensor_tensor(a, a, psum[:, AB + o % 4, :], ALU.add).then_inc(y_ok, 1)

            def slot(g, par):
                weigh(g, par)
                if not is_first(g):
                    add(g - 1)

            dve.engine_nop().then_inc(a_ge, FREE_GE)
            dve.engine_nop().then_inc(a_w, FREE_W)
            dve.engine_nop().then_inc(y_ok, FREE_BANK)
            slots(dve, slot)
            add(GROUPS - 1)


def final_norm(nc, ctx, sb, sems, h_acc, small, final_g, out):
    fg = sb(ctx, "fg", [P, D], F32)
    sq = sb(ctx, "fsq", [P, TB, D], F32)
    g_in, sq_ok, ms_ok, rms_ok, rs_ok = (sems(n) for n in ("fg_in", "f_sq", "f_ms", "f_rms", "f_rs"))
    o_ok = sems("f_out")
    stored = sems("stored")
    ss, ms, rms, rstd = (small[:, TB * i:TB * (i + 1)] for i in range(4))
    with nc.Block() as blk:
        @blk.sync
        def _(sp):
            sp.dma_start(fg[:, :], final_g).then_inc(g_in, 16)
            for t in range(TB):
                sp.wait_ge(o_ok, t + 1)
                sp.dma_start(out[t * P:(t + 1) * P, :], sq[:, t, :]).then_inc(stored, 16)
            sp.wait_ge(stored, 16 * TB)

        @blk.scalar
        def _(act):
            for t in range(TB):
                act.activation(sq[:, t, :], h_acc[:, t, :], ACT.Square, accum_out=ss[:, t:t + 1]).then_inc(sq_ok, 1)
            act.wait_ge(ms_ok, 1)
            act.activation(rms, ms, ACT.Sqrt).then_inc(rms_ok, 1)

        @blk.vector
        def _(dve):
            dve.wait_ge(sq_ok, TB)
            dve.tensor_scalar(ms, ss, 1.0 / D, EPS, ALU.mult, ALU.add).then_inc(ms_ok, 1)
            dve.wait_ge(rms_ok, 1)
            dve.reciprocal(rstd, rms).then_inc(rs_ok, 1)
            dve.wait_ge(rs_ok, 1)
            dve.wait_ge(g_in, 16)
            for t in range(TB):
                dve.scalar_tensor_tensor(out=sq[:, t, :], in0=h_acc[:, t, :], scalar=rstd[:, t:t + 1],
                                         in1=fg[:, :], op0=ALU.mult, op1=ALU.mult).then_inc(o_ok, 1)


def _layout(i):
    import numpy as np

    f = np.float32
    c = np.ascontiguousarray
    eye = np.eye(P, dtype=f)
    groups = np.kron(np.eye(P // GROUP, dtype=f), np.full((GROUP, GROUP), 1.0 / GROUP, f))
    heads = np.full((P, P), 1.0 / P, f)
    iota16 = np.broadcast_to(np.arange(TOPK, dtype=f), (P, TOPK))
    restart = np.ones((P, T), f)
    restart[:, ::CHUNK] = 0.0
    iota = np.broadcast_to(np.arange(P, dtype=f), (P, P))
    s, t = np.arange(P)[:, None], np.arange(P)[None, :]
    masks = []
    for level in range(LEVELS):
        n = CHUNK >> level
        masks.append((s // n == t // n) & (s % n < n // 2) & (t % n >= n // 2))
    masks.append(s == t)
    cols = lambda v, n: np.asarray(v, f).reshape(n, P).T
    w_in = np.asarray(i["w_in"])[0].reshape(KC, P, 6, CG, P)
    stream = w_in[:, :, [3, 1, 0, 2, 5]].transpose(2, 3, 1, 0, 4).reshape(5 * CG, P, D)
    w_v = w_in[:, :, 4].reshape(KC, P, HALF).transpose(1, 0, 2)
    conv_w = np.asarray(i["conv_w"])[0].T.reshape(CG, P, TAPS).transpose(1, 0, 2).reshape(P, CG * TAPS)
    params = np.concatenate([
        cols(i["norm_mix_g"], KC), cols(i["norm_ffn_g"], KC), conv_w, cols(i["conv_b"], CG),
        cols(i["conv_norm_g"], CG), cols(i["conv_norm_b"], CG), cols(i["hgrn_norm_g"], CG),
        cols(np.asarray(i["hgrn_lb_logits"])[0], CG), cols(np.asarray(i["hgrn_lb_logits"])[1], CG)], axis=1)
    return {
        "x": c(np.asarray(i["x"]).reshape(T, D)),
        "const_f": c(np.concatenate([eye, groups, heads, iota16], axis=1)),
        "const_b": c(np.concatenate([iota, restart], axis=1)),
        "const_m": c(np.concatenate(masks, axis=1).astype(np.int32)),
        "params": c(params),
        "w_stream": c(stream),
        "w_v": c(w_v),
        "w_out": c(np.asarray(i["w_out"])[0]),
        "w_q": c(np.asarray(i["peer_w_query"])[0].reshape(KC, P, HP, P).transpose(2, 1, 0, 3).reshape(HP, P, D)),
        "keys": c(np.asarray(i["peer_sub_keys"])[0].reshape(HP, NK, P).transpose(2, 0, 1)),
        "u_t": c(np.asarray(i["peer_u"])[0].reshape(NK, NK, KC, P).transpose(1, 3, 2, 0).reshape(NK, P, D)),
        "v_t": c(np.asarray(i["peer_v"])[0].reshape(NK, NK, D).transpose(1, 0, 2)),
        "final_g": c(np.broadcast_to(np.asarray(i["final_norm_g"]), (P, D))),
    }


def kernel(**inputs):
    import numpy as np
    import concourse.bacc as bacc
    from concourse.bass_utils import run_bass_kernel_spmd as run

    nc = bacc.Bacc("TRN2", target_bir_lowering=False, num_devices=1)
    arrays = {f"in_{n}_dram": a for n, a in _layout(inputs).items()}
    args = [nc.dram_tensor(n, a.shape, mybir.dt.from_np(a.dtype), kind="ExternalInput").ap()
            for n, a in arrays.items()]
    args.append(nc.dram_tensor("out_0_dram", (T, D), F32, kind="ExternalOutput").ap())
    args.append(nc.dram_tensor("gates_dram", (T // GT, P, NK * GT), F32, kind="Internal").ap())
    hybrid_block(nc, *args)
    r = run(nc, [arrays], core_ids=[0])
    return np.asarray(r.results[0]["out_0_dram"]).reshape(1, T, D)
```

```python
from contextlib import ExitStack

import concourse.bass as bass
from concourse import mybir
from concourse.bass import ds

P = 128
T = 1024
D = 1024
TB = T // P
KC = D // P
HALF = 512
NH = T // HALF
CG = 4
TAPS = 31
PAD = TAPS - 1
GROUP = 64
CHUNK = 64
LEVELS = 6
HEADS = 8
HP = 2 * HEADS
NK = 128
TOPK = 16
SEL = HEADS * TOPK
GT = 32
CPG = 4
GROUPS = NK // CPG
EPS = 1e-6
BASE = 1
NEG = -3.0e38

ALU = mybir.AluOpType
ACT = mybir.ActivationFunctionType
F32 = mybir.dt.float32
BF16 = mybir.dt.bfloat16
U32 = mybir.dt.uint32
I32 = mybir.dt.int32
AX = mybir.AxisListType

PAR = {}
_at = 0
for _name, _n in (("mix_g", KC), ("ffn_g", KC), ("conv_w", CG * TAPS), ("conv_b", CG), ("conv_g", CG),
                  ("conv_nb", CG), ("hgrn_g", CG), ("lb0", CG), ("lb1", CG)):
    PAR[_name] = (_at, _at + _n)
    _at += _n
NPAR = _at


def begin(eng, counters):
    for c in counters:
        eng.sem_inc(c, BASE)


def norm_and_transpose(nc, sems, label, src, load, scaled, small, psum, ident, gain, dst, src_gate):
    loaded = [sems(f"{label}_x{t}") for t in range(TB)] if load is not None else None
    sq_done = sems(f"{label}_sq")
    ms_done = sems(f"{label}_ms")
    rms_done = sems(f"{label}_rms")
    rstd_done = sems(f"{label}_rstd")
    scaled_done = sems(f"{label}_scaled")
    tp_done = sems(f"{label}_tp")
    out_a = sems(f"{label}_out_a")
    out_v = sems(f"{label}_out_v")
    ss, ms, rms, rstd = (small[:, TB * i:TB * (i + 1)] for i in range(4))

    block = nc.Block()
    with block as blk:
        @blk.sync
        def _(sp):
            if load is not None:
                for t in range(TB):
                    sp.dma_start(src[:, t, :], load[t * P:(t + 1) * P, :]).then_inc(loaded[t], 16)

        @blk.scalar
        def _(act):
            for t in range(TB):
                if load is not None:
                    act.wait_ge(loaded[t], 16)
                act.activation(scaled[:, t, :], src[:, t, :], ACT.Square,
                               accum_out=ss[:, t:t + 1]).then_inc(sq_done, 1)
            act.wait_ge(ms_done, 1)
            act.activation(rms, ms, ACT.Sqrt).then_inc(rms_done, 1)
            for k in range(KC):
                act.wait_ge(tp_done, 2 * k + 1)
                act.activation(dst[:, k, 0:HALF], psum[:, (2 * k) % 4, :], ACT.Copy,
                               scale=gain[:, k:k + 1]).then_inc(out_a, 1)

        @blk.vector
        def _(dve):
            dve.wait_ge(sq_done, TB)
            dve.tensor_scalar(ms, ss, 1.0 / D, EPS, ALU.mult, ALU.add).then_inc(ms_done, 1)
            dve.wait_ge(rms_done, 1)
            dve.reciprocal(rstd, rms).then_inc(rstd_done, 1)
            dve.wait_ge(rstd_done, 1)
            for t in range(TB):
                dve.tensor_scalar(scaled[:, t, :], src[:, t, :], rstd[:, t:t + 1], None,
                                  ALU.mult).then_inc(scaled_done, 1)
            for k in range(KC):
                dve.wait_ge(tp_done, 2 * k + 2)
                dve.tensor_scalar(dst[:, k, HALF:T], psum[:, (2 * k + 1) % 4, :], gain[:, k:k + 1], None,
                                  ALU.mult).then_inc(out_v, 1)

        @blk.tensor
        def _(pe):
            for k in range(KC):
                for h, evacuated in ((0, out_a), (1, out_v)):
                    if k == 0:
                        pe.wait_ge(scaled_done, 4 * h + 4)
                    if k >= 2:
                        pe.wait_ge(evacuated, k - 1)
                    for j in range(4):
                        t = 4 * h + j
                        last = pe.transpose(psum[:, (2 * k + h) % 4, j * P:(j + 1) * P],
                                            scaled[:, t, k * P:(k + 1) * P], ident)
                    last.then_inc(tp_done, 1)


def hybrid_block(nc, x, const_f, const_b, const_m, params, w_stream, w_v, w_out, w_q, keys, u_t, v_t,
                 final_g, out, gates, acts):
    top = ExitStack()
    with top:
        def sb(ctx, name, shape, dt):
            return ctx.enter_context(nc.sbuf_tensor(name, shape, dt))

        def sems(name):
            return top.enter_context(nc.semaphore(name))

        psum = top.enter_context(nc.psum_tensor("psum", [P, 8, HALF], F32))
        cf = sb(top, "cf", [P, 3 * P + TOPK], F32)
        ident, group_mean, head_mean = cf[:, 0:P], cf[:, P:2 * P], cf[:, 2 * P:3 * P]
        iota16 = cf[:, 3 * P:3 * P + TOPK]
        par = sb(top, "par", [P, NPAR], F32)
        small = sb(top, "small", [P, 4 * TB], F32)
        lbs = sb(top, "lbs", [P, 8 * CG], F32)
        region_y = sb(top, "region_y", [P, 8, T], F32)
        region_x = sb(top, "region_x", [P, 8, T], F32)

        def param(name):
            return par[:, PAR[name][0]:PAR[name][1]]

        const_in = sems("const_in")
        with nc.Block() as blk:
            @blk.sync
            def _(sp):
                sp.dma_start(cf[:, :], const_f).then_inc(const_in, 16)
                sp.dma_start(par[:, :], params).then_inc(const_in, 16)
                sp.wait_ge(const_in, 32)

        with ExitStack() as ctx:
            xin = sb(ctx, "xin", [P, TB, D], F32)
            scaled = sb(ctx, "scaled1", [P, TB, D], F32)
            norm_and_transpose(nc, sems, "n1", xin, x, scaled, small, psum, ident, param("mix_g"),
                               region_x, None)

        with ExitStack() as ctx:
            mixer(nc, ctx, sb, sems, psum, region_x, region_y, ident, group_mean, head_mean, const_b, const_m,
                  param, lbs, w_stream, w_v)

        with ExitStack() as ctx:
            project_out(nc, ctx, sb, sems, psum, region_y, region_x, x, w_out)

        h_acc = region_x
        xh = region_y[:, 0:4, :].bitcast(BF16).rearrange("p a (b n) -> p (a b) n", b=2)
        xl = region_y[:, 4:8, :].bitcast(BF16).rearrange("p a (b n) -> p (a b) n", b=2)
        with ExitStack() as ctx:
            scores = sb(ctx, "scores", [P, TB, HP, NK], F32)
            with ExitStack() as inner:
                xn2 = sb(inner, "xn2", [P, KC, T], F32)
                scaled = scores[:, 0:4, :, :].rearrange("p a b n -> p (a b n)").rearrange(
                    "p (t n) -> p t n", t=TB)
                norm_and_transpose(nc, sems, "n2", h_acc, None, scaled, small, psum, ident,
                                   param("ffn_g"), xn2, None)
                queries(nc, inner, sb, sems, psum, xn2, xh, xl, w_q, keys, scores)
            select_and_activate(nc, ctx, sb, sems, psum, scores, ident, iota16, const_b, xh, xl, u_t,
                                gates, acts)
        with ExitStack() as ctx:
            combine(nc, ctx, sb, sems, psum, h_acc, v_t, gates, acts)
        with ExitStack() as ctx:
            final_norm(nc, ctx, sb, sems, h_acc, small, final_g, out)


def mixer(nc, ctx, sb, sems, psum, xn, y, ident, group_mean, head_mean, const_b, const_m, param, lbs,
          w_stream, w_v):
    W_SLOTS = 2
    wr = sb(ctx, "w_ring", [P, W_SLOTS, D], F32)
    logf = sb(ctx, "logf", [P, CG, T], F32)
    key = sb(ctx, "key", [P, CG, T], F32)
    glu = sb(ctx, "glu", [P, CG, PAD + T], F32)
    qry = sb(ctx, "qry", [P, CG, T], F32)
    gte = sb(ctx, "gte", [P, CG, T], F32)
    val = sb(ctx, "val", [P, TB, HALF], F32)
    restart = sb(ctx, "restart", [P, T], BF16)
    cm = sb(ctx, "cm", [P, (LEVELS + 1) * P], I32)
    wv = y[:, 4:8, :].rearrange("p a (b n) -> p (a b) n", b=2)
    lb, omlb = lbs[:, 0:CG], lbs[:, CG:2 * CG]
    tmp = [lbs[:, (2 + i) * CG:(3 + i) * CG] for i in range(6)]

    w_in = [sems(f"w_in{s}") for s in range(W_SLOTS)]
    wv_in = sems("wv_in")
    masks_in = sems("masks_in")
    restart_in = sems("restart_in")
    proj = [sems(f"proj{b}") for b in range(4)]
    proj_out = [sems(f"proj_out{b}") for b in range(4)]
    val_mm = sems("val_mm")
    val_ok = sems("val_ok")
    pad_ok = sems("pad_ok")
    lb_step = sems("lb_step")
    lb_exp = sems("lb_exp")
    f_ok = sems("f_ok")
    ln_ok = sems("ln_ok")
    glu_ok = sems("glu_ok")
    conv = sems("conv")
    F_PAIRS, GATE_PAIRS, A_PAIRS, Q_PAIRS, G_PAIRS = (0, 2), (2, 4), (4, 6), (6, 8), (8, 10)

    with nc.Block() as blk:
        @blk.sync
        def _(sp):
            sp.dma_start(wv, w_v).then_inc(wv_in, 16)
            sp.dma_start(cm[:, :], const_m).then_inc(masks_in, 16)
            with sp.Fori(0, G_PAIRS[1]) as pair:
                for s in range(W_SLOTS):
                    sp.wait_ge(proj[2 * s + 1], BASE + pair)
                    sp.dma_start(wr[:, s, :], w_stream[ds(pair * W_SLOTS + s, 1), :, :].rearrange(
                        "a p n -> (a p) n")).then_inc(w_in[s], 16)
            sp.wait_ge(masks_in, 16)

        @blk.tensor
        def _(pe):
            begin(pe, [*proj, val_mm])
            def pairs(first, end):
                with pe.Fori(first, end) as pair:
                    for s in range(W_SLOTS):
                        pe.wait_ge(w_in[s], 16 * pair + 16)
                        for h in range(NH):
                            b = 2 * s + h
                            pe.wait_ge(proj_out[b], BASE + pair)
                            for k in range(KC):
                                last = pe.matmul(psum[:, b, :], wr[:, s, k * P:(k + 1) * P],
                                                 xn[:, k, h * HALF:(h + 1) * HALF],
                                                 start=(k == 0), stop=(k == KC - 1))
                            last.then_inc(proj[b], 1)

            pairs(F_PAIRS[0], A_PAIRS[1])
            pe.wait_ge(wv_in, 16)
            for t in range(TB):
                if t >= 4:
                    pe.wait_ge(val_ok, BASE + t - 3)
                for k in range(KC):
                    last = pe.matmul(psum[:, 4 + t % 4, :], xn[:, k, t * P:(t + 1) * P], wv[:, k, :],
                                     start=(k == 0), stop=(k == KC - 1))
                last.then_inc(val_mm, 1)
            pairs(Q_PAIRS[0], G_PAIRS[1])

        @blk.scalar
        def _(act):
            begin(act, [*proj_out, val_ok, lb_exp, ln_ok])
            act.wait_ge(lb_step, BASE + 3)
            act.activation(tmp[2], tmp[1], ACT.Exp)
            act.activation(tmp[3], tmp[4], ACT.Exp).then_inc(lb_exp, 1)

            def each(pairs, base, body):
                with act.Fori(*pairs) as pair:
                    for s in range(W_SLOTS):
                        for h in range(NH):
                            b = 2 * s + h
                            act.wait_ge(proj[b], BASE + pair + 1)
                            body(psum[:, b, :], pair * W_SLOTS + (s - W_SLOTS * base), h).then_inc(proj_out[b], 1)

            def forget(ps, c, h):
                act.activation(logf[:, ds(c, 1), h * HALF:(h + 1) * HALF], ps, ACT.Sigmoid)
                return act.activation(key[:, ds(c, 1), h * HALF:(h + 1) * HALF], ps, ACT.Sigmoid, scale=-1.0)

            def gate(ps, c, h):
                return act.activation(glu[:, ds(c, 1), PAD + h * HALF:PAD + (h + 1) * HALF], ps, ACT.Sigmoid)

            def silu_to(buf):
                return lambda ps, c, h: act.activation(buf[:, ds(c, 1), h * HALF:(h + 1) * HALF], ps, ACT.Silu)

            each(F_PAIRS, F_PAIRS[0], forget)
            each(GATE_PAIRS, GATE_PAIRS[0], gate)
            for c in range(CG):
                act.wait_ge(f_ok, BASE + 2 * c + 1)
                act.activation(logf[:, c, :], logf[:, c, :], ACT.Ln).then_inc(ln_ok, 1)
            for t in range(TB):
                act.wait_ge(val_mm, BASE + t + 1)
                act.activation(val[:, t, :], psum[:, 4 + t % 4, :], ACT.Copy).then_inc(val_ok, 1)
            each(Q_PAIRS, Q_PAIRS[0], silu_to(qry))
            each(G_PAIRS, G_PAIRS[0], silu_to(gte))

        @blk.gpsimd
        def _(pool):
            begin(pool, [pad_ok, f_ok])
            pool.dma_start(restart[:, :], const_b[:, P * 8:P * 8 + T]).then_inc(restart_in, 16)
            pool.memset(glu[:, :, 0:PAD], 0.0).then_inc(pad_ok, 1)
            pool.wait_ge(lb_step, BASE + 7)
            for b in range(4):
                pool.wait_ge(proj_out[b], BASE + F_PAIRS[1])
            for c in range(CG):
                pool.tensor_scalar(logf[:, c, :], logf[:, c, :], omlb[:, c:c + 1], lb[:, c:c + 1],
                                   ALU.mult, ALU.add).then_inc(f_ok, 1)
                pool.tensor_scalar(key[:, c, :], key[:, c, :], omlb[:, c:c + 1], 1.0,
                                   ALU.mult, ALU.mult).then_inc(f_ok, 1)

        @blk.vector
        def _(dve):
            begin(dve, [lb_step, conv])
            l0, l1 = param("lb0"), param("lb1")
            dve.tensor_tensor(tmp[0], l0, l1, ALU.max).then_inc(lb_step, 1)
            dve.wait_ge(lb_step, BASE + 1)
            dve.tensor_tensor(tmp[1], l0, tmp[0], ALU.subtract).then_inc(lb_step, 1)
            dve.tensor_tensor(tmp[4], l1, tmp[0], ALU.subtract).then_inc(lb_step, 1)
            dve.wait_ge(lb_exp, BASE + 1)
            dve.tensor_tensor(tmp[5], tmp[2], tmp[3], ALU.add).then_inc(lb_step, 1)
            dve.wait_ge(lb_step, BASE + 4)
            dve.reciprocal(tmp[0], tmp[5]).then_inc(lb_step, 1)
            dve.wait_ge(lb_step, BASE + 5)
            dve.tensor_tensor(lb, tmp[2], tmp[0], ALU.mult).then_inc(lb_step, 1)
            dve.tensor_tensor(omlb, tmp[3], tmp[0], ALU.mult).then_inc(lb_step, 1)
            for b in range(4):
                dve.wait_ge(proj_out[b], BASE + GATE_PAIRS[1])
            with dve.Fori(*A_PAIRS) as pair:
                for s in range(W_SLOTS):
                    for h in range(NH):
                        b = 2 * s + h
                        dve.wait_ge(proj[b], BASE + pair + 1)
                        at = glu[:, ds(pair * W_SLOTS + (s - W_SLOTS * A_PAIRS[0]), 1),
                                 PAD + h * HALF:PAD + (h + 1) * HALF].rearrange("p a n -> p (a n)")
                        dve.tensor_tensor(at, at, psum[:, b, :], ALU.mult).then_inc(proj_out[b], 1)
            dve.wait_ge(restart_in, 16)
            for c in range(CG):
                dve.wait_ge(ln_ok, BASE + c + 1)
                dve.tensor_tensor_scan(logf[:, c, :], restart[:, :], logf[:, c, :], 0.0, ALU.mult, ALU.add)
            dve.wait_ge(pad_ok, BASE + 1)
            for b in range(4):
                dve.wait_ge(proj_out[b], BASE + A_PAIRS[1])
            cw, cbias = param("conv_w"), param("conv_b")
            for c in range(CG):
                dve.tensor_scalar(y[:, c, :], glu[:, c, 0:T], cw[:, c * TAPS:c * TAPS + 1], cbias[:, c:c + 1],
                                  ALU.mult, ALU.add).then_inc(conv, 1)
            with dve.Fori(1, TAPS) as tap:
                for c in range(CG):
                    dve.wait_ge(conv, BASE + CG * tap + (c + 1 - CG))
                    dve.scalar_tensor_tensor(out=y[:, c, :], in0=glu[:, c, ds(tap, T)],
                                             scalar=cw[:, ds(tap + c * TAPS, 1)], in1=y[:, c, :],
                                             op0=ALU.mult, op1=ALU.add).then_inc(conv, 1)

    used = [0]

    def carve(n):
        flat = xn[:, :, :].rearrange("p a n -> p (a n)")
        used[0] += n
        return flat[:, used[0] - n:used[0]]

    lev = [carve(CG * P).rearrange("p (h t) -> p h t", h=CG) for _ in range(LEVELS)]
    k_end = carve(CG * P).rearrange("p (h t) -> p h t", h=CG)
    q_beg = carve(CG * P).rearrange("p (h t) -> p h t", h=CG)
    k_blk = carve(CG * P).rearrange("p (h t) -> p h t", h=CG)
    v_blk = carve(CG * P).rearrange("p (h t) -> p h t", h=CG)
    att = carve(CG * P).rearrange("p (h t) -> p h t", h=CG)
    k_end_t = carve(CG * P).rearrange("p (h t) -> p h t", h=CG)
    state = [carve(CG * P).rearrange("p (h t) -> p h t", h=CG) for _ in range(2)]
    decay = carve(3 * CG).rearrange("p (h c) -> p h c", h=CG)

    LV = LEVELS
    init = sems("hg_init")
    x_sub, x_exp, k_mul, q_mul = sems("x_sub"), sems("x_exp"), sems("k_mul"), sems("q_mul")
    sc_mm, sc_ok = sems("sc_mm"), sems("sc_ok")
    kt_mm, kt_ok = sems("kt_mm"), sems("kt_ok")
    u_mm, s_ok, o_mm, o_ok = sems("u_mm"), sems("s_ok"), sems("o_mm"), sems("o_ok")

    def bank(i):
        return psum[:, i, :].rearrange("p (h t) -> p h t", h=CG)

    def seg(ap, n):
        return ap.rearrange("p h (s i) -> p h s i", i=n)

    with nc.Block() as blk:
        @blk.vector
        def _(dve):
            begin(dve, [init, x_sub, q_mul, sc_ok, s_ok])
            dve.memset(att, 0.0)
            dve.memset(state[0], 0.0).then_inc(init, 1)
            dve.wait_ge(init, BASE + 1)
            with dve.Fori(0, TB) as n:
                b_blk = logf[:, :, ds(n * P, P)]
                q_blk = qry[:, :, ds(n * P, P)]
                dve.wait_ge(sc_mm, BASE + n * (LV + 1))
                for l in range(LV):
                    hs = CHUNK >> (l + 1)
                    for hh in range(CG):
                        bs = b_blk[:, hh, :].rearrange("p (s i) -> p s i", i=2 * hs)
                        ref = bs[:, :, hs - 1:hs].to_broadcast([P, P // (2 * hs), 2 * hs])
                        last = dve.tensor_tensor(lev[l][:, hh, :].rearrange("p (s i) -> p s i", i=2 * hs),
                                                 bs, ref, ALU.subtract)
                    last.then_inc(x_sub, 1)
                dve.wait_ge(kt_mm, BASE + n)
                bs = seg(b_blk, CHUNK)
                dve.tensor_tensor(seg(k_end, CHUNK), bs,
                                  bs[:, :, :, CHUNK - 1:CHUNK].to_broadcast([P, CG, P // CHUNK, CHUNK]),
                                  ALU.subtract).then_inc(x_sub, 1)
                for l in range(LV):
                    hs = CHUNK >> (l + 1)
                    dve.wait_ge(x_exp, BASE + n * (LV + 3) + (l + 1))
                    a = seg(lev[l], 2 * hs)[:, :, :, hs:2 * hs]
                    dve.tensor_tensor(a, a, seg(q_blk, 2 * hs)[:, :, :, hs:2 * hs], ALU.mult).then_inc(q_mul, 1)
                dve.wait_ge(x_exp, BASE + n * (LV + 3) + (LV + 2))
                dve.tensor_tensor(q_beg, q_beg, q_blk, ALU.mult).then_inc(q_mul, 1)
                dve.wait_ge(o_mm, BASE + 2 * n)
                for l in range(LV + 1):
                    dve.wait_ge(sc_mm, BASE + n * (LV + 1) + (l + 1))
                    dve.wait_ge(sc_ok, BASE + n * (LV + 1) + l)
                    dve.memset(decay[:, 0:1, 2:3], 0.0)
                    mask = cm[:, l * P:(l + 1) * P].rearrange("p (a t) -> p a t", a=1).to_broadcast([P, CG, P])
                    dve.copy_predicated(att, mask, bank(l % 2)).then_inc(sc_ok, 1)
                for c in range(2):
                    dve.wait_ge(u_mm, BASE + 2 * n + (c + 1))
                    dve.wait_ge(s_ok, BASE + 2 * n + c)
                    if c == 0:
                        dve.wait_ge(x_exp, BASE + n * (LV + 3) + (LV + 3))
                    else:
                        dve.wait_ge(o_mm, BASE + 2 * n + 1)
                    for hh in range(CG):
                        last = dve.scalar_tensor_tensor(out=state[1 - c][:, hh, :], in0=state[c][:, hh, :],
                                                        scalar=decay[:, hh, c:c + 1], in1=bank(3 + c)[:, hh, :],
                                                        op0=ALU.mult, op1=ALU.add)
                    last.then_inc(s_ok, 1)

        @blk.scalar
        def _(act):
            begin(act, [x_exp, kt_ok, o_ok])
            with act.Fori(0, TB) as n:
                b_blk = logf[:, :, ds(n * P, P)]
                for l in range(LV):
                    hs = CHUNK >> (l + 1)
                    act.wait_ge(x_sub, BASE + n * (LV + 1) + (l + 1))
                    a = seg(lev[l], 2 * hs)
                    act.activation(a[:, :, :, 0:hs], a[:, :, :, 0:hs], ACT.Exp, scale=-1.0)
                    act.activation(a[:, :, :, hs:2 * hs], a[:, :, :, hs:2 * hs], ACT.Exp).then_inc(x_exp, 1)
                act.wait_ge(x_sub, BASE + n * (LV + 1) + (LV + 1))
                act.activation(k_end, k_end, ACT.Exp, scale=-1.0).then_inc(x_exp, 1)
                act.wait_ge(o_mm, BASE + 2 * n)
                act.activation(q_beg, b_blk, ACT.Exp).then_inc(x_exp, 1)
                act.wait_ge(s_ok, BASE + 2 * n)
                act.activation(decay[:, :, 0:2], seg(b_blk, CHUNK)[:, :, :, CHUNK - 1], ACT.Exp).then_inc(x_exp, 1)
                act.wait_ge(kt_mm, BASE + n + 1)
                act.wait_ge(u_mm, BASE + 2 * n)
                act.activation(k_end_t, bank(2), ACT.Copy).then_inc(kt_ok, 1)
                act.wait_ge(o_mm, BASE + 2 * n + 2)
                act.activation(y[:, 4:8, ds(n * P, P)], bank(5), ACT.Copy).then_inc(o_ok, 1)

        @blk.gpsimd
        def _(pool):
            begin(pool, [k_mul])
            with pool.Fori(0, TB) as n:
                kb = key[:, :, ds(n * P, P)]
                pool.wait_ge(o_mm, BASE + 2 * n)
                pool.tensor_copy(v_blk, val[:, ds(n, 1), :].rearrange("p a (h t) -> p (a h) t", h=CG))
                pool.tensor_copy(k_blk, kb).then_inc(k_mul, 1)
                pool.wait_ge(k_mul, BASE + n * (LV + 2) + 1)
                for l in range(LV):
                    hs = CHUNK >> (l + 1)
                    pool.wait_ge(x_exp, BASE + n * (LV + 3) + (l + 1))
                    a = seg(lev[l], 2 * hs)[:, :, :, 0:hs]
                    pool.tensor_tensor(a, a, seg(k_blk, 2 * hs)[:, :, :, 0:hs], ALU.mult).then_inc(k_mul, 1)
                pool.wait_ge(x_exp, BASE + n * (LV + 3) + (LV + 1))
                pool.tensor_tensor(k_end, k_end, k_blk, ALU.mult).then_inc(k_mul, 1)

        @blk.tensor
        def _(pe):
            begin(pe, [sc_mm, kt_mm, u_mm, o_mm])
            pe.wait_ge(init, BASE + 1)
            with pe.Fori(0, TB) as n:
                q_blk = qry[:, :, ds(n * P, P)]
                for l in range(LV + 1):
                    if l < LV:
                        pe.wait_ge(q_mul, BASE + n * (LV + 1) + (l + 1))
                        pe.wait_ge(k_mul, BASE + n * (LV + 2) + (l + 2))
                    pe.wait_ge(sc_ok, BASE + n * (LV + 1) + max(l - 1, 0))
                    for hh in range(CG):
                        if l < LV:
                            last = pe.matmul(bank(l % 2)[:, hh, :], lev[l][:, hh, :], lev[l][:, hh, :],
                                             start=True, stop=True)
                        else:
                            last = pe.matmul(bank(l % 2)[:, hh, :], k_blk[:, hh, :], q_blk[:, hh, :],
                                             start=True, stop=True)
                    last.then_inc(sc_mm, 1)
                pe.wait_ge(k_mul, BASE + n * (LV + 2) + (LV + 2))
                pe.wait_ge(kt_ok, BASE + n)
                for hh in range(CG):
                    last = pe.transpose(bank(2)[:, hh, :], k_end[:, hh, :], ident)
                last.then_inc(kt_mm, 1)
                pe.wait_ge(kt_ok, BASE + n + 1)
                pe.wait_ge(s_ok, BASE + 2 * n)
                for c in range(2):
                    r = slice(c * CHUNK, (c + 1) * CHUNK)
                    for hh in range(CG):
                        last = pe.matmul(bank(3 + c)[:, hh, :], k_end_t[r, hh, :], v_blk[r, hh, :],
                                         start=True, stop=True)
                    last.then_inc(u_mm, 1)
                pe.wait_ge(sc_ok, BASE + n * (LV + 1) + (LV + 1))
                pe.wait_ge(o_ok, BASE + n)
                for hh in range(CG):
                    pe.matmul(bank(5)[:, hh, :], v_blk[:, hh, :], att[:, hh, :], start=(hh == 0), stop=False,
                              skip_group_check=True)
                pe.wait_ge(q_mul, BASE + n * (LV + 1) + (LV + 1))
                for c in range(2):
                    pe.wait_ge(s_ok, BASE + 2 * n + c)
                    for hh in range(CG):
                        last = pe.matmul(bank(5)[:, hh, c * CHUNK:(c + 1) * CHUNK], state[c][:, hh, :],
                                         q_beg[:, hh, c * CHUNK:(c + 1) * CHUNK], start=False,
                                         stop=(c == 1), skip_group_check=True)
                    last.then_inc(o_mm, 1)

    rt = xn[:, :, :].rearrange("p a (b n) -> p (a b) n", b=2)
    yt = y[:, :, :].rearrange("p a (b n) -> p (a b) n", b=2)
    N = 2 * 2 * CG
    CV = 2 * CG
    mean_mm, mean_ok, sq_ok, ms_mm = sems("cn_mean_mm"), sems("cn_mean_ok"), sems("cn_sq"), sems("cn_ms_mm")
    ms_ok, rt_ok, rc_ok, ya_ok = sems("cn_ms_ok"), sems("cn_rt"), sems("cn_rc"), sems("cn_ya")
    mix_done = sems("mix_done")

    with nc.Block() as blk:
        @blk.tensor
        def _(pe):
            begin(pe, [mean_mm, ms_mm])
            with pe.Fori(0, CV // 4) as i:
                for j in range(4):
                    pe.wait_ge(mean_ok, BASE + 4 * i)
                    pe.matmul(psum[:, j, :], group_mean, yt[:, ds(4 * i + j, 1), :].rearrange("p a n -> p (a n)"),
                              start=True, stop=True).then_inc(mean_mm, 1)
            with pe.Fori(0, N // 4) as i:
                for j in range(4):
                    pe.wait_ge(sq_ok, BASE + 4 * i + j + 1)
                    pe.wait_ge(ms_ok, BASE + 4 * i)
                    sq = rt[:, ds(4 * i + j, 1), :].rearrange("p a n -> p (a n)")
                    pe.matmul(psum[:, j, :], group_mean, sq, start=True, stop=True)
                    pe.matmul(psum[:, 4 + j, :], head_mean, sq, start=True, stop=True).then_inc(ms_mm, 1)

        @blk.scalar
        def _(act):
            begin(act, [sq_ok, rt_ok])
            with act.Fori(0, N) as i:
                act.wait_ge(mean_ok, BASE + CV)
                act.activation(rt[:, ds(i, 1), :], yt[:, ds(i, 1), :], ACT.Square).then_inc(sq_ok, 1)
            with act.Fori(0, N) as i:
                act.wait_ge(ms_ok, BASE + i + 1)
                act.activation(rt[:, ds(i, 1), :], rt[:, ds(i, 1), :], ACT.Sqrt).then_inc(rt_ok, 1)
            g, b = param("conv_g"), param("conv_nb")
            for c in range(CG):
                act.wait_ge(ya_ok, BASE + 2 * c + 2)
                act.activation(y[:, c, :], y[:, c, :], ACT.Silu, scale=g[:, c:c + 1],
                               bias=b[:, c:c + 1]).then_inc(mix_done, 1)

        @blk.vector
        def _(dve):
            begin(dve, [mean_ok, ms_ok, rc_ok, ya_ok])
            with dve.Fori(0, CV // 4) as i:
                for j in range(4):
                    dve.wait_ge(mean_mm, BASE + 4 * i + j + 1)
                    a = yt[:, ds(4 * i + j, 1), :].rearrange("p a n -> p (a n)")
                    dve.tensor_tensor(a, a, psum[:, j, :], ALU.subtract).then_inc(mean_ok, 1)
            for first, base in ((0, 0), (CV // 4, 4)):
                with dve.Fori(first, first + CV // 4) as i:
                    for j in range(4):
                        dve.wait_ge(ms_mm, BASE + 4 * i + j + 1)
                        dve.tensor_scalar(rt[:, ds(4 * i + j, 1), :].rearrange("p a n -> p (a n)"),
                                          psum[:, base + j, :], EPS, None, ALU.add).then_inc(ms_ok, 1)
            with dve.Fori(0, N) as i:
                dve.wait_ge(rt_ok, BASE + i + 1)
                a = rt[:, ds(i, 1), :]
                dve.reciprocal(a, a).then_inc(rc_ok, 1)
            with dve.Fori(0, N) as i:
                dve.wait_ge(rc_ok, BASE + i + 1)
                a = yt[:, ds(i, 1), :]
                dve.tensor_tensor(a, a, rt[:, ds(i, 1), :], ALU.mult).then_inc(ya_ok, 1)
            g = param("hgrn_g")
            for c in range(CG):
                dve.wait_ge(ya_ok, BASE + CV + 2 * c + 2)
                dve.scalar_tensor_tensor(out=y[:, CG + c, :], in0=y[:, CG + c, :], scalar=g[:, c:c + 1],
                                         in1=gte[:, c, :], op0=ALU.mult, op1=ALU.mult)


def project_out(nc, ctx, sb, sems, psum, y, h_acc, x, w_out):
    wo = sb(ctx, "wo", [P, KC, D], F32)
    wo_in, x_in, o_mm, h_ok = sems("wo_in"), sems("x_in"), sems("wo_mm"), sems("h_ok")
    with nc.Block() as blk:
        @blk.sync
        def _(sp):
            sp.dma_start(wo[:, :, :], w_out.rearrange("(k p) n -> p k n", p=P)).then_inc(wo_in, 16)
            sp.dma_start(h_acc[:, :, :], x.rearrange("(t p) n -> p t n", p=P)).then_inc(x_in, 16)

        @blk.tensor
        def _(pe):
            pe.wait_ge(wo_in, 16)
            for i in range(2 * TB):
                t, h = i // 2, i % 2
                if i >= 8:
                    pe.wait_ge(h_ok, i - 7)
                for k in range(KC):
                    last = pe.matmul(psum[:, i % 8, :], y[:, k, t * P:(t + 1) * P],
                                     wo[:, k, h * HALF:(h + 1) * HALF], start=(k == 0), stop=(k == KC - 1))
                last.then_inc(o_mm, 1)

        @blk.vector
        def _(dve):
            dve.wait_ge(x_in, 16)
            for i in range(2 * TB):
                t, h = i // 2, i % 2
                dve.wait_ge(o_mm, i + 1)
                a = h_acc[:, t, h * HALF:(h + 1) * HALF]
                dve.tensor_tensor(a, a, psum[:, i % 8, :], ALU.add).then_inc(h_ok, 1)


def queries(nc, ctx, sb, sems, psum, xn2, xh, xl, w_q, keys, scores):
    wr = sb(ctx, "wq_ring", [P, 2, D], F32)
    qt = sb(ctx, "qt", [P, 2, T], F32)
    kt = sb(ctx, "kt", [P, HP, NK], F32)
    k_in = sems("keys_in")
    w_in = [sems(f"wq_in{s}") for s in range(2)]
    q_mm = [sems(f"q_mm{b}") for b in range(4)]
    q_ok = [sems(f"q_ok{b}") for b in range(4)]
    s_mm = [sems(f"s_mm{b}") for b in range(4)]
    s_ok = [sems(f"s_ok{b}") for b in range(4)]
    hi_ok = sems("xh_ok")
    lo_ok = sems("xl_ok")
    with nc.Block() as blk:
        @blk.sync
        def _(sp):
            sp.dma_start(kt[:, :, :], keys).then_inc(k_in, 16)
            with sp.Fori(0, HP // 2) as pair:
                for s in range(2):
                    sp.wait_ge(q_mm[2 * s + 1], BASE + pair)
                    sp.dma_start(wr[:, s, :], w_q[ds(pair * 2 + s, 1), :, :].rearrange(
                        "a p n -> (a p) n")).then_inc(w_in[s], 16)

        @blk.tensor
        def _(pe):
            begin(pe, [*q_mm, *s_mm])
            pe.wait_ge(k_in, 16)
            with pe.Fori(0, HP // 2) as pair:
                for s in range(2):
                    pe.wait_ge(w_in[s], 16 * pair + 16)
                    for h in range(NH):
                        b = 2 * s + h
                        pe.wait_ge(q_ok[b], BASE + pair)
                        for k in range(KC):
                            last = pe.matmul(psum[:, b, :], wr[:, s, k * P:(k + 1) * P],
                                             xn2[:, k, h * HALF:(h + 1) * HALF],
                                             start=(k == 0), stop=(k == KC - 1))
                        last.then_inc(q_mm[b], 1)
                for s in range(2):
                    for h in range(NH):
                        b = 2 * s + h
                        pe.wait_ge(q_ok[b], BASE + pair + 1)
                        pe.wait_ge(s_ok[b], BASE + pair)
                        for j in range(4):
                            last = pe.matmul(psum[:, 4 + b, j * P:(j + 1) * P],
                                             qt[:, s, h * HALF + j * P:h * HALF + (j + 1) * P],
                                             kt[:, ds(2 * pair + s, 1), :].rearrange("p a n -> p (a n)"),
                                             start=True, stop=True)
                        last.then_inc(s_mm[b], 1)

        @blk.scalar
        def _(act):
            begin(act, [*q_ok, hi_ok])
            with act.Fori(0, HP // 2) as pair:
                for b in range(4):
                    act.wait_ge(q_mm[b], BASE + pair + 1)
                    act.wait_ge(s_mm[b], BASE + pair)
                    act.activation(qt[:, b // 2, (b % 2) * HALF:(b % 2 + 1) * HALF], psum[:, b, :],
                                   ACT.Copy).then_inc(q_ok[b], 1)
            for k in range(KC):
                act.activation(xh[:, k, :], xn2[:, k, :], ACT.Copy).then_inc(hi_ok, 1)

        @blk.gpsimd
        def _(pool):
            for k in range(KC):
                pool.wait_ge(hi_ok, BASE + k + 1)
                pool.tensor_tensor(xl[:, k, :], xn2[:, k, :], xh[:, k, :], ALU.subtract).then_inc(lo_ok, 1)

        @blk.vector
        def _(dve):
            begin(dve, s_ok)
            with dve.Fori(0, HP // 2) as pair:
                for s in range(2):
                    for h in range(NH):
                        b = 2 * s + h
                        dve.wait_ge(s_mm[b], BASE + pair + 1)
                        dve.tensor_copy(scores[:, 4 * h:4 * h + 4, ds(2 * pair + s, 1), :].rearrange(
                            "p t a n -> p t (a n)"),
                            psum[:, 4 + b, :].rearrange("p (t n) -> p t n", t=4)).then_inc(s_ok[b], 1)


def after(eng, sem, count):
    if not (isinstance(count, int) and count <= 0):
        eng.wait_ge(sem, count)


def select_and_activate(nc, ctx, sb, sems, psum, scores, ident, iota16, const_b, xh, xl, u_t, gates, acts):
    PICK = 6
    PICKED = PICK * TB
    OCT = 8
    SPREAD = T // OCT // 2
    ALONE = NK - PICKED - SPREAD
    LOOP = 4
    FIRST_G = PICKED
    assert ALONE > 0 and ALONE % 2 == 0 and SPREAD % LOOP == 0

    uf = sb(ctx, "uf", [P, 2, D], F32)
    uh = sb(ctx, "uh", [P, 2, D], BF16)
    ul = sb(ctx, "ul", [P, 2, D], BF16)
    ge = sb(ctx, "ge", [P, 2, T], F32)

    sc = sb(ctx, "tk_sc", [P, HP, NK], F32)
    work = sb(ctx, "tk_work", [P, 2 * SEL * TOPK], F32)
    best = sb(ctx, "tk_best", [P, HP, TOPK], F32)
    bidx = sb(ctx, "tk_bidx", [P, HP, TOPK], U32)
    bidf = sb(ctx, "tk_bidf", [P, HP, TOPK], F32)
    tops = sb(ctx, "tk_tops", [P, HEADS, TOPK], F32)
    ci = sb(ctx, "tk_ci", [P, HEADS, TOPK], U32)
    cab = sb(ctx, "tk_cab", [P, 2, SEL], U32)
    cabf = sb(ctx, "tk_cabf", [P, 2, SEL], F32)
    sel = sb(ctx, "tk_sel", [P, 3, SEL], F32)
    ex = sb(ctx, "tk_ex", [P, HEADS, TOPK], F32)
    es = sb(ctx, "tk_es", [P, 2, HEADS], F32)
    spare = sb(ctx, "tk_spare", [P, 2], F32)
    rest = work[:, 0:HP * NK].rearrange("p (h n) -> p h n", h=HP)
    crest = work[:, 0:HP * NK].rearrange("p (h n) -> p h n", h=HEADS)
    hit = work[:, :].rearrange("p (i k a) -> p i k a", i=2, k=SEL)
    cand = sc[:, :, :].rearrange("p (h a) n -> p h (a n)", a=2)

    picks = sb(ctx, "picks", [P, 2, T], BF16)
    gate = sb(ctx, "gate", [P, T], F32)
    parts = sb(ctx, "gate_parts", [P, 2, T], BF16)

    flat = scores[:, :, :, :].rearrange("p a h n -> p (a h n)")
    tile = flat[:, 0:2 * NK * GT].rearrange("p (u c t) -> p u c t", u=2, c=NK)
    hot = flat[:, 2 * NK * GT:2 * NK * GT + 2 * 4 * P * OCT // 2].bitcast(BF16).rearrange(
        "p (r n i t) -> p r n i t", r=2, n=4, i=P)
    at = 2 * NK * GT + 4 * P * OCT
    iota_x = flat[:, at:at + P * OCT // 2].bitcast(BF16).rearrange("p (i t) -> p i t", t=OCT)

    u_in = [sems(f"u_in{s}") for s in range(2)]
    ge_st = [sems(f"ge_st{s}") for s in range(2)]
    g_st = [sems(f"g_st{s}") for s in range(2)]
    u_hi, u_lo, a_mm, a_ge = sems("u_hi"), sems("u_lo"), sems("a_mm"), sems("a_ge")
    sc_in, step, e_ok, tp, tp_ok = sems("tk_in"), sems("tk_step"), sems("tk_e_ok"), sems("tk_tp"), sems("tk_tp_ok")
    chosen, found = sems("tk_chosen"), sems("tk_found")
    iota_in, pre, two_hot, hot_ok, g_mm, g_ok = (sems(n) for n in (
        "iota_in", "g_pre", "two_hot", "hot_ok", "g_mm", "g_ok"))
    STEPS = 15
    CAND_DONE = 9
    EXP_IN = 11

    def slots(eng, pick, spread, between=None):
        for j in range(PICK):
            pick(j, j % 2, 0, j)
        with eng.Fori(1, TB) as n:
            for j in range(PICK):
                pick(PICK * n + j, j % 2, n, j)
        if between is not None:
            between()
        for j in range(LOOP):
            spread(PICKED + j, j % 2, 0, j)
        with eng.Fori(1, SPREAD // LOOP) as n:
            for j in range(LOOP):
                spread(LOOP * n + (PICKED + j), j % 2, n, j)
        with eng.Fori(0, ALONE // 2 - 1) as n:
            for j in range(2):
                pick(2 * n + (PICKED + SPREAD + j), j, None, n)
        for j in range(2):
            pick(NK - 2 + j, j, None, ALONE // 2 - 1)

    def half_pick(n, j):
        return j + (PICKED + SPREAD) // 2 if n is None else (PICK // 2) * n + j // 2

    def half_spread(n, j):
        return (LOOP // 2) * n + (PICKED // 2 + j // 2)

    def more(s):
        return not (isinstance(s, int) and s >= NK - 2)

    with nc.Block() as blk:
        @blk.sync
        def _(sp):
            def load(s, par):
                after(sp, u_lo, s - 1)
                sp.dma_start(uf[:, par, :], u_t[ds(s, 1), :, :].rearrange("a p n -> (a p) n")).then_inc(u_in[par], 16)

            def pick(s, par, n, j):
                if more(s):
                    load(s + 2, par)
                sp.wait_ge(a_ge, 2 * s + 2)
                sp.dma_start(acts[ds(s, 1), :, :].rearrange("a p n -> (a p) n"), ge[:, par, :]).then_inc(ge_st[par], 16)

            def spread(s, par, n, j):
                pick(s, par, n, j)
                if j % 2 == 1:
                    u = j // 2
                    sp.wait_ge(g_ok, 16 * n + (8 * u + 8))
                    sp.dma_start(gates[ds(2 * n + u, 1), :, :].rearrange("a p n -> (a p) n"),
                                 tile[:, u, :, :].rearrange("p c t -> p (c t)")).then_inc(g_st[u], 16)

            for s in range(2):
                load(s, s)
            slots(sp, pick, spread)
            for par in range(2):
                sp.wait_ge(ge_st[par], 16 * NK // 2)
                sp.wait_ge(g_st[par], 16 * (SPREAD // LOOP))

        @blk.tensor
        def _(pe):
            def unit(s, par, h):
                after(pe, a_ge, 2 * s + (h - 3))
                cols = slice(h * HALF, (h + 1) * HALF)
                a = psum[:, 2 * par + h, :]
                for n in range(KC):
                    row = slice(n * P, (n + 1) * P)
                    pe.matmul(a, uh[:, par, row], xh[:, n, cols], start=(n == 0), stop=False)
                    pe.matmul(a, uh[:, par, row], xl[:, n, cols], start=False, stop=False)
                    last = pe.matmul(a, ul[:, par, row], xh[:, n, cols], start=False, stop=(n == KC - 1))
                last.then_inc(a_mm, 1)

            def pick(s, par, n, j):
                pe.wait_ge(u_hi, s + 1)
                pe.wait_ge(u_lo, s + 1)
                unit(s, par, 0)
                unit(s, par, 1)
                if n is not None and j == PICK - 1:
                    pe.wait_ge(step, STEPS * n + STEPS)
                    after(pe, tp_ok, 2 * n)
                    for i in range(3):
                        last = pe.transpose(psum[:, 7, i * P:(i + 1) * P], sel[:, i, :], ident)
                    last.then_inc(tp, 1)

            def octet(n, o):
                r = o % 2
                pe.wait_ge(hot_ok, 8 * n + (o + 1))
                after(pe, g_ok, 16 * n + (2 * o - 2))
                for b in range(2):
                    for q in range(4):
                        t = 4 * b + q
                        for part in (2, 3):
                            last = pe.matmul(psum[:, 4 + 2 * r + b, q * P:(q + 1) * P], hot[:, r, 0, :, t],
                                             hot[:, r, part, :, t], start=(part == 2), stop=(part == 3))
                last.then_inc(g_mm, 1)

            def spread(s, par, n, j):
                pe.wait_ge(u_hi, s + 1)
                pe.wait_ge(u_lo, s + 1)
                for h in range(2):
                    unit(s, par, h)
                    octet(n, 2 * j + h)

            slots(pe, pick, spread)

        @blk.scalar
        def _(act):
            def split(par, half):
                act.wait_ge(u_in[par], 16 * half + 16)
                act.activation(uh[:, par, :], uf[:, par, :], ACT.Copy).then_inc(u_hi, 1)

            def gelu(s, par, h, half):
                act.wait_ge(a_mm, 2 * s + (h + 1))
                if h == 0:
                    after(act, ge_st[par], 16 * half)
                act.activation(ge[:, par, h * HALF:(h + 1) * HALF], psum[:, 2 * par + h, :],
                               ACT.Gelu).then_inc(a_ge, 1)

            def pick(s, par, n, j):
                if n is not None and j == 0:
                    after(act, step, STEPS * n - STEPS + CAND_DONE)
                    act.activation(sc[:, :, :], scores[:, ds(n, 1), :, :].rearrange("p a h n -> p (a h) n"),
                                   ACT.Copy).then_inc(sc_in, 1)
                half = half_pick(n, j)
                gelu(s, par, 0, half)
                gelu(s, par, 1, half)
                if more(s):
                    split(par, half + 1)
                if n is not None and j == PICK - 3:
                    act.wait_ge(step, STEPS * n + EXP_IN)
                    act.activation(ex[:, :, :], ex[:, :, :], ACT.Exp).then_inc(e_ok, 1)
                if n is not None and j == PICK - 1:
                    act.wait_ge(tp, n + 1)
                    act.activation(picks[:, :, ds(n * P, P)],
                                   psum[:, 7, 0:2 * P].rearrange("p (a t) -> p a t", a=2), ACT.Copy).then_inc(tp_ok, 1)
                    act.activation(gate[:, ds(n * P, P)], psum[:, 7, 2 * P:3 * P], ACT.Copy).then_inc(tp_ok, 1)

            def spread(s, par, n, j):
                half = half_spread(n, j)
                for h in range(2):
                    gelu(s, par, h, half)
                    o = 2 * j + h
                    u, r = o // 4, o % 2
                    act.wait_ge(g_mm, 8 * n + (o + 1))
                    if o % 4 == 0:
                        after(act, g_st[u], 16 * n)
                    for b in range(2):
                        at = OCT * (o % 4) + 4 * b
                        act.activation(tile[:, u, :, at:at + 4].rearrange("p c t -> p t c"),
                                       psum[:, 4 + 2 * r + b, :].rearrange("p (t c) -> p t c", t=4),
                                       ACT.Copy).then_inc(g_ok, 1)
                split(par, half + 1)

            split(0, 0)
            split(1, 0)
            slots(act, pick, spread)

        @blk.gpsimd
        def _(pool):
            def low(s, par):
                pool.wait_ge(u_hi, s + 1)
                pool.tensor_tensor(ul[:, par, :], uf[:, par, :], uh[:, par, :], ALU.subtract).then_inc(u_lo, 1)

            def pick(s, par, n, j):
                if more(s):
                    low(s + 2, par)
                if n is not None and j == PICK - 3:
                    pool.wait_ge(chosen, n + 1)
                    for i in range(2):
                        for h in range(HEADS):
                            idx = bidf[:, 2 * h + i:2 * h + i + 1, :].to_broadcast([P, TOPK, TOPK])
                            a = hit[:, i, h * TOPK:(h + 1) * TOPK, :]
                            last = pool.tensor_tensor(a, a, idx, ALU.mult)
                    last.then_inc(found, 1)

            def spread(s, par, n, j):
                low(s + 2, par)

            def load_iota():
                pool.wait_ge(sc_in, TB)
                pool.dma_start(iota_x, const_b[:, 0:P * OCT].rearrange("p (i t) -> p i t", t=OCT)).then_inc(iota_in, 16)

            low(0, 0)
            low(1, 1)
            slots(pool, pick, spread, load_iota)

        @blk.vector
        def _(dve):
            def search(n):
                done = [0]

                def then(ins):
                    done[0] += 1
                    ins.then_inc(step, 1)
                    dve.wait_ge(step, STEPS * n + done[0])
                    dve.memset(spare[:, 0:1], 0.0)

                dve.wait_ge(sc_in, n + 1)
                dve.memset(spare[:, 1:2], 0.0)
                for h in range(HP):
                    last = dve.max(best[:, h, 0:8], sc[:, h, :])
                then(last)
                for h in range(HP):
                    dve.match_replace(rest[:, h, :], best[:, h, 0:8], sc[:, h, :], NEG)
                    last = dve.max_index(bidx[:, h, 0:8], best[:, h, 0:8], sc[:, h, :])
                then(last)
                for h in range(HP):
                    last = dve.max(best[:, h, 8:16], rest[:, h, :])
                then(last)
                for h in range(HP):
                    last = dve.max_index(bidx[:, h, 8:16], best[:, h, 8:16], rest[:, h, :])
                then(last)
                two = best[:, :, :].rearrange("p (h a) k -> p h a k", a=2)
                a = two[:, :, 0:1, :].rearrange("p h a k -> p h k a").to_broadcast([P, HEADS, TOPK, TOPK])
                b = two[:, :, 1:2, :].to_broadcast([P, HEADS, TOPK, TOPK])
                dve.tensor_copy(bidf[:, :, :], bidx[:, :, :])
                then(dve.tensor_tensor(cand.rearrange("p h (a b) -> p h a b", a=TOPK), a, b, ALU.add))
                for h in range(HEADS):
                    last = dve.max(tops[:, h, 0:8], cand[:, h, :])
                then(last)
                for h in range(HEADS):
                    dve.match_replace(crest[:, h, :], tops[:, h, 0:8], cand[:, h, :], NEG)
                    last = dve.max_index(ci[:, h, 0:8], tops[:, h, 0:8], cand[:, h, :])
                then(last)
                for h in range(HEADS):
                    last = dve.max(tops[:, h, 8:16], crest[:, h, :])
                then(last)
                for h in range(HEADS):
                    last = dve.max_index(ci[:, h, 8:16], tops[:, h, 8:16], crest[:, h, :])
                then(last)
                assert done[0] == CAND_DONE
                cflat = ci[:, :, :].rearrange("p h k -> p (h k)")
                dve.tensor_scalar(cab[:, 0, :], cflat, 4, None, ALU.logical_shift_right)
                then(dve.tensor_scalar(cab[:, 1, :], cflat, TOPK - 1, None, ALU.bitwise_and))
                dve.tensor_copy(cabf[:, :, :], cab[:, :, :])
                then(dve.tensor_tensor(ex[:, :, :], tops[:, :, :],
                                       tops[:, :, 0:1].to_broadcast([P, HEADS, TOPK]), ALU.subtract))
                for i in range(2):
                    rank = cabf[:, i, :].rearrange("p (k a) -> p k a", a=1).to_broadcast([P, SEL, TOPK])
                    last = dve.tensor_tensor(hit[:, i, :, :], rank, iota16.rearrange(
                        "p (a k) -> p a k", a=1).to_broadcast([P, SEL, TOPK]), ALU.is_equal)
                last.then_inc(chosen, 1)
                dve.wait_ge(e_ok, n + 1)
                then(dve.reduce_sum(es[:, 0, :], ex[:, :, :], AX.X))
                then(dve.reciprocal(es[:, 1, :], es[:, 0, :]))
                after(dve, tp, n)
                then(dve.tensor_tensor(sel[:, 2, :].rearrange("p (h k) -> p h k", h=HEADS), ex[:, :, :],
                                       es[:, 1, :].rearrange("p (h a) -> p h a", a=1).to_broadcast(
                                           [P, HEADS, TOPK]), ALU.mult))
                dve.wait_ge(found, n + 1)
                then(dve.reduce_sum(sel[:, 0:2, :], hit[:, :, :, :], AX.X))
                assert done[0] == STEPS

            def octet(n, o):
                r = o % 2

                def per_token(ap):
                    return ap.rearrange("p (a t) -> p a t", a=1).to_broadcast([P, P, OCT])

                tokens = ds(8 * OCT * n + OCT * o, OCT)
                after(dve, g_mm, 8 * n + (o - 1))
                dve.tensor_tensor(hot[:, r, 1, :, :], iota_x, per_token(picks[:, 1, tokens]),
                                  ALU.is_equal).then_inc(two_hot, 1)
                dve.tensor_tensor(hot[:, r, 0, :, :], iota_x, per_token(picks[:, 0, tokens]), ALU.is_equal)
                dve.wait_ge(two_hot, 8 * n + (o + 1))
                dve.tensor_tensor(hot[:, r, 2, :, :], hot[:, r, 1, :, :], per_token(parts[:, 0, tokens]), ALU.mult)
                dve.tensor_tensor(hot[:, r, 3, :, :], hot[:, r, 1, :, :], per_token(parts[:, 1, tokens]),
                                  ALU.mult).then_inc(hot_ok, 1)

            search(0)
            with dve.Fori(1, TB) as n:
                search(n)
            dve.wait_ge(tp_ok, 2 * TB)
            dve.wait_ge(iota_in, 16)
            dve.tensor_copy(parts[:, 0, :], gate[:, :]).then_inc(pre, 1)
            dve.wait_ge(pre, 1)
            dve.tensor_tensor(parts[:, 1, :], gate[:, :], parts[:, 0, :], ALU.subtract).then_inc(pre, 1)
            dve.wait_ge(pre, 2)
            for o in range(8):
                octet(0, o)
            with dve.Fori(1, T // (8 * OCT)) as n:
                for o in range(8):
                    octet(n, o)


def combine(nc, ctx, sb, sems, psum, h_acc, v_t, gates, acts):
    vf = sb(ctx, "vf", [P, 2, D], F32)
    vh = sb(ctx, "vh", [P, 2, CPG, D], BF16)
    vl = sb(ctx, "vl", [P, 2, CPG, D], BF16)
    gt = sb(ctx, "gt", [P, 2, T // GT, CPG, GT], F32)
    at = sb(ctx, "at", [P, 2, CPG, T], F32)
    wh = sb(ctx, "wh", [P, 2, CPG, T], BF16)
    wl = sb(ctx, "wl", [P, 2, CPG, T], BF16)
    O = 2 * TB
    NB = 8

    v_in = [sems(f"v_in{s}") for s in range(2)]
    g_in = [sems(f"gt_in{s}") for s in range(2)]
    a_in = [sems(f"at_in{s}") for s in range(2)]
    v_hi, v_lo, w_ok, w_hi, w_lo = sems("v_hi"), sems("v_lo"), sems("w_ok"), sems("w_hi"), sems("w_lo")
    y_mm, y_ok = sems("y_mm"), sems("y_ok")

    def groups(eng, body):
        body(0, 0, 0)
        body(1, 1, 0)
        with eng.Fori(1, GROUPS // 2) as i:
            body(2 * i, 0, i)
            body(2 * i + 1, 1, i)

    with nc.Block() as blk:
        @blk.sync
        def _(sp):
            def body(g, par, half):
                after(sp, w_lo, CPG * g - CPG)
                sp.dma_start(gt[:, par, :, :, :].rearrange("p b c t -> p b (c t)"),
                             gates.rearrange("b p (g n) -> g p b n", g=GROUPS)[ds(g, 1), :, :, :].rearrange(
                                 "g p b n -> (g p) b n")).then_inc(g_in[par], 16)
                sp.dma_start(at[:, par, :, :], acts.rearrange("(g c) p n -> g p c n", g=GROUPS)[
                    ds(g, 1), :, :, :].rearrange("g p c n -> (g p) c n")).then_inc(a_in[par], 16)
                for c in range(CPG):
                    after(sp, v_lo, CPG * g + (c - 1))
                    sp.dma_start(vf[:, c % 2, :], v_t[ds(CPG * g + c, 1), :, :].rearrange(
                        "a p n -> (a p) n")).then_inc(v_in[c % 2], 16)

            groups(sp, body)

        @blk.tensor
        def _(pe):
            def body(g, par, half):
                pe.wait_ge(v_lo, CPG * g + CPG)
                pe.wait_ge(w_lo, CPG * g + CPG)
                for o in range(O):
                    rows, cols = slice((o // 2) * P, (o // 2 + 1) * P), slice((o % 2) * HALF, (o % 2 + 1) * HALF)
                    after(pe, y_ok, O * g + (o + 1 - NB))
                    a = psum[:, o % NB, :]
                    for c in range(CPG):
                        pe.matmul(a, wh[:, par, c, rows], vh[:, par, c, cols], start=(c == 0), stop=False)
                        pe.matmul(a, wh[:, par, c, rows], vl[:, par, c, cols], start=False, stop=False)
                        last = pe.matmul(a, wl[:, par, c, rows], vh[:, par, c, cols], start=False,
                                         stop=(c == CPG - 1))
                    last.then_inc(y_mm, 1)

            groups(pe, body)

        @blk.scalar
        def _(act):
            def body(g, par, half):
                after(act, y_mm, O * g - O)
                for c in range(CPG):
                    act.wait_ge(v_in[c % 2], 2 * 16 * g + (16 * (c // 2) + 16))
                    act.activation(vh[:, par, c, :], vf[:, c % 2, :], ACT.Copy).then_inc(v_hi, 1)
                    act.wait_ge(w_ok, CPG * g + (c + 1))
                    act.activation(wh[:, par, c, :], at[:, par, c, :], ACT.Copy).then_inc(w_hi, 1)

            groups(act, body)

        @blk.gpsimd
        def _(pool):
            def body(g, par, half):
                for c in range(CPG):
                    pool.wait_ge(v_hi, CPG * g + (c + 1))
                    pool.tensor_tensor(vl[:, par, c, :], vf[:, c % 2, :], vh[:, par, c, :],
                                       ALU.subtract).then_inc(v_lo, 1)
                    pool.wait_ge(w_hi, CPG * g + (c + 1))
                    pool.tensor_tensor(wl[:, par, c, :], at[:, par, c, :], wh[:, par, c, :],
                                       ALU.subtract).then_inc(w_lo, 1)

            groups(pool, body)

        @blk.vector
        def _(dve):
            def weigh(g, par, half):
                dve.wait_ge(g_in[par], 16 * half + 16)
                dve.wait_ge(a_in[par], 16 * half + 16)
                for c in range(CPG):
                    a = at[:, par, c, :].rearrange("p (b t) -> p b t", t=GT)
                    dve.tensor_tensor(a, a, gt[:, par, :, c, :], ALU.mult).then_inc(w_ok, 1)

            def add(g):
                for o in range(O):
                    dve.wait_ge(y_mm, O * g + (o + 1))
                    after(dve, y_ok, O * g + (o + 1 - O))
                    a = h_acc[:, o // 2, (o % 2) * HALF:(o % 2 + 1) * HALF]
                    dve.tensor_tensor(a, a, psum[:, o % NB, :], ALU.add).then_inc(y_ok, 1)

            weigh(0, 0, 0)
            weigh(1, 1, 0)
            add(0)
            with dve.Fori(1, GROUPS // 2) as i:
                weigh(2 * i, 0, i)
                add(2 * i - 1)
                weigh(2 * i + 1, 1, i)
                add(2 * i)
            add(GROUPS - 1)


def final_norm(nc, ctx, sb, sems, h_acc, small, final_g, out):
    fg = sb(ctx, "fg", [P, D], F32)
    sq = sb(ctx, "fsq", [P, TB, D], F32)
    g_in, sq_ok, ms_ok, rms_ok, rs_ok = (sems(n) for n in ("fg_in", "f_sq", "f_ms", "f_rms", "f_rs"))
    o_ok = sems("f_out")
    stored = sems("stored")
    ss, ms, rms, rstd = (small[:, TB * i:TB * (i + 1)] for i in range(4))
    with nc.Block() as blk:
        @blk.sync
        def _(sp):
            sp.dma_start(fg[:, :], final_g).then_inc(g_in, 16)
            for t in range(TB):
                sp.wait_ge(o_ok, t + 1)
                sp.dma_start(out[t * P:(t + 1) * P, :], sq[:, t, :]).then_inc(stored, 16)
            sp.wait_ge(stored, 16 * TB)

        @blk.scalar
        def _(act):
            for t in range(TB):
                act.activation(sq[:, t, :], h_acc[:, t, :], ACT.Square, accum_out=ss[:, t:t + 1]).then_inc(sq_ok, 1)
            act.wait_ge(ms_ok, 1)
            act.activation(rms, ms, ACT.Sqrt).then_inc(rms_ok, 1)

        @blk.vector
        def _(dve):
            dve.wait_ge(sq_ok, TB)
            dve.tensor_scalar(ms, ss, 1.0 / D, EPS, ALU.mult, ALU.add).then_inc(ms_ok, 1)
            dve.wait_ge(rms_ok, 1)
            dve.reciprocal(rstd, rms).then_inc(rs_ok, 1)
            dve.wait_ge(rs_ok, 1)
            dve.wait_ge(g_in, 16)
            for t in range(TB):
                dve.scalar_tensor_tensor(out=sq[:, t, :], in0=h_acc[:, t, :], scalar=rstd[:, t:t + 1],
                                         in1=fg[:, :], op0=ALU.mult, op1=ALU.mult).then_inc(o_ok, 1)


def _layout(i):
    import numpy as np

    f = np.float32
    c = np.ascontiguousarray
    eye = np.eye(P, dtype=f)
    groups = np.kron(np.eye(P // GROUP, dtype=f), np.full((GROUP, GROUP), 1.0 / GROUP, f))
    heads = np.full((P, P), 1.0 / P, f)
    iota16 = np.broadcast_to(np.arange(TOPK, dtype=f), (P, TOPK))
    restart = np.ones((P, T), f)
    restart[:, ::CHUNK] = 0.0
    iota = np.broadcast_to(np.repeat(np.arange(P, dtype=f), 8), (P, P * 8))
    s, t = np.arange(P)[:, None], np.arange(P)[None, :]
    masks = []
    for level in range(LEVELS):
        n = CHUNK >> level
        masks.append((s // n == t // n) & (s % n < n // 2) & (t % n >= n // 2))
    masks.append(s == t)
    cols = lambda v, n: np.asarray(v, f).reshape(n, P).T
    w_in = np.asarray(i["w_in"])[0].reshape(KC, P, 6, CG, P)
    stream = w_in[:, :, [3, 1, 0, 2, 5]].transpose(2, 3, 1, 0, 4).reshape(5 * CG, P, D)
    w_v = w_in[:, :, 4].reshape(KC, P, HALF).transpose(1, 0, 2)
    conv_w = np.asarray(i["conv_w"])[0].T.reshape(CG, P, TAPS).transpose(1, 0, 2).reshape(P, CG * TAPS)
    params = np.concatenate([
        cols(i["norm_mix_g"], KC), cols(i["norm_ffn_g"], KC), conv_w, cols(i["conv_b"], CG),
        cols(i["conv_norm_g"], CG), cols(i["conv_norm_b"], CG), cols(i["hgrn_norm_g"], CG),
        cols(np.asarray(i["hgrn_lb_logits"])[0], CG), cols(np.asarray(i["hgrn_lb_logits"])[1], CG)], axis=1)
    return {
        "x": c(np.asarray(i["x"]).reshape(T, D)),
        "const_f": c(np.concatenate([eye, groups, heads, iota16], axis=1)),
        "const_b": c(np.concatenate([iota, restart], axis=1)),
        "const_m": c(np.concatenate(masks, axis=1).astype(np.int32)),
        "params": c(params),
        "w_stream": c(stream),
        "w_v": c(w_v),
        "w_out": c(np.asarray(i["w_out"])[0]),
        "w_q": c(np.asarray(i["peer_w_query"])[0].reshape(KC, P, HP, P).transpose(2, 1, 0, 3).reshape(HP, P, D)),
        "keys": c(np.asarray(i["peer_sub_keys"])[0].reshape(HP, NK, P).transpose(2, 0, 1)),
        "u_t": c(np.asarray(i["peer_u"])[0].reshape(NK, NK, KC, P).transpose(1, 3, 2, 0).reshape(NK, P, D)),
        "v_t": c(np.asarray(i["peer_v"])[0].reshape(NK, NK, D).transpose(1, 0, 2)),
        "final_g": c(np.broadcast_to(np.asarray(i["final_norm_g"]), (P, D))),
    }


def kernel(**inputs):
    import numpy as np
    import concourse.bacc as bacc
    from concourse.bass_utils import run_bass_kernel_spmd as run

    nc = bacc.Bacc("TRN2", target_bir_lowering=False, num_devices=1)
    arrays = {f"in_{n}_dram": a for n, a in _layout(inputs).items()}
    args = [nc.dram_tensor(n, a.shape, mybir.dt.from_np(a.dtype), kind="ExternalInput").ap()
            for n, a in arrays.items()]
    args.append(nc.dram_tensor("out_0_dram", (T, D), F32, kind="ExternalOutput").ap())
    args.append(nc.dram_tensor("gates_dram", (T // GT, P, NK * GT), F32, kind="Internal").ap())
    args.append(nc.dram_tensor("acts_dram", (NK, P, T), F32, kind="Internal").ap())
    hybrid_block(nc, *args)
    r = run(nc, [arrays], core_ids=[0])
    return np.asarray(r.results[0]["out_0_dram"]).reshape(1, T, D)
```

```python
from contextlib import ExitStack

import concourse.bass as bass
from concourse import mybir
from concourse.bass import IndirectOffsetOnAxis, ds

P = 128
T = 1024
D = 1024
TB = T // P
KC = D // P
HALF = 512
NH = T // HALF
CG = 4
TAPS = 31
PAD = TAPS - 1
GROUP = 64
CHUNK = 64
LEVELS = 6
HEADS = 8
HP = 2 * HEADS
NK = 128
TOPK = 16
SEL = HEADS * TOPK
GATHERED = 2
DENSE = TB - GATHERED
TD = DENSE * P
DHALF = TD // 2
GT = 32
CPG = 4
GROUPS = NK // CPG
NSTAT = 16
EPS = 1e-6
BASE = 1
FOUR = 4
NEG = -3.0e38
XS = 16.0
WS = 256.0
BACK = 1.0 / (XS * WS)

ALU = mybir.AluOpType
ACT = mybir.ActivationFunctionType
F32 = mybir.dt.float32
BF16 = mybir.dt.bfloat16
F16 = mybir.dt.float16
U32 = mybir.dt.uint32
I32 = mybir.dt.int32
AX = mybir.AxisListType

PAR = {}
_at = 0
for _name, _n in (("conv_w", CG * TAPS), ("conv_b", CG), ("conv_g", CG),
                  ("conv_nb", CG), ("hgrn_g", CG), ("lb0", CG), ("lb1", CG)):
    PAR[_name] = (_at, _at + _n)
    _at += _n
NPAR = _at


def begin(eng, counters, base=BASE):
    for c in counters:
        eng.sem_inc(c, base)


class Ring:

    def __init__(self, sems, label, buffers, base):
        self.wf, self.wh, self.wl = buffers
        self.w_in = [sems(f"{label}_in{s}") for s in range(2)]
        self.w_hi, self.w_lo = sems(f"{label}_hi"), sems(f"{label}_lo")
        self.base = base

    def load(self, sp, s, source):
        sp.dma_start(self.wf[:, s, :], source.rearrange("a p n -> (a p) n")).then_inc(self.w_in[s], 16)

    def high(self, act, s, turn):
        act.wait_ge(self.w_in[s], 16 * turn + 16)
        act.activation(self.wh[:, s, :], self.wf[:, s, :], ACT.Copy, scale=WS)
        act.activation(self.wf[:, s, :], self.wf[:, s, :], ACT.Copy, scale=WS).then_inc(self.w_hi, 1)

    def low(self, pool, s, item):
        pool.wait_ge(self.w_hi, item + (self.base + 1))
        pool.tensor_tensor(self.wl[:, s, :], self.wf[:, s, :], self.wh[:, s, :], ALU.subtract).then_inc(self.w_lo, 1)

    def first_load(self, sp, table):
        for s in range(2):
            self.load(sp, s, table[s:s + 1, :, :])

    def first_high(self, act):
        if self.base:
            begin(act, [self.w_hi], self.base)
        for s in range(2):
            self.high(act, s, 0)

    def first_low(self, pool):
        if self.base:
            begin(pool, [self.w_lo], self.base)
        for s in range(2):
            self.low(pool, s, s)


def load_pair(sp, dst, x, x_in, i):
    sp.dma_start(dst[:, 2 * i:2 * i + 2, :], x[2 * i * P:(2 * i + 2) * P, :].rearrange(
        "(t p) n -> p t n", p=P)).then_inc(x_in[i], 16)


class NormSplit:

    def __init__(self, sems, label, src, scaled, small, psum, banks, ident, gain, xh, xl):
        self.src, self.scaled, self.psum, self.banks = src, scaled, psum, banks
        self.ident, self.gain, self.xh, self.xl = ident, gain, xh, xl
        self.ss, self.ms, self.rms, self.rstd = (small[:, TB * i:TB * (i + 1)] for i in range(4))
        (self.sq_done, self.ms_done, self.rms_done, self.rstd_done, self.scaled_done, self.tp_done, self.hi_ok,
         self.lo_ok) = (sems(f"{label}_{n}") for n in ("sq", "ms", "rms", "rstd", "scaled", "tp", "hi", "lo"))

    def out(self, t, u):
        return slice(4 * u, 4 * u + 4), slice(t * P, (t + 1) * P)

    def bank(self, t, u):
        return self.psum[:, self.banks[(2 * t + u) % 4], :]

    def square(self, act, t):
        if t >= 3:
            act.wait_ge(self.tp_done, 2 * (t - 2))
        act.activation(self.scaled[:, t % 3, :], self.src[:, t, :], ACT.Square,
                       accum_out=self.ss[:, t:t + 1]).then_inc(self.sq_done, 1)

    def root(self, act, t):
        act.wait_ge(self.ms_done, t + 1)
        act.activation(self.rms[:, t:t + 1], self.ms[:, t:t + 1], ACT.Sqrt).then_inc(self.rms_done, 1)

    def high(self, act, t):
        for u in range(2):
            k, cols = self.out(t, u)
            act.wait_ge(self.tp_done, 2 * t + u + 1)
            act.activation(self.xh[:, k, cols], self.bank(t, u).rearrange("p (k n) -> p k n", k=4),
                           ACT.Copy).then_inc(self.hi_ok, 1)

    def mean(self, dve, t):
        dve.wait_ge(self.sq_done, t + 1)
        dve.tensor_scalar(self.ms[:, t:t + 1], self.ss[:, t:t + 1], 1.0 / (D * XS * XS), EPS / (XS * XS),
                          ALU.mult, ALU.add).then_inc(self.ms_done, 1)

    def scale(self, dve, t):
        dve.wait_ge(self.rms_done, t + 1)
        dve.reciprocal(self.rstd[:, t:t + 1], self.rms[:, t:t + 1]).then_inc(self.rstd_done, 1)
        dve.wait_ge(self.rstd_done, t + 1)
        dve.scalar_tensor_tensor(out=self.scaled[:, t % 3, :], in0=self.src[:, t, :], scalar=self.rstd[:, t:t + 1],
                                 in1=self.gain, op0=ALU.mult, op1=ALU.mult).then_inc(self.scaled_done, 1)

    def low(self, dve, t):
        for u in range(2):
            k, cols = self.out(t, u)
            dve.wait_ge(self.hi_ok, 2 * t + u + 1)
            dve.tensor_tensor(self.xl[:, k, cols], self.bank(t, u).rearrange("p (k n) -> p k n", k=4),
                              self.xh[:, k, cols], ALU.subtract).then_inc(self.lo_ok, 1)

    def transpose(self, pe, t):
        pe.wait_ge(self.scaled_done, t + 1)
        for u in range(2):
            if t >= 2:
                pe.wait_ge(self.lo_ok, 2 * (t - 2) + u + 1)
            for j in range(4):
                last = pe.transpose(self.bank(t, u)[:, j * P:(j + 1) * P],
                                    self.scaled[:, t % 3, (4 * u + j) * P:(4 * u + j + 1) * P], self.ident)
            last.then_inc(self.tp_done, 1)


def halves(region):
    return tuple(region[:, 4 * i:4 * i + 4, :].bitcast(F16).rearrange("p a (b n) -> p (a b) n", b=2)
                 for i in range(2))


def norm_input(nc, ctx, sb, sems, psum, x, x_in, mix_g, small, ident, xh, xl, ring, w_stream):
    xin = sb(ctx, "xin", [P, TB, D], F32)
    scaled = sb(ctx, "scaled1", [P, 3, D], F32)
    gain = sb(ctx, "mix_gain", [P, D], F32)
    gain_in = sems("n1_gain")
    n = NormSplit(sems, "n1", xin, scaled, small, psum, (0, 1, 2, 3), ident, gain[:, :], xh, xl)
    with nc.Block() as blk:
        @blk.sync
        def _(sp):
            for i in range(TB // 2):
                load_pair(sp, xin, x, x_in, i)
                if i == 0:
                    sp.dma_start(gain[:, :], mix_g).then_inc(gain_in, 16)
            ring.first_load(sp, w_stream)

        @blk.scalar
        def _(act):
            for i in range(TB + 2):
                if i < TB:
                    act.wait_ge(x_in[i // 2], 16)
                    n.square(act, i)
                if 1 <= i <= TB:
                    n.root(act, i - 1)
                if i >= 2:
                    n.high(act, i - 2)
                if i == TB:
                    ring.first_high(act)

        @blk.vector
        def _(dve):
            for i in range(TB + 2):
                if i < TB:
                    n.mean(dve, i)
                if i == 1:
                    dve.wait_ge(gain_in, 16)
                if 1 <= i <= TB:
                    n.scale(dve, i - 1)
                if i >= 2:
                    n.low(dve, i - 2)

        @blk.gpsimd
        def _(pool):
            ring.first_low(pool)

        @blk.tensor
        def _(pe):
            for t in range(TB):
                n.transpose(pe, t)


def hybrid_block(nc, x, const_f, const_b, const_m, const_e, params, mix_g, ffn_g, w_stream, w_v, w_out, w_q,
                 keys, u_t, u_rows, v_t, final_g, out, gates, acts, normed):
    top = ExitStack()
    with top:
        def sb(ctx, name, shape, dt):
            return ctx.enter_context(nc.sbuf_tensor(name, shape, dt))

        def sems(name):
            return top.enter_context(nc.semaphore(name))

        psum = top.enter_context(nc.psum_tensor("psum", [P, 8, HALF], F32))
        cf = sb(top, "cf", [P, 3 * P + TOPK], F32)
        ident, group_mean, stat = cf[:, 0:P], cf[:, P:2 * P], cf[:, 2 * P:3 * P]
        iota16 = cf[:, 3 * P:3 * P + TOPK]
        par = sb(top, "par", [P, NPAR], F32)
        small = sb(top, "small", [P, 4 * TB], F32)
        lbs = sb(top, "lbs", [P, 8 * CG], F32)
        buffers = (sb(top, "w_ring", [P, 2, D], F32), sb(top, "w_high", [P, 2, D], F16),
                   sb(top, "w_low", [P, 2, D], F16))
        ring_in, ring_q, ring_u = (Ring(sems, label, buffers, base) for label, base in (
            ("w", BASE), ("wq", FOUR), ("u", 0)))
        region_y = sb(top, "region_y", [P, 8, T], F32)
        region_x = sb(top, "region_x", [P, 8, T], F32)

        def param(name):
            return par[:, PAR[name][0]:PAR[name][1]]

        const_in = sems("const_in")
        with nc.Block() as blk:
            @blk.sync
            def _(sp):
                sp.dma_start(cf[:, :], const_f).then_inc(const_in, 16)
                sp.dma_start(par[:, :], params).then_inc(const_in, 16)
                sp.wait_ge(const_in, 32)

        x_in = [sems(f"x_in{i}") for i in range(TB // 2)]

        with ExitStack() as ctx:
            norm_input(nc, ctx, sb, sems, psum, x, x_in, mix_g, small, ident, *halves(region_x), ring_in, w_stream)

        with ExitStack() as outer:
            region_k = sb(outer, "region_k", [P, 8, T], F32)
            region_w = sb(outer, "region_w", [P, 8, T], F32)
            with ExitStack() as ctx:
                mixer(nc, ctx, sb, sems, psum, region_x, region_y, region_k, region_w, ident, group_mean, stat,
                      const_b, const_m, const_e, param, lbs, ring_in, w_stream, w_v, w_out)

            with ExitStack() as ctx:
                project_out(nc, ctx, sb, sems, psum, halves(region_k), halves(region_w), region_x, x, x_in, ffn_g,
                            small, ident, *halves(region_y), normed, ring_q, w_q)

        h_acc = region_x
        xh, xl = halves(region_y)
        rows = sb(top, "rows", [P, GATHERED, 2 * SEL], I32)
        row_gate = sb(top, "row_gate", [P, GATHERED, SEL], F32)
        dot = sb(top, "dot", [P, GATHERED, SEL], F32)
        with ExitStack() as ctx:
            scores = sb(ctx, "scores", [P, TB, HP, NK], F32)
            with ExitStack() as inner:
                queries(nc, inner, sb, sems, psum, xh, xl, ring_q, w_q, ring_u, u_t, keys, scores)
            select_and_activate(nc, ctx, sb, sems, psum, scores, ident, iota16, const_b, xh, xl, ring_u, u_t,
                                gates, acts, rows, row_gate, dot, normed, u_rows)
        with ExitStack() as ctx:
            combine(nc, ctx, sb, sems, psum, h_acc, region_y, buffers, u_rows, v_t, gates, acts, normed, rows,
                    row_gate, dot, small, final_g, out)

def mixer(nc, ctx, sb, sems, psum, region_x, y, region_k, region_w, ident, group_mean, stat, const_b, const_m,
          const_e, param, lbs, ring, w_stream, w_v, w_out):
    xh, xl = halves(region_x)
    wf, wh, wl = ring.wf, ring.wh, ring.wl
    w_in, w_hi, w_lo = ring.w_in, ring.w_hi, ring.w_lo
    logf = region_k[:, 0:CG, :]
    key = region_k[:, CG:2 * CG, :]
    qry = region_w[:, 0:CG, :]
    val = region_w[:, CG:2 * CG, :].rearrange("p a (b n) -> p (a b) n", b=2)
    glu = sb(ctx, "glu", [P, CG, PAD + T], F32)
    gte = sb(ctx, "gte", [P, CG, T], F32)
    restart = sb(ctx, "restart", [P, T], BF16)
    cm = sb(ctx, "cm", [P, (LEVELS + 1) * P], I32)
    wvh, wvl = (y[:, CG + 2 * i:CG + 2 * i + 2, :].bitcast(F16).rearrange("p a (b n) -> p (a b) n", b=4)
                for i in range(2))
    lb, omlb = lbs[:, 0:CG], lbs[:, CG:2 * CG]
    tmp = [lbs[:, (2 + i) * CG:(3 + i) * CG] for i in range(6)]

    masks_in = sems("masks_in")
    restart_in = sems("restart_in")
    proj = [sems(f"proj{b}") for b in range(4)]
    proj_out = [sems(f"proj_out{b}") for b in range(4)]
    val_mm = sems("val_mm")
    val_ok = sems("val_ok")
    pad_ok = sems("pad_ok")
    lb_step = sems("lb_step")
    lb_exp = sems("lb_exp")
    ln_ok = sems("ln_ok")
    key_ok = sems("key_ok")
    conv = sems("conv")
    GATE, A, F, Q, G = (0, 2), (2, 4), (4, 6), (6, 8), (8, 10)
    BEFORE_V, TURNS, V_ITEMS = A[1], G[1], KC // 2
    V_FIRST = 2 * BEFORE_V

    def item(turn, s, before_v):
        return 2 * turn + s + (0 if before_v else V_ITEMS)

    with nc.Block() as blk:
        @blk.sync
        def _(sp):
            def load(turn, s):
                ring.load(sp, s, w_stream[ds(turn * 2 + s, 1), :, :])

            sp.dma_start(cm[:, :], const_m).then_inc(masks_in, 16)
            with sp.Fori(1, BEFORE_V) as turn:
                for s in range(2):
                    sp.wait_ge(w_lo, BASE + item(turn, s, True) - 1)
                    load(turn, s)
            for j in range(V_ITEMS):
                sp.wait_ge(w_lo, BASE + V_FIRST + j - 1)
                sp.dma_start(wf[:, j % 2, :], w_v[j, :, :]).then_inc(w_in[j % 2], 16)
            with sp.Fori(BEFORE_V, TURNS) as turn:
                for s in range(2):
                    sp.wait_ge(w_lo, BASE + item(turn, s, False) - 1)
                    load(turn, s)
            sp.wait_ge(masks_in, 16)

        @blk.tensor
        def _(pe):
            begin(pe, [*proj, val_mm])

            def turns(first, end, before_v):
                with pe.Fori(first, end) as turn:
                    for s in range(2):
                        pe.wait_ge(w_lo, BASE + item(turn, s, before_v) + 1)
                        for h in range(NH):
                            b = 2 * s + h
                            cols = slice(h * HALF, (h + 1) * HALF)
                            pe.wait_ge(proj_out[b], BASE + turn)
                            for k in range(KC):
                                row = slice(k * P, (k + 1) * P)
                                pe.matmul(psum[:, b, :], wh[:, s, row], xh[:, k, cols], start=(k == 0), stop=False)
                                pe.matmul(psum[:, b, :], wh[:, s, row], xl[:, k, cols], start=False, stop=False)
                                last = pe.matmul(psum[:, b, :], wl[:, s, row], xh[:, k, cols], start=False,
                                                 stop=(k == KC - 1))
                            last.then_inc(proj[b], 1)

            turns(0, BEFORE_V, True)
            turns(BEFORE_V, F[1], False)
            pe.wait_ge(w_lo, BASE + V_FIRST + V_ITEMS)
            for t in range(TB):
                a, cols = psum[:, 4 + t % 4, :], slice(t * P, (t + 1) * P)
                if t >= 4:
                    pe.wait_ge(val_ok, BASE + t - 3)
                for k in range(KC):
                    pe.matmul(a, xh[:, k, cols], wvh[:, k, :], start=(k == 0), stop=False)
                    pe.matmul(a, xh[:, k, cols], wvl[:, k, :], start=False, stop=False)
                    last = pe.matmul(a, xl[:, k, cols], wvh[:, k, :], start=False, stop=(k == KC - 1))
                last.then_inc(val_mm, 1)
            turns(F[1], TURNS, False)

        @blk.scalar
        def _(act):
            begin(act, [*proj_out, val_ok, lb_exp, ln_ok])

            def high(turn, s, before_v):
                ring.high(act, s, turn + (0 if before_v else V_ITEMS // 2))

            def slices(turn, first, body, ahead, before_v):
                for s in range(2):
                    for h in range(NH):
                        b = 2 * s + h
                        act.wait_ge(proj[b], BASE + turn + 1)
                        if body is not None:
                            body(psum[:, b, :], turn * 2 + (s - 2 * first), h).then_inc(proj_out[b], 1)
                    if ahead:
                        high(turn + 1, s, before_v)

            def forget(ps, c, h):
                act.activation(logf[:, ds(c, 1), h * HALF:(h + 1) * HALF], ps, ACT.Sigmoid, scale=BACK)
                return act.activation(key[:, ds(c, 1), h * HALF:(h + 1) * HALF], ps, ACT.Sigmoid, scale=-BACK)

            def gate(ps, c, h):
                return act.activation(glu[:, ds(c, 1), PAD + h * HALF:PAD + (h + 1) * HALF], ps, ACT.Sigmoid,
                                      scale=BACK)

            def silu_to(buf):
                return lambda ps, c, h: act.activation(buf[:, ds(c, 1), h * HALF:(h + 1) * HALF], ps, ACT.Silu,
                                                       scale=BACK)

            act.wait_ge(lb_step, BASE + 3)
            act.activation(tmp[2], tmp[1], ACT.Exp)
            act.activation(tmp[3], tmp[4], ACT.Exp).then_inc(lb_exp, 1)
            with act.Fori(*GATE) as turn:
                slices(turn, GATE[0], gate, True, True)
            slices(A[0], A[0], None, True, True)
            for j in range(V_ITEMS):
                act.wait_ge(w_in[j % 2], 16 * (BEFORE_V + j // 2) + 16)
                act.activation(wvh[:, 2 * j:2 * j + 2, :], wf[:, j % 2, :].rearrange("p (a n) -> p a n", a=2),
                               ACT.Copy, scale=WS)
                act.activation(wf[:, j % 2, :], wf[:, j % 2, :], ACT.Copy, scale=WS).then_inc(w_hi, 1)
            slices(A[0] + 1, A[0], None, True, False)
            with act.Fori(*F) as turn:
                slices(turn, F[0], forget, True, False)
            for t in range(TB):
                act.wait_ge(val_mm, BASE + t + 1)
                act.activation(val[:, t, :], psum[:, 4 + t % 4, :], ACT.Copy, scale=BACK).then_inc(val_ok, 1)
            act.wait_ge(lb_step, BASE + 7)
            for b in range(4):
                act.wait_ge(proj_out[b], BASE + F[1])
            for c in range(CG):
                act.activation(logf[:, c, :], logf[:, c, :], ACT.Ln, scale=omlb[:, c:c + 1],
                               bias=lb[:, c:c + 1]).then_inc(ln_ok, 1)
            with act.Fori(*Q) as turn:
                slices(turn, Q[0], silu_to(qry), True, False)
            slices(G[0], G[0], silu_to(gte), True, False)
            slices(G[0] + 1, G[0], silu_to(gte), False, False)

        @blk.gpsimd
        def _(pool):
            begin(pool, [pad_ok, key_ok])

            def low(turn, s, before_v):
                ring.low(pool, s, item(turn, s, before_v))

            pool.memset(glu[:, :, 0:PAD], 0.0).then_inc(pad_ok, 1)
            pool.dma_start(restart[:, :], const_b[:, P * 8:P * 8 + T]).then_inc(restart_in, 16)
            with pool.Fori(1, BEFORE_V) as turn:
                for s in range(2):
                    low(turn, s, True)
            for j in range(V_ITEMS):
                pool.wait_ge(w_hi, BASE + V_FIRST + j + 1)
                pool.tensor_tensor(wvl[:, 2 * j:2 * j + 2, :], wf[:, j % 2, :].rearrange("p (a n) -> p a n", a=2),
                                   wvh[:, 2 * j:2 * j + 2, :], ALU.subtract).then_inc(w_lo, 1)
            with pool.Fori(BEFORE_V, F[1] + 1) as turn:
                for s in range(2):
                    low(turn, s, False)
            pool.wait_ge(lb_step, BASE + 7)
            for b in range(4):
                pool.wait_ge(proj_out[b], BASE + F[1])
            for c in range(CG):
                pool.tensor_scalar(key[:, c, :], key[:, c, :], omlb[:, c:c + 1], 1.0,
                                   ALU.mult, ALU.mult).then_inc(key_ok, 1)
            with pool.Fori(F[1] + 1, TURNS) as turn:
                for s in range(2):
                    low(turn, s, False)

        @blk.vector
        def _(dve):
            begin(dve, [lb_step, conv])
            l0, l1 = param("lb0"), param("lb1")
            dve.tensor_tensor(tmp[0], l0, l1, ALU.max).then_inc(lb_step, 1)
            dve.wait_ge(lb_step, BASE + 1)
            dve.tensor_tensor(tmp[1], l0, tmp[0], ALU.subtract).then_inc(lb_step, 1)
            dve.tensor_tensor(tmp[4], l1, tmp[0], ALU.subtract).then_inc(lb_step, 1)
            dve.wait_ge(lb_exp, BASE + 1)
            dve.tensor_tensor(tmp[5], tmp[2], tmp[3], ALU.add).then_inc(lb_step, 1)
            dve.wait_ge(lb_step, BASE + 4)
            dve.reciprocal(tmp[0], tmp[5]).then_inc(lb_step, 1)
            dve.wait_ge(lb_step, BASE + 5)
            dve.tensor_tensor(lb, tmp[2], tmp[0], ALU.mult).then_inc(lb_step, 1)
            dve.tensor_tensor(omlb, tmp[3], tmp[0], ALU.mult).then_inc(lb_step, 1)
            for b in range(4):
                dve.wait_ge(proj_out[b], BASE + GATE[1])
            with dve.Fori(*A) as turn:
                for s in range(2):
                    for h in range(NH):
                        b = 2 * s + h
                        dve.wait_ge(proj[b], BASE + turn + 1)
                        at = glu[:, ds(turn * 2 + (s - 2 * A[0]), 1),
                                 PAD + h * HALF:PAD + (h + 1) * HALF].rearrange("p a n -> p (a n)")
                        dve.scalar_tensor_tensor(out=at, in0=psum[:, b, :], scalar=BACK, in1=at, op0=ALU.mult,
                                                 op1=ALU.mult).then_inc(proj_out[b], 1)
            dve.wait_ge(pad_ok, BASE + 1)
            for b in range(4):
                dve.wait_ge(proj_out[b], BASE + A[1])
            cw, cbias = param("conv_w"), param("conv_b")
            for c in range(CG):
                dve.tensor_scalar(y[:, c, :], glu[:, c, 0:T], cw[:, c * TAPS:c * TAPS + 1], cbias[:, c:c + 1],
                                  ALU.mult, ALU.add).then_inc(conv, 1)
            with dve.Fori(1, TAPS) as tap:
                for c in range(CG):
                    dve.wait_ge(conv, BASE + CG * tap + (c + 1 - CG))
                    dve.scalar_tensor_tensor(out=y[:, c, :], in0=glu[:, c, ds(tap, T)],
                                             scalar=cw[:, ds(tap + c * TAPS, 1)], in1=y[:, c, :],
                                             op0=ALU.mult, op1=ALU.add).then_inc(conv, 1)
            dve.wait_ge(restart_in, 16)
            for c in range(CG):
                dve.wait_ge(ln_ok, BASE + c + 1)
                dve.tensor_tensor_scan(logf[:, c, :], restart[:, :], logf[:, c, :], 0.0, ALU.mult, ALU.add)

    used = [0]

    def carve(n):
        flat = region_x[:, :, :].rearrange("p a n -> p (a n)")
        used[0] += n
        return flat[:, used[0] - n:used[0]]

    lev = [carve(CG * P).rearrange("p (h t) -> p h t", h=CG) for _ in range(LEVELS)]
    k_end = carve(CG * P).rearrange("p (h t) -> p h t", h=CG)
    q_beg = carve(CG * P).rearrange("p (h t) -> p h t", h=CG)
    k_blk = carve(CG * P).rearrange("p (h t) -> p h t", h=CG)
    v_blk = carve(CG * P).rearrange("p (h t) -> p h t", h=CG)
    att = carve(CG * P).rearrange("p (h t) -> p h t", h=CG)
    k_end_t = carve(CG * P).rearrange("p (h t) -> p h t", h=CG)
    state = [carve(CG * P).rearrange("p (h t) -> p h t", h=CG) for _ in range(2)]
    decay = carve(3 * CG).rearrange("p (h c) -> p h c", h=CG)

    LV = LEVELS
    SCORE = (0, 1, 6, 7)
    init = sems("hg_init")
    x_sub, x_exp, k_mul, q_mul = sems("x_sub"), sems("x_exp"), sems("k_mul"), sems("q_mul")
    sc_mm, sc_ok = sems("sc_mm"), sems("sc_ok")
    kt_mm, kt_ok = sems("kt_mm"), sems("kt_ok")
    u_mm, s_ok, o_mm, o_ok = sems("u_mm"), sems("s_ok"), sems("o_mm"), sems("o_ok")

    def bank(i):
        return psum[:, i, :].rearrange("p (h t) -> p h t", h=CG)

    def seg(ap, n):
        return ap.rearrange("p h (s i) -> p h s i", i=n)

    with nc.Block() as blk:
        @blk.vector
        def _(dve):
            begin(dve, [init, x_sub, q_mul, sc_ok, s_ok])

            def exponents(n):
                b_blk = logf[:, :, ds(n * P, P)]
                dve.wait_ge(sc_mm, BASE + n * (LV + 1))
                for l in range(LV):
                    hs = CHUNK >> (l + 1)
                    bs = seg(b_blk, 2 * hs)
                    ref = bs[:, :, :, hs - 1:hs].to_broadcast([P, CG, P // (2 * hs), 2 * hs])
                    dve.tensor_tensor(seg(lev[l], 2 * hs), bs, ref, ALU.subtract).then_inc(x_sub, 1)
                dve.wait_ge(kt_mm, BASE + n)
                bs = seg(b_blk, CHUNK)
                dve.tensor_tensor(seg(k_end, CHUNK), bs,
                                  bs[:, :, :, CHUNK - 1:CHUNK].to_broadcast([P, CG, P // CHUNK, CHUNK]),
                                  ALU.subtract).then_inc(x_sub, 1)

            def intra(n):
                q_blk = qry[:, :, ds(n * P, P)]
                for l in range(LV):
                    hs = CHUNK >> (l + 1)
                    dve.wait_ge(x_exp, BASE + n * (LV + 3) + (l + 1))
                    a = seg(lev[l], 2 * hs)[:, :, :, hs:2 * hs]
                    dve.tensor_tensor(a, a, seg(q_blk, 2 * hs)[:, :, :, hs:2 * hs], ALU.mult).then_inc(q_mul, 1)
                dve.wait_ge(x_exp, BASE + n * (LV + 3) + (LV + 2))
                dve.tensor_tensor(q_beg, q_beg, q_blk, ALU.mult).then_inc(q_mul, 1)
                dve.wait_ge(o_mm, BASE + 2 * n)
                for l in range(LV + 1):
                    dve.wait_ge(sc_mm, BASE + n * (LV + 1) + (l + 1))
                    dve.wait_ge(sc_ok, BASE + n * (LV + 1) + l)
                    dve.memset(decay[:, 0:1, 2:3], 0.0)
                    mask = cm[:, l * P:(l + 1) * P].rearrange("p (a t) -> p a t", a=1).to_broadcast([P, CG, P])
                    dve.copy_predicated(att, mask, bank(SCORE[l % 4])).then_inc(sc_ok, 1)

            def states(n):
                for c in range(2):
                    dve.wait_ge(u_mm, BASE + 2 * n + (c + 1))
                    dve.wait_ge(s_ok, BASE + 2 * n + c)
                    if c == 0:
                        dve.wait_ge(x_exp, BASE + n * (LV + 3) + (LV + 3))
                    else:
                        dve.wait_ge(o_mm, BASE + 2 * n + 1)
                    for hh in range(CG):
                        last = dve.scalar_tensor_tensor(out=state[1 - c][:, hh, :], in0=state[c][:, hh, :],
                                                        scalar=decay[:, hh, c:c + 1], in1=bank(3 + c)[:, hh, :],
                                                        op0=ALU.mult, op1=ALU.add)
                    last.then_inc(s_ok, 1)

            dve.memset(att, 0.0)
            dve.memset(state[0], 0.0).then_inc(init, 1)
            exponents(0)
            dve.wait_ge(init, BASE + 1)
            with dve.Fori(0, TB - 1) as n:
                intra(n)
                exponents(n + 1)
                states(n)
            intra(TB - 1)
            states(TB - 1)

        @blk.scalar
        def _(act):
            begin(act, [x_exp, kt_ok, o_ok])

            def outputs(n):
                act.wait_ge(o_mm, BASE + 2 * n + 2)
                act.activation(y[:, 4:8, ds(n * P, P)], bank(5), ACT.Copy).then_inc(o_ok, 1)

            def decays(n, first):
                b_blk = logf[:, :, ds(n * P, P)]
                for l in range(LV):
                    hs = CHUNK >> (l + 1)
                    act.wait_ge(x_sub, BASE + n * (LV + 1) + (l + 1))
                    a = seg(lev[l], 2 * hs)
                    act.activation(a[:, :, :, 0:hs], a[:, :, :, 0:hs], ACT.Exp, scale=-1.0)
                    act.activation(a[:, :, :, hs:2 * hs], a[:, :, :, hs:2 * hs], ACT.Exp).then_inc(x_exp, 1)
                act.wait_ge(x_sub, BASE + n * (LV + 1) + (LV + 1))
                act.activation(k_end, k_end, ACT.Exp, scale=-1.0).then_inc(x_exp, 1)
                if not first:
                    outputs(n - 1)
                act.wait_ge(o_mm, BASE + 2 * n)
                act.activation(q_beg, b_blk, ACT.Exp).then_inc(x_exp, 1)
                act.wait_ge(s_ok, BASE + 2 * n)
                act.activation(decay[:, :, 0:2], seg(b_blk, CHUNK)[:, :, :, CHUNK - 1], ACT.Exp).then_inc(x_exp, 1)
                act.wait_ge(kt_mm, BASE + n + 1)
                act.wait_ge(u_mm, BASE + 2 * n)
                act.activation(k_end_t, bank(2), ACT.Copy).then_inc(kt_ok, 1)

            decays(0, True)
            with act.Fori(1, TB) as n:
                decays(n, False)
            outputs(TB - 1)

        @blk.gpsimd
        def _(pool):
            begin(pool, [k_mul])
            with pool.Fori(0, TB) as n:
                kb = key[:, :, ds(n * P, P)]
                pool.wait_ge(k_mul, BASE + n * (LV + 2))
                pool.wait_ge(sc_mm, BASE + n * (LV + 1))
                pool.tensor_copy(k_blk, kb).then_inc(k_mul, 1)
                pool.wait_ge(k_mul, BASE + n * (LV + 2) + 1)
                for l in range(LV):
                    hs = CHUNK >> (l + 1)
                    pool.wait_ge(x_exp, BASE + n * (LV + 3) + (l + 1))
                    a = seg(lev[l], 2 * hs)[:, :, :, 0:hs]
                    pool.tensor_tensor(a, a, seg(k_blk, 2 * hs)[:, :, :, 0:hs], ALU.mult).then_inc(k_mul, 1)
                pool.wait_ge(o_mm, BASE + 2 * n)
                pool.tensor_copy(v_blk, val[:, ds(n, 1), :].rearrange("p a (h t) -> p (a h) t", h=CG))
                pool.wait_ge(x_exp, BASE + n * (LV + 3) + (LV + 1))
                pool.tensor_tensor(k_end, k_end, k_blk, ALU.mult).then_inc(k_mul, 1)
            for c in range(CG):
                pool.tensor_scalar(gte[:, c, :], gte[:, c, :], param("hgrn_g")[:, c:c + 1], XS, ALU.mult, ALU.mult)

        @blk.tensor
        def _(pe):
            begin(pe, [sc_mm, kt_mm, u_mm, o_mm])
            pe.wait_ge(init, BASE + 1)
            with pe.Fori(0, TB) as n:
                q_blk = qry[:, :, ds(n * P, P)]
                for l in range(LV + 1):
                    if l < LV:
                        pe.wait_ge(q_mul, BASE + n * (LV + 1) + (l + 1))
                        pe.wait_ge(k_mul, BASE + n * (LV + 2) + (l + 2))
                    pe.wait_ge(sc_ok, BASE + n * (LV + 1) + max(l - 3, 0))
                    for hh in range(CG):
                        if l < LV:
                            last = pe.matmul(bank(SCORE[l % 4])[:, hh, :], lev[l][:, hh, :], lev[l][:, hh, :],
                                             start=True, stop=True)
                        else:
                            last = pe.matmul(bank(SCORE[l % 4])[:, hh, :], k_blk[:, hh, :], q_blk[:, hh, :],
                                             start=True, stop=True)
                    last.then_inc(sc_mm, 1)
                pe.wait_ge(k_mul, BASE + n * (LV + 2) + (LV + 2))
                pe.wait_ge(kt_ok, BASE + n)
                for hh in range(CG):
                    last = pe.transpose(bank(2)[:, hh, :], k_end[:, hh, :], ident)
                last.then_inc(kt_mm, 1)
                pe.wait_ge(kt_ok, BASE + n + 1)
                pe.wait_ge(s_ok, BASE + 2 * n)
                for c in range(2):
                    r = slice(c * CHUNK, (c + 1) * CHUNK)
                    for hh in range(CG):
                        last = pe.matmul(bank(3 + c)[:, hh, :], k_end_t[r, hh, :], v_blk[r, hh, :],
                                         start=True, stop=True)
                    last.then_inc(u_mm, 1)
                pe.wait_ge(sc_ok, BASE + n * (LV + 1) + (LV + 1))
                pe.wait_ge(o_ok, BASE + n)
                for hh in range(CG):
                    pe.matmul(bank(5)[:, hh, :], v_blk[:, hh, :], att[:, hh, :], start=(hh == 0), stop=False,
                              skip_group_check=True)
                pe.wait_ge(q_mul, BASE + n * (LV + 1) + (LV + 1))
                for c in range(2):
                    pe.wait_ge(s_ok, BASE + 2 * n + c)
                    for hh in range(CG):
                        last = pe.matmul(bank(5)[:, hh, c * CHUNK:(c + 1) * CHUNK], state[c][:, hh, :],
                                         q_beg[:, hh, c * CHUNK:(c + 1) * CHUNK], start=False,
                                         stop=(c == 1), skip_group_check=True)
                    last.then_inc(o_mm, 1)

    yh, yl = halves(region_k)
    oh, ol = halves(region_w)
    sq = region_x
    spread = glu[0:NSTAT, 0, 0:2 * CG * P].rearrange("p (c n) -> p c n", n=P)
    rstd = glu[0:NSTAT, 1, 0:T]
    wo_in = [sems(f"wo_in{s}") for s in range(2)]
    (mean_mm, mean_ok, sq_ok, stat_mm, root_ok, rstd_ok, spread_mm, scaled_ok, gated_ok, silu_ok, hi_ok, e_in,
     wo_hi, wo_lo) = (sems(f"cn_{n}") for n in (
         "mean_mm", "mean_ok", "sq", "stat_mm", "root", "rstd", "spread_mm", "scaled", "gated", "silu", "hi",
         "e_in", "wo_hi", "wo_lo"))
    ORDER = [*range(CG, 2 * CG), *range(CG)]
    UNITS = [(c, h) for h in range(NH) for c in ORDER]

    def at(buf, unit):
        c, h = unit
        return buf[:, c, h * HALF:(h + 1) * HALF]

    def place(i):
        return sum(c >= CG for c, _ in UNITS[:i]), sum(c < CG for c, _ in UNITS[:i])

    with nc.Block() as blk:
        @blk.sync
        def _(sp):
            sp.dma_start(glu[0:NSTAT, 0, 0:2 * CG * P], const_e).then_inc(e_in, 16)
            for j in range(KC):
                if j >= 2:
                    sp.wait_ge(wo_lo, j - 1)
                sp.dma_start(wf[:, j % 2, :], w_out[j * P:(j + 1) * P, :]).then_inc(wo_in[j % 2], 16)

        @blk.tensor
        def _(pe):
            for i in range(2 * CG):
                if i >= 4:
                    pe.wait_ge(mean_ok, i - 3)
                pe.matmul(psum[:, i % 4, :], group_mean, at(y, (i // 2, i % 2)), start=True,
                          stop=True).then_inc(mean_mm, 1)
            for i, c in enumerate(ORDER):
                pe.wait_ge(sq_ok, i + 1)
                for h in range(NH):
                    last = pe.matmul(psum[0:NSTAT, 4 + h, :], stat[:, c * NSTAT:(c + 1) * NSTAT], at(sq, (c, h)),
                                     start=(i == 0), stop=(i == 2 * CG - 1))
                    if i == 2 * CG - 1:
                        last.then_inc(stat_mm, 1)
            pe.wait_ge(e_in, 16)
            for i, (c, h) in enumerate(UNITS):
                pe.wait_ge(rstd_ok, h + 1)
                if i >= 4:
                    pe.wait_ge(scaled_ok, i - 3)
                pe.matmul(psum[:, i % 4, :], spread[:, c, :], rstd[:, h * HALF:(h + 1) * HALF], start=True,
                          stop=True).then_inc(spread_mm, 1)

        @blk.scalar
        def _(act):
            def w_high(j):
                act.wait_ge(wo_in[j % 2], 16 * (j // 2) + 16)
                act.activation(oh[:, j, :], wf[:, j % 2, :], ACT.Copy, scale=WS)
                act.activation(wf[:, j % 2, :], wf[:, j % 2, :], ACT.Copy, scale=WS).then_inc(wo_hi, 1)

            def high(i):
                c, h = UNITS[i]
                hgrn, conv_units = place(i)
                if c >= CG:
                    act.wait_ge(gated_ok, hgrn + 1)
                else:
                    act.wait_ge(silu_ok, conv_units + 1)
                act.activation(at(yh, (c, h)), at(y, (c, h)), ACT.Copy,
                               scale=1.0 if c >= CG else XS).then_inc(hi_ok, 1)

            for i, c in enumerate(ORDER):
                if c < CG:
                    act.wait_ge(mean_ok, 2 * c + 2)
                act.activation(sq[:, c, :], y[:, c, :], ACT.Square).then_inc(sq_ok, 1)
                if i >= 3:
                    w_high(i - 3)
            for h in range(NH):
                act.wait_ge(stat_mm, h + 1)
                act.activation(rstd[:, h * HALF:(h + 1) * HALF], psum[0:NSTAT, 4 + h, :], ACT.Sqrt,
                               bias=EPS).then_inc(root_ok, 1)
            for j in range(5, KC):
                w_high(j)
            g, b = param("conv_g"), param("conv_nb")
            for i, (c, h) in enumerate(UNITS):
                if c < CG:
                    act.wait_ge(scaled_ok, i + 1)
                    act.activation(at(y, (c, h)), at(y, (c, h)), ACT.Silu, scale=g[:, c:c + 1],
                                   bias=b[:, c:c + 1]).then_inc(silu_ok, 1)
                if i >= 1:
                    high(i - 1)
            high(len(UNITS) - 1)

        @blk.vector
        def _(dve):
            for i in range(2 * CG):
                dve.wait_ge(mean_mm, i + 1)
                a = at(y, (i // 2, i % 2))
                dve.tensor_tensor(a, a, psum[:, i % 4, :], ALU.subtract).then_inc(mean_ok, 1)
            for h in range(NH):
                dve.wait_ge(root_ok, h + 1)
                a = rstd[:, h * HALF:(h + 1) * HALF]
                dve.reciprocal(a, a).then_inc(rstd_ok, 1)

            def gate(i):
                c, h = UNITS[i]
                if c >= CG:
                    dve.wait_ge(scaled_ok, i + 1)
                    dve.tensor_tensor(at(y, (c, h)), at(y, (c, h)), at(gte, (c - CG, h)),
                                      ALU.mult).then_inc(gated_ok, 1)

            def low(i):
                if UNITS[i][0] < CG:
                    dve.wait_ge(hi_ok, i + 1)
                    dve.scalar_tensor_tensor(out=at(yl, UNITS[i]), in0=at(y, UNITS[i]), scalar=XS,
                                             in1=at(yh, UNITS[i]), op0=ALU.mult, op1=ALU.subtract)

            for i, unit in enumerate(UNITS):
                dve.wait_ge(spread_mm, i + 1)
                dve.tensor_tensor(at(y, unit), at(y, unit), psum[:, i % 4, :], ALU.mult).then_inc(scaled_ok, 1)
                if i >= 1:
                    gate(i - 1)
                if i >= 3:
                    low(i - 3)
            for i in range(len(UNITS) - 3, len(UNITS)):
                low(i)

        @blk.gpsimd
        def _(pool):
            for j in range(KC):
                pool.wait_ge(wo_hi, j + 1)
                pool.tensor_tensor(ol[:, j, :], wf[:, j % 2, :], oh[:, j, :], ALU.subtract).then_inc(wo_lo, 1)
            for i, unit in enumerate(UNITS):
                if unit[0] >= CG:
                    pool.wait_ge(hi_ok, i + 1)
                    pool.tensor_tensor(at(yl, unit), at(y, unit), at(yh, unit), ALU.subtract)


def project_out(nc, ctx, sb, sems, psum, y_parts, w_parts, h_acc, x, x_in, ffn_g, small, ident, xh, xl, normed,
                ring, w_q):
    yh, yl = y_parts
    oh, ol = w_parts
    scaled = sb(ctx, "scaled2", [P, 3, D], F32)
    gain = sb(ctx, "ffn_gain", [P, D], F32)
    gain_in, o_mm, h_ok, normed_out = sems("n2_gain"), sems("wo_mm"), sems("h_ok"), sems("normed_out")
    n = NormSplit(sems, "n2", h_acc, scaled, small, psum, (0, 1, 2, 3), ident, gain[:, :], xh, xl)
    with nc.Block() as blk:
        @blk.sync
        def _(sp):
            for i in range(TB // 2):
                load_pair(sp, h_acc, x, x_in, i)
                if i == 0:
                    sp.dma_start(gain[:, :], ffn_g).then_inc(gain_in, 16)
            ring.first_load(sp, w_q)
            for t in range(GATHERED):
                sp.wait_ge(n.scaled_done, t + 1)
                sp.dma_start(normed[t, :, :], scaled[:, t, :]).then_inc(normed_out, 16)
            sp.wait_ge(normed_out, 16 * GATHERED)

        @blk.tensor
        def _(pe):
            for t in range(TB):
                rows = slice(t * P, (t + 1) * P)
                for h in range(2):
                    i = 2 * t + h
                    cols = slice(h * HALF, (h + 1) * HALF)
                    a = psum[:, 4 + i % 4, :]
                    if i >= 4:
                        pe.wait_ge(h_ok, i - 3)
                    for k in range(KC):
                        pe.matmul(a, yh[:, k, rows], oh[:, k, cols], start=(k == 0), stop=False)
                        pe.matmul(a, yh[:, k, rows], ol[:, k, cols], start=False, stop=False)
                        last = pe.matmul(a, yl[:, k, rows], oh[:, k, cols], start=False, stop=(k == KC - 1))
                    last.then_inc(o_mm, 1)
                if t >= 1:
                    n.transpose(pe, t - 1)
            n.transpose(pe, TB - 1)

        @blk.gpsimd
        def _(pool):
            ring.first_low(pool)

        @blk.scalar
        def _(act):
            ring.first_high(act)
            for t in range(TB):
                act.wait_ge(h_ok, 2 * t + 2)
                if t == 3:
                    act.wait_ge(normed_out, 16 * GATHERED)
                n.square(act, t)
                n.root(act, t)
                if t >= 1:
                    n.high(act, t - 1)
            n.high(act, TB - 1)

        @blk.vector
        def _(dve):
            for t in range(TB):
                dve.wait_ge(x_in[t // 2], 32)
                for h in range(2):
                    i = 2 * t + h
                    dve.wait_ge(o_mm, i + 1)
                    a = h_acc[:, t, h * HALF:(h + 1) * HALF]
                    dve.scalar_tensor_tensor(out=a, in0=psum[:, 4 + i % 4, :], scalar=BACK, in1=a, op0=ALU.mult,
                                             op1=ALU.add).then_inc(h_ok, 1)
                n.mean(dve, t)
                if t == 0:
                    dve.wait_ge(gain_in, 16)
                n.scale(dve, t)
                if t >= 1:
                    n.low(dve, t - 1)
            n.low(dve, TB - 1)


def queries(nc, ctx, sb, sems, psum, xh, xl, ring, w_q, next_ring, u_t, keys, scores):
    wh, wl, w_lo = ring.wh, ring.wl, ring.w_lo
    qt = sb(ctx, "qt", [P, 2, T], F32)
    kt = sb(ctx, "kt", [P, HP, NK], F32)
    k_in = sems("keys_in")
    q_mm, q_ok, s_mm, s_ok = (sems(f"qu_{n}") for n in ("q_mm", "q_ok", "s_mm", "s_ok"))
    PAIRS = HP // 2
    with nc.Block() as blk:
        @blk.sync
        def _(sp):
            sp.dma_start(kt[:, :, :], keys).then_inc(k_in, 16)
            with sp.Fori(1, PAIRS) as pair:
                for s in range(2):
                    sp.wait_ge(w_lo, FOUR + 2 * pair + s - 1)
                    ring.load(sp, s, w_q[ds(pair * 2 + s, 1), :, :])
            sp.wait_ge(w_lo, FOUR + HP)
            next_ring.first_load(sp, u_t)

        @blk.tensor
        def _(pe):
            begin(pe, [q_mm, s_mm], FOUR)
            pe.wait_ge(k_in, 16)
            with pe.Fori(0, PAIRS) as pair:
                for s in range(2):
                    pe.wait_ge(w_lo, FOUR + 2 * pair + s + 1)
                    for h in range(NH):
                        b = 2 * s + h
                        cols = slice(h * HALF, (h + 1) * HALF)
                        pe.wait_ge(q_ok, FOUR + 4 * pair + (b - 3))
                        for k in range(KC):
                            row = slice(k * P, (k + 1) * P)
                            pe.matmul(psum[:, b, :], wh[:, s, row], xh[:, k, cols], start=(k == 0), stop=False)
                            pe.matmul(psum[:, b, :], wh[:, s, row], xl[:, k, cols], start=False, stop=False)
                            last = pe.matmul(psum[:, b, :], wl[:, s, row], xh[:, k, cols], start=False,
                                             stop=(k == KC - 1))
                        last.then_inc(q_mm, 1)
                for s in range(2):
                    for h in range(NH):
                        b = 2 * s + h
                        pe.wait_ge(q_ok, FOUR + 4 * pair + (b + 1))
                        pe.wait_ge(s_ok, FOUR + 4 * pair + (b - 3))
                        for j in range(4):
                            last = pe.matmul(psum[:, 4 + b, j * P:(j + 1) * P],
                                             qt[:, s, h * HALF + j * P:h * HALF + (j + 1) * P],
                                             kt[:, ds(2 * pair + s, 1), :].rearrange("p a n -> p (a n)"),
                                             start=True, stop=True)
                        last.then_inc(s_mm, 1)

        @blk.scalar
        def _(act):
            begin(act, [q_ok], FOUR)

            def body(pair, next_high):
                for s in range(2):
                    for h in range(NH):
                        b = 2 * s + h
                        act.wait_ge(q_mm, FOUR + 4 * pair + (b + 1))
                        act.wait_ge(s_mm, FOUR + 4 * pair + (b - 3))
                        act.activation(qt[:, s, h * HALF:(h + 1) * HALF], psum[:, b, :], ACT.Copy,
                                       scale=BACK).then_inc(q_ok, 1)
                    next_high(act, s, pair + 1)

            with act.Fori(0, PAIRS - 1) as pair:
                body(pair, ring.high)
            body(PAIRS - 1, lambda act, s, _: next_ring.high(act, s, 0))

        @blk.gpsimd
        def _(pool):
            with pool.Fori(1, PAIRS) as pair:
                for s in range(2):
                    ring.low(pool, s, 2 * pair + s)
            next_ring.first_low(pool)

        @blk.vector
        def _(dve):
            begin(dve, [s_ok], FOUR)
            with dve.Fori(0, PAIRS) as pair:
                for s in range(2):
                    for h in range(NH):
                        b = 2 * s + h
                        dve.wait_ge(s_mm, FOUR + 4 * pair + (b + 1))
                        dve.tensor_copy(scores[:, 4 * h:4 * h + 4, ds(2 * pair + s, 1), :].rearrange(
                            "p t a n -> p t (a n)"),
                            psum[:, 4 + b, :].rearrange("p (t n) -> p t n", t=4)).then_inc(s_ok, 1)


def after(eng, sem, count):
    if not (isinstance(count, int) and count <= 0):
        eng.wait_ge(sem, count)


def select_and_activate(nc, ctx, sb, sems, psum, scores, ident, iota16, const_b, xh, xl, ring, u_t, gates, acts, rows,
                        row_gate, dot, normed, u_rows):
    PICK = 8
    PICKED = PICK * TB
    OCT = 8
    SPREAD = TD // OCT // 2
    ALONE = NK - PICKED - SPREAD
    LOOP = 4
    assert ALONE > 0 and ALONE % 2 == 0 and SPREAD % LOOP == 0

    uh, ul, u_hi, u_lo = ring.wh, ring.wl, ring.w_hi, ring.w_lo
    ge = sb(ctx, "ge", [P, 2, TD], F32)

    sc = sb(ctx, "tk_sc", [P, HP, NK], F32)
    work = sb(ctx, "tk_work", [P, 2 * SEL * TOPK], F32)
    best = sb(ctx, "tk_best", [P, HP, TOPK], F32)
    bidx = sb(ctx, "tk_bidx", [P, HP, TOPK], U32)
    bidf = sb(ctx, "tk_bidf", [P, HP, TOPK], F32)
    tops = sb(ctx, "tk_tops", [P, HEADS, TOPK], F32)
    ci = sb(ctx, "tk_ci", [P, HEADS, TOPK], U32)
    cab = sb(ctx, "tk_cab", [P, 2, SEL], U32)
    cabf = sb(ctx, "tk_cabf", [P, 2, SEL], F32)
    sel = sb(ctx, "tk_sel", [P, 3, SEL], F32)
    ex = sb(ctx, "tk_ex", [P, HEADS, TOPK], F32)
    es = sb(ctx, "tk_es", [P, 2, HEADS], F32)
    spare = sb(ctx, "tk_spare", [P, 4], F32)
    rowf = sb(ctx, "tk_rowf", [P, 2, SEL], F32)
    SLOT_ROWS = SEL // (NK - PICKED)
    row = work[:, 0:2 * SLOT_ROWS * D].rearrange("p (r n) -> p r n", r=2 * SLOT_ROWS)
    xtok = sc[:, 0:D // NK, :].rearrange("p h n -> p (h n)")
    step_rows = sb(ctx, "u_step_rows", [P, 2, SLOT_ROWS], I32)
    dots = sb(ctx, "u_dots", [P, SLOT_ROWS], F32)
    zero = sb(ctx, "u_zero", [P, 1], F32)
    p_spare = sb(ctx, "u_spare", [P, 2], F32)
    row_in = [sems(f"u_row_in{r}") for r in range(2 * SLOT_ROWS)]
    zero_ok, step_ok, row_used, dot_ok = (sems(f"u_{n}") for n in (
        "zero_ok", "step_ok", "row_used", "dot_ok"))
    rest = work[:, 0:HP * NK].rearrange("p (h n) -> p h n", h=HP)
    crest = work[:, 0:HP * NK].rearrange("p (h n) -> p h n", h=HEADS)
    hit = work[:, :].rearrange("p (i k a) -> p i k a", i=2, k=SEL)
    cand = sc[:, :, :].rearrange("p (h a) n -> p h (a n)", a=2)

    picks = sb(ctx, "picks", [P, 2, T], BF16)
    gate = sb(ctx, "gate", [P, T], F32)
    parts = sb(ctx, "gate_parts", [P, 2, T], BF16)

    flat = scores[:, :, :, :].rearrange("p a h n -> p (a h n)")
    tile = flat[:, 0:2 * NK * GT].rearrange("p (u c t) -> p u c t", u=2, c=NK)
    hot = flat[:, 2 * NK * GT:2 * NK * GT + 2 * 4 * P * OCT // 2].bitcast(BF16).rearrange(
        "p (r n i t) -> p r n i t", r=2, n=4, i=P)
    at = 2 * NK * GT + 4 * P * OCT
    iota_x = flat[:, at:at + P * OCT // 2].bitcast(BF16).rearrange("p (i t) -> p i t", t=OCT)

    ge_st = [sems(f"ge_st{s}") for s in range(2)]
    g_st = [sems(f"g_st{s}") for s in range(2)]
    a_mm, a_ge = sems("a_mm"), sems("a_ge")
    sc_in, step, e_ok, tp, tp_ok = sems("tk_in"), sems("tk_step"), sems("tk_e_ok"), sems("tk_tp"), sems("tk_tp_ok")
    chosen, found = sems("tk_chosen"), sems("tk_found")
    iota_in, pre, two_hot, hot_ok, g_mm, g_ok = (sems(n) for n in (
        "iota_in", "g_pre", "two_hot", "hot_ok", "g_mm", "g_ok"))
    STEPS = 23
    CAND_DONE = 17
    EXP_IN = 19

    def slots(eng, pick, spread, between=None):
        for j in range(PICK):
            pick(j, j % 2, 0, j)
        with eng.Fori(1, TB) as n:
            for j in range(PICK):
                pick(PICK * n + j, j % 2, n, j)
        if between is not None:
            between()
        for j in range(LOOP):
            spread(PICKED + j, j % 2, 0, j)
        with eng.Fori(1, SPREAD // LOOP) as n:
            for j in range(LOOP):
                spread(LOOP * n + (PICKED + j), j % 2, n, j)
        with eng.Fori(0, ALONE // 2 - 1) as n:
            for j in range(2):
                pick(2 * n + (PICKED + SPREAD + j), j, None, n)
        for j in range(2):
            pick(NK - 2 + j, j, None, ALONE // 2 - 1)

    def half_pick(n, j):
        return j + (PICKED + SPREAD) // 2 if n is None else (PICK // 2) * n + j // 2

    def half_spread(n, j):
        return (LOOP // 2) * n + (PICKED // 2 + j // 2)

    def more(s):
        return not (isinstance(s, int) and s >= NK - 2)

    with nc.Block() as blk:
        @blk.sync
        def _(sp):
            def load(s, par):
                after(sp, u_lo, s - 1)
                ring.load(sp, par, u_t[ds(s, 1), :, :])

            def pick(s, par, n, j):
                if more(s):
                    load(s + 2, par)
                sp.wait_ge(a_ge, 2 * s + 2)
                sp.dma_start(acts[ds(s, 1), :, :].rearrange("a p n -> (a p) n"), ge[:, par, :]).then_inc(ge_st[par], 16)

            def spread(s, par, n, j):
                pick(s, par, n, j)
                if j % 2 == 1:
                    u = j // 2
                    sp.wait_ge(g_ok, 16 * n + (8 * u + 8))
                    sp.dma_start(gates[ds(2 * n + u, 1), :, :].rearrange("a p n -> (a p) n"),
                                 tile[:, u, :, :].rearrange("p c t -> p (c t)")).then_inc(g_st[u], 16)

            slots(sp, pick, spread)
            for par in range(2):
                sp.wait_ge(ge_st[par], 16 * NK // 2)
                sp.wait_ge(g_st[par], 16 * (SPREAD // LOOP))

        @blk.tensor
        def _(pe):
            def unit(s, par, h):
                after(pe, a_ge, 2 * s + (h - 3))
                cols = slice(GATHERED * P + h * DHALF, GATHERED * P + (h + 1) * DHALF)
                a = psum[:, 2 * par + h, 0:DHALF]
                for n in range(KC):
                    row = slice(n * P, (n + 1) * P)
                    pe.matmul(a, uh[:, par, row], xh[:, n, cols], start=(n == 0), stop=False)
                    pe.matmul(a, uh[:, par, row], xl[:, n, cols], start=False, stop=False)
                    last = pe.matmul(a, ul[:, par, row], xh[:, n, cols], start=False, stop=(n == KC - 1))
                last.then_inc(a_mm, 1)

            def pick(s, par, n, j):
                pe.wait_ge(u_hi, s + 1)
                pe.wait_ge(u_lo, s + 1)
                unit(s, par, 0)
                unit(s, par, 1)
                if n is not None and j == 1:
                    turn_selection(n)

            def turn_selection(n):
                if isinstance(n, int) and n == 0:
                    return
                pe.wait_ge(step, STEPS * n)
                pe.wait_ge(tp_ok, 2 * n)
                for i in range(3):
                    last = pe.transpose(psum[:, 7, i * P:(i + 1) * P], sel[:, i, :], ident)
                last.then_inc(tp, 1)

            def octet(n, o):
                r = o % 2
                pe.wait_ge(hot_ok, 8 * n + (o + 1))
                after(pe, g_ok, 16 * n + (2 * o - 2))
                for b in range(2):
                    for q in range(4):
                        t = 4 * b + q
                        for part in (2, 3):
                            last = pe.matmul(psum[:, 4 + 2 * r + b, q * P:(q + 1) * P], hot[:, r, 0, :, t],
                                             hot[:, r, part, :, t], start=(part == 2), stop=(part == 3))
                last.then_inc(g_mm, 1)

            def spread(s, par, n, j):
                pe.wait_ge(u_hi, s + 1)
                pe.wait_ge(u_lo, s + 1)
                for h in range(2):
                    unit(s, par, h)
                    octet(n, 2 * j + h)

            slots(pe, pick, spread, lambda: turn_selection(TB))

        @blk.scalar
        def _(act):
            def gelu(s, par, h, half):
                act.wait_ge(a_mm, 2 * s + (h + 1))
                if h == 0:
                    after(act, ge_st[par], 16 * half)
                act.activation(ge[:, par, h * DHALF:(h + 1) * DHALF], psum[:, 2 * par + h, 0:DHALF],
                               ACT.Gelu, scale=BACK).then_inc(a_ge, 1)

            def pick(s, par, n, j):
                if n is not None and j == 0:
                    after(act, step, STEPS * n - STEPS + CAND_DONE)
                    act.activation(sc[:, :, :], scores[:, ds(n, 1), :, :].rearrange("p a h n -> p (a h) n"),
                                   ACT.Copy).then_inc(sc_in, 1)
                half = half_pick(n, j)
                gelu(s, par, 0, half)
                gelu(s, par, 1, half)
                if more(s):
                    ring.high(act, par, half + 1)
                if n is not None and j == PICK - 3:
                    act.wait_ge(step, STEPS * n + EXP_IN)
                    act.activation(ex[:, :, :], ex[:, :, :], ACT.Exp).then_inc(e_ok, 1)
                if n is not None and j == 1:
                    keep_selection(n)

            def keep_selection(n):
                if isinstance(n, int) and n == 0:
                    return
                act.wait_ge(tp, n)
                act.activation(picks[:, :, ds(n * P - P, P)],
                               psum[:, 7, 0:2 * P].rearrange("p (a t) -> p a t", a=2), ACT.Copy).then_inc(tp_ok, 1)
                act.activation(gate[:, ds(n * P - P, P)], psum[:, 7, 2 * P:3 * P], ACT.Copy).then_inc(tp_ok, 1)

            def spread(s, par, n, j):
                half = half_spread(n, j)
                for h in range(2):
                    gelu(s, par, h, half)
                    o = 2 * j + h
                    u, r = o // 4, o % 2
                    act.wait_ge(g_mm, 8 * n + (o + 1))
                    if o % 4 == 0:
                        after(act, g_st[u], 16 * n)
                    for b in range(2):
                        at = OCT * (o % 4) + 4 * b
                        act.activation(tile[:, u, :, at:at + 4].rearrange("p c t -> p t c"),
                                       psum[:, 4 + 2 * r + b, :].rearrange("p (t c) -> p t c", t=4),
                                       ACT.Copy).then_inc(g_ok, 1)
                ring.high(act, par, half + 1)

            begin(act, [tp_ok], 2)
            slots(act, pick, spread, lambda: keep_selection(TB))

        @blk.gpsimd
        def _(pool):
            def pick(s, par, n, j):
                if n is None and more(s - 1):
                    gather(s - (PICKED - 1), 1 - par)
                if more(s):
                    ring.low(pool, par, s + 2)
                if n is not None and j == PICK - 3:
                    pool.wait_ge(chosen, n + 1)
                    for i in range(2):
                        for h in range(HEADS):
                            idx = bidf[:, 2 * h + i:2 * h + i + 1, :].to_broadcast([P, TOPK, TOPK])
                            a = hit[:, i, h * TOPK:(h + 1) * TOPK, :]
                            last = pool.tensor_tensor(a, a, idx, ALU.mult)
                    last.then_inc(found, 1)
            def gather(q, par):
                after(pool, step_ok, 2 * q)
                after(pool, row_used, SLOT_ROWS * q - SLOT_ROWS)
                pool.tensor_tensor(p_spare[:, 0:1], zero[:, :], zero[:, :], ALU.add)
                pool.tensor_copy(step_rows[:, par, :], rows[:, 0, ds(SLOT_ROWS * q, SLOT_ROWS)]).then_inc(step_ok, 1)
                pool.wait_ge(step_ok, 2 * q + 1)
                pool.tensor_tensor(p_spare[:, 1:2], zero[:, :], zero[:, :], ALU.add).then_inc(step_ok, 1)
                for j in range(SLOT_ROWS):
                    r = par * SLOT_ROWS + j
                    pool.indirect_dma_start(row[:, r, :], None, u_rows,
                                            IndirectOffsetOnAxis(step_rows[:, par, j:j + 1], 0)).then_inc(row_in[r], 16)

            def spread(s, par, n, j):
                gather(LOOP * n + (j + 1), (j + 1) % 2)
                ring.low(pool, par, s + 2)

            def load_iota():
                pool.wait_ge(sc_in, TB)
                pool.dma_start(iota_x, const_b[:, 0:P * OCT].rearrange("p (i t) -> p i t", t=OCT)).then_inc(iota_in, 16)
                pool.wait_ge(step, STEPS * TB)
                pool.dma_start(xtok, normed[0, :, :]).then_inc(iota_in, 16)
                gather(0, 0)

            pool.memset(zero[:, :], 0.0).then_inc(zero_ok, 1)
            pool.wait_ge(zero_ok, 1)
            slots(pool, pick, spread, load_iota)

        @blk.vector
        def _(dve):
            def search(n):
                done = [0]

                def then(ins):
                    done[0] += 1
                    ins.then_inc(step, 1)
                    dve.wait_ge(step, STEPS * n + done[0])
                    dve.memset(spare[:, 0:1], 0.0)

                def by_head(heads, works):
                    for w, work_of in enumerate(works):
                        for part in range(2):
                            if w > 0:
                                dve.wait_ge(step, STEPS * n + (done[0] - 1))
                                dve.memset(spare[:, 2 + part:3 + part], 0.0)
                            for h in range(part * heads // 2, (part + 1) * heads // 2):
                                last = work_of(h)
                            done[0] += 1
                            last.then_inc(step, 1)
                    dve.wait_ge(step, STEPS * n + done[0])
                    dve.memset(spare[:, 0:1], 0.0)

                dve.wait_ge(sc_in, n + 1)
                dve.memset(spare[:, 1:2], 0.0)
                by_head(HP, [
                    lambda h: dve.max(best[:, h, 0:8], sc[:, h, :]),
                    lambda h: (dve.match_replace(rest[:, h, :], best[:, h, 0:8], sc[:, h, :], NEG),
                               dve.max_index(bidx[:, h, 0:8], best[:, h, 0:8], sc[:, h, :]))[1],
                    lambda h: dve.max(best[:, h, 8:16], rest[:, h, :]),
                    lambda h: dve.max_index(bidx[:, h, 8:16], best[:, h, 8:16], rest[:, h, :])])
                two = best[:, :, :].rearrange("p (h a) k -> p h a k", a=2)
                a = two[:, :, 0:1, :].rearrange("p h a k -> p h k a").to_broadcast([P, HEADS, TOPK, TOPK])
                b = two[:, :, 1:2, :].to_broadcast([P, HEADS, TOPK, TOPK])
                dve.tensor_copy(bidf[:, :, :], bidx[:, :, :])
                then(dve.tensor_tensor(cand.rearrange("p h (a b) -> p h a b", a=TOPK), a, b, ALU.add))
                by_head(HEADS, [
                    lambda h: dve.max(tops[:, h, 0:8], cand[:, h, :]),
                    lambda h: (dve.match_replace(crest[:, h, :], tops[:, h, 0:8], cand[:, h, :], NEG),
                               dve.max_index(ci[:, h, 0:8], tops[:, h, 0:8], cand[:, h, :]))[1],
                    lambda h: dve.max(tops[:, h, 8:16], crest[:, h, :]),
                    lambda h: dve.max_index(ci[:, h, 8:16], tops[:, h, 8:16], crest[:, h, :])])
                assert done[0] == CAND_DONE
                cflat = ci[:, :, :].rearrange("p h k -> p (h k)")
                dve.tensor_scalar(cab[:, 0, :], cflat, 4, None, ALU.logical_shift_right)
                then(dve.tensor_scalar(cab[:, 1, :], cflat, TOPK - 1, None, ALU.bitwise_and))
                dve.tensor_copy(cabf[:, :, :], cab[:, :, :])
                then(dve.tensor_tensor(ex[:, :, :], tops[:, :, :],
                                       tops[:, :, 0:1].to_broadcast([P, HEADS, TOPK]), ALU.subtract))
                for i in range(2):
                    rank = cabf[:, i, :].rearrange("p (k a) -> p k a", a=1).to_broadcast([P, SEL, TOPK])
                    last = dve.tensor_tensor(hit[:, i, :, :], rank, iota16.rearrange(
                        "p (a k) -> p a k", a=1).to_broadcast([P, SEL, TOPK]), ALU.is_equal)
                last.then_inc(chosen, 1)
                dve.wait_ge(e_ok, n + 1)
                then(dve.reduce_sum(es[:, 0, :], ex[:, :, :], AX.X))
                then(dve.reciprocal(es[:, 1, :], es[:, 0, :]))
                after(dve, tp, n)
                then(dve.tensor_tensor(sel[:, 2, :].rearrange("p (h k) -> p h k", h=HEADS), ex[:, :, :],
                                       es[:, 1, :].rearrange("p (h a) -> p h a", a=1).to_broadcast(
                                           [P, HEADS, TOPK]), ALU.mult))
                dve.wait_ge(found, n + 1)
                then(dve.reduce_sum(sel[:, 0:2, :], hit[:, :, :, :], AX.X))
                assert done[0] == STEPS

            def octet(n, o):
                r = o % 2

                def per_token(ap):
                    return ap.rearrange("p (a t) -> p a t", a=1).to_broadcast([P, P, OCT])

                tokens = ds(8 * OCT * n + (OCT * o + GATHERED * P), OCT)
                after(dve, g_mm, 8 * n + (o - 1))
                dve.tensor_tensor(hot[:, r, 1, :, :], iota_x, per_token(picks[:, 1, tokens]),
                                  ALU.is_equal).then_inc(two_hot, 1)
                dve.tensor_tensor(hot[:, r, 0, :, :], iota_x, per_token(picks[:, 0, tokens]), ALU.is_equal)
                dve.wait_ge(two_hot, 8 * n + (o + 1))
                dve.tensor_tensor(hot[:, r, 2, :, :], hot[:, r, 1, :, :], per_token(parts[:, 0, tokens]), ALU.mult)
                dve.tensor_tensor(hot[:, r, 3, :, :], hot[:, r, 1, :, :], per_token(parts[:, 1, tokens]),
                                  ALU.mult).then_inc(hot_ok, 1)

            def keep(n):
                dve.tensor_copy(row_gate[:, n, :], sel[:, 2, :])
                for i in range(2):
                    last = dve.scalar_tensor_tensor(out=rowf[:, i, :], in0=sel[:, i, :], scalar=float(NK),
                                                    in1=sel[:, 1 - i, :], op0=ALU.mult, op1=ALU.add)
                last.then_inc(pre, 1)
                dve.wait_ge(pre, 2 * n + 1)
                dve.tensor_copy(rows[:, n, :], rowf[:, :, :].rearrange("p i k -> p (i k)")).then_inc(pre, 1)
                dve.wait_ge(pre, 2 * n + 2)

            for n in range(GATHERED):
                search(n)
                keep(n)
            with dve.Fori(GATHERED, TB) as n:
                search(n)
            dve.wait_ge(tp_ok, 2 * TB + 2)
            dve.wait_ge(iota_in, 32)
            dve.tensor_copy(parts[:, 0, :], gate[:, :]).then_inc(pre, 1)
            dve.wait_ge(pre, 2 * GATHERED + 1)
            dve.tensor_tensor(parts[:, 1, :], gate[:, :], parts[:, 0, :], ALU.subtract).then_inc(pre, 1)
            dve.wait_ge(pre, 2 * GATHERED + 2)

            def take(q, par, half):
                after(dve, dot_ok, q)
                for j in range(SLOT_ROWS):
                    r = par * SLOT_ROWS + j
                    dve.wait_ge(row_in[r], 16 * half + 16)
                    dve.scalar_tensor_tensor(out=row[:, r, :], in0=row[:, r, :], scalar=1.0, in1=xtok[:, :],
                                             op0=ALU.mult, op1=ALU.mult,
                                             accum_out=dots[:, j:j + 1]).then_inc(row_used, 1)
                dve.wait_ge(row_used, SLOT_ROWS * q + SLOT_ROWS)
                dve.tensor_copy(dot[:, 0, ds(SLOT_ROWS * q, SLOT_ROWS)], dots[:, :]).then_inc(dot_ok, 1)

            def turn(n):
                for j in range(LOOP):
                    octet(n, 2 * j)
                    octet(n, 2 * j + 1)
                    take(LOOP * n + j, j % 2, (LOOP // 2) * n + j // 2)

            turn(0)
            with dve.Fori(1, SPREAD // LOOP) as n:
                turn(n)
            with dve.Fori(SPREAD // 2, (NK - PICKED) // 2) as half:
                for par in range(2):
                    take(2 * half + par, par, half)


def combine(nc, ctx, sb, sems, psum, h_acc, region_y, buffers, u_rows, v_t, gates, acts, normed, rows,
            row_gate, dot, small, final_g, out):
    vf = buffers[0]
    vh = sb(ctx, "vh", [P, 2, CPG, D], BF16)
    vl = sb(ctx, "vl", [P, 2, CPG, D], BF16)
    gt = sb(ctx, "gt", [P, 2, TD // GT, CPG, GT], F32)
    at = sb(ctx, "at", [P, 2, CPG, TD], F32)
    wh = sb(ctx, "wh", [P, 2, CPG, TD], BF16)
    wl = sb(ctx, "wl", [P, 2, CPG, TD], BF16)
    O = 2 * DENSE
    NB = 6
    ONE, TWO = 2 * SEL // GROUPS, SEL // GROUPS
    BOTH = ONE + TWO
    more_rows = sb(ctx, "more_rows", [P, TWO - 2, D], F32)
    row = ([region_y[:, j, :] for j in range(ONE)] + [more_rows[:, j, :] for j in range(TWO - 2)]
           + [buffers[i][:, :, :].bitcast(F32).rearrange("p a n -> p (a n)") for i in (1, 2)])
    xtok = sb(ctx, "xtok", [P, D], F32)
    step_rows = sb(ctx, "step_rows", [P, BOTH], I32)
    dots = sb(ctx, "dots", [P, ONE], F32)
    weight = sb(ctx, "weight", [P, GATHERED, SEL], F32)
    step_w = sb(ctx, "step_w", [P, BOTH], F32)
    zero = sb(ctx, "zero", [P, 1], F32)
    spare = sb(ctx, "spare", [P, 2], F32)

    v_in = [sems(f"v_in{s}") for s in range(2)]
    g_in = [sems(f"gt_in{s}") for s in range(2)]
    a_in = [sems(f"at_in{s}") for s in range(2)]
    v_hi, v_lo, w_ok, w_hi, w_lo = (sems(n) for n in ("v_hi", "v_lo", "gw_ok", "gw_hi", "gw_lo"))
    y_mm, y_ok = sems("y_mm"), sems("y_ok")
    row_in = [sems(f"row_in{j}") for j in range(BOTH)]
    xtok_in, zero_ok, step_ok, row_used, dot_ok, gelu_ok, weight_ok, step_w_ok = (sems(n) for n in (
        "xtok_in", "zero_ok", "step_ok", "row_used", "dot_ok", "gelu_ok", "weight_ok", "step_w_ok"))

    TILES = [*range(GATHERED, TB), *range(GATHERED)]
    ss, rms, rstd = (small[:, TB * i:TB * (i + 1)] for i in range(3))
    sq_ok, rms_ok, rs_ok, o_ok, stored = (sems(f"f_{n}") for n in ("sq", "rms", "rs", "out", "stored"))
    ORDER = [j for i in range(TWO) for j in (2 * i, 2 * i + 1, ONE + i)]
    assert len(ORDER) == BOTH == O and ONE == 2 * TWO
    def is_first(g):
        return isinstance(g, int) and g == 0

    def split_order(g):
        order = [(what, c) for c in range(CPG) for what in ("v", "w")]
        return sorted(order, key=lambda o: o[0]) if is_first(g) else order

    v_rows = v_t.rearrange("c p n -> (c p) n")

    def groups(eng, body, between=None):
        body(0, 0, 0, True)
        body(1, 1, 0, True)
        with eng.Fori(1, GROUPS // 4) as i:
            body(2 * i, 0, i, True)
            body(2 * i + 1, 1, i, True)
        body(GROUPS // 2, 0, GROUPS // 4, False)
        body(GROUPS // 2 + 1, 1, GROUPS // 4, False)
        if between is not None:
            between()
        with eng.Fori(GROUPS // 4 + 1, GROUPS // 2) as i:
            body(2 * i, 0, i, False)
            body(2 * i + 1, 1, i, False)

    with nc.Block() as blk:
        @blk.sync
        def _(sp):
            def column(g, c):
                after(sp, v_lo, CPG * g + (c - 1))
                sp.dma_start(vf[:, c % 2, :], v_t[ds(CPG * g + c, 1), :, :].rearrange(
                    "a p n -> (a p) n")).then_inc(v_in[c % 2], 16)

            def body(g, par, half, of_u):
                if is_first(g):
                    column(g, 0)
                    column(g, 1)
                after(sp, w_lo, CPG * g - CPG)
                sp.dma_start(gt[:, par, :, :, :].rearrange("p b c t -> p b (c t)"),
                             gates.rearrange("b p (g n) -> g p b n", g=GROUPS)[ds(g, 1), :, :, :].rearrange(
                                 "g p b n -> (g p) b n")).then_inc(g_in[par], 16)
                sp.dma_start(at[:, par, :, :], acts.rearrange("(g c) p n -> g p c n", g=GROUPS)[
                    ds(g, 1), :, :, :].rearrange("g p c n -> (g p) c n")).then_inc(a_in[par], 16)
                for c in range(2 if is_first(g) else 0, CPG):
                    column(g, c)
                if is_first(g):
                    sp.dma_start(xtok[:, :], normed[1, :, :]).then_inc(xtok_in, 16)

            groups(sp, body)
            sp.wait_ge(dot_ok, GROUPS // 2)
            sp.dma_start(xtok[:, :], final_g).then_inc(xtok_in, 16)
            for i, t in enumerate(TILES):
                sp.wait_ge(o_ok, i + 1)
                sp.dma_start(out[t * P:(t + 1) * P, :], h_acc[:, t, :]).then_inc(stored, 16)
            sp.wait_ge(stored, 16 * TB)

        @blk.tensor
        def _(pe):
            def body(g, par, half, of_u):
                pe.wait_ge(v_lo, CPG * g + CPG)
                pe.wait_ge(w_lo, CPG * g + CPG)
                for o in range(O):
                    rows, cols = slice((o // 2) * P, (o // 2 + 1) * P), slice((o % 2) * HALF, (o % 2 + 1) * HALF)
                    after(pe, y_ok, O * g + (o + 1 - NB))
                    a = psum[:, o % NB, :]
                    for c in range(CPG):
                        pe.matmul(a, wh[:, par, c, rows], vh[:, par, c, cols], start=(c == 0), stop=False)
                        pe.matmul(a, wh[:, par, c, rows], vl[:, par, c, cols], start=False, stop=False)
                        last = pe.matmul(a, wl[:, par, c, rows], vh[:, par, c, cols], start=False,
                                         stop=(c == CPG - 1))
                    last.then_inc(y_mm, 1)

            groups(pe, body)

        @blk.scalar
        def _(act):
            def body(g, par, half, of_u):
                after(act, y_mm, O * g - O)
                for what, c in split_order(g):
                    if what == "v":
                        act.wait_ge(v_in[c % 2], 2 * 16 * g + (16 * (c // 2) + 16))
                        act.activation(vh[:, par, c, :], vf[:, c % 2, :], ACT.Copy).then_inc(v_hi, 1)
                    else:
                        act.wait_ge(w_ok, CPG * g + (c + 1))
                        act.activation(wh[:, par, c, :], at[:, par, c, :], ACT.Copy).then_inc(w_hi, 1)

            def activate():
                act.wait_ge(dot_ok, GROUPS // 2)
                act.activation(dot[:, 1, :], dot[:, 1, :], ACT.Gelu, scale=1.0 / XS).then_inc(gelu_ok, 1)

            act.activation(dot[:, 0, :], dot[:, 0, :], ACT.Gelu, scale=1.0 / XS).then_inc(gelu_ok, 1)
            groups(act, body, activate)
            for i, t in enumerate(TILES):
                if t >= GATHERED:
                    act.wait_ge(y_ok, O * (GROUPS - 1) + 2 * (t - GATHERED) + 2)
                else:
                    act.wait_ge(row_used, BOTH * GROUPS)
                act.activation((vh if i % 2 else vl)[:, 0, i // 2, :], h_acc[:, t, :], ACT.Square,
                               accum_out=ss[:, t:t + 1]).then_inc(sq_ok, 1)
                act.wait_ge(sq_ok, i + 1)
                act.activation(rms[:, t:t + 1], ss[:, t:t + 1], ACT.Sqrt, scale=1.0 / D,
                               bias=EPS).then_inc(rms_ok, 1)

        @blk.gpsimd
        def _(pool):
            def body(g, par, half, of_u):
                for what, c in split_order(g):
                    if what == "v":
                        pool.wait_ge(v_hi, CPG * g + (c + 1))
                        pool.tensor_tensor(vl[:, par, c, :], vf[:, c % 2, :], vh[:, par, c, :],
                                           ALU.subtract).then_inc(v_lo, 1)
                    else:
                        pool.wait_ge(w_hi, CPG * g + (c + 1))
                        pool.tensor_tensor(wl[:, par, c, :], at[:, par, c, :], wh[:, par, c, :],
                                           ALU.subtract).then_inc(w_lo, 1)
                after(pool, step_ok, 2 * g)
                after(pool, row_used, BOTH * g)
                pool.tensor_tensor(spare[:, 0:1], zero[:, :], zero[:, :], ALU.add)
                pool.tensor_copy(step_rows[:, 0:ONE], rows[:, 1, ds(ONE * g, ONE)])
                pool.tensor_copy(step_rows[:, ONE:BOTH], rows[:, 0, ds(TWO * g + SEL, TWO)]).then_inc(step_ok, 1)
                pool.wait_ge(step_ok, 2 * g + 1)
                pool.tensor_tensor(spare[:, 1:2], zero[:, :], zero[:, :], ALU.add).then_inc(step_ok, 1)
                for j in ORDER:
                    pool.indirect_dma_start(row[j], None, u_rows if of_u and j < ONE else v_rows,
                                            IndirectOffsetOnAxis(step_rows[:, j:j + 1], 0)).then_inc(row_in[j], 16)

            pool.memset(zero[:, :], 0.0).then_inc(zero_ok, 1)
            pool.wait_ge(zero_ok, 1)
            groups(pool, body)

        @blk.vector
        def _(dve):
            def weigh(g, par, half):
                dve.wait_ge(g_in[par], 16 * half + 16)
                dve.wait_ge(a_in[par], 16 * half + 16)
                for c in range(CPG):
                    a = at[:, par, c, :].rearrange("p (b t) -> p b t", t=GT)
                    dve.tensor_tensor(a, a, gt[:, par, :, c, :], ALU.mult).then_inc(w_ok, 1)

            def take(g, i, of_u):
                j = ORDER[i]
                after(dve, row_used, BOTH * g + i)
                dve.wait_ge(row_in[j], 16 * g + 16)
                if of_u and j < ONE:
                    dve.scalar_tensor_tensor(out=row[j], in0=row[j], scalar=1.0, in1=xtok[:, :], op0=ALU.mult,
                                             op1=ALU.mult, accum_out=dots[:, j:j + 1]).then_inc(row_used, 1)
                else:
                    a = h_acc[:, 1 if j < ONE else 0, :]
                    dve.scalar_tensor_tensor(out=a, in0=row[j], scalar=step_w[:, j:j + 1], in1=a,
                                             op0=ALU.mult, op1=ALU.add).then_inc(row_used, 1)

            def finish(i):
                t = TILES[i]
                dve.wait_ge(rms_ok, i + 1)
                dve.reciprocal(rstd[:, t:t + 1], rms[:, t:t + 1]).then_inc(rs_ok, 1)
                dve.wait_ge(rs_ok, i + 1)
                dve.scalar_tensor_tensor(out=h_acc[:, t, :], in0=h_acc[:, t, :], scalar=rstd[:, t:t + 1],
                                         in1=xtok[:, :], op0=ALU.mult, op1=ALU.mult).then_inc(o_ok, 1)

            def add(g, of_u):
                after(dve, row_used, BOTH * g)
                if not of_u:
                    dve.tensor_copy(step_w[:, 0:ONE], weight[:, 1, ds(ONE * g - SEL, ONE)])
                dve.tensor_copy(step_w[:, ONE:BOTH], weight[:, 0, ds(TWO * g, TWO)]).then_inc(step_w_ok, 1)
                dve.wait_ge(step_w_ok, g + 1)
                if of_u:
                    after(dve, dot_ok, g)
                for o in range(O):
                    dve.wait_ge(y_mm, O * g + (o + 1))
                    after(dve, y_ok, O * g + (o + 1 - O))
                    a = h_acc[:, GATHERED + o // 2, (o % 2) * HALF:(o % 2 + 1) * HALF]
                    dve.tensor_tensor(a, a, psum[:, o % NB, :], ALU.add).then_inc(y_ok, 1)
                    take(g, o, of_u)
                    if isinstance(g, int) and g == GROUPS - 1 and o % 2 == 1 and o >= 5:
                        finish(o // 2 - 2)
                if of_u:
                    dve.wait_ge(row_used, BOTH * g + BOTH)
                    dve.tensor_copy(dot[:, 1, ds(ONE * g, ONE)], dots[:, :]).then_inc(dot_ok, 1)

            def weights(i):
                dve.wait_ge(gelu_ok, i + 1)
                dve.tensor_tensor(weight[:, i, :], dot[:, i, :], row_gate[:, i, :], ALU.mult).then_inc(weight_ok, 1)
                dve.wait_ge(weight_ok, i + 1)

            weights(0)
            dve.wait_ge(xtok_in, 16)
            weigh(0, 0, 0)
            weigh(1, 1, 0)
            add(0, True)
            with dve.Fori(1, GROUPS // 4) as i:
                weigh(2 * i, 0, i)
                add(2 * i - 1, True)
                weigh(2 * i + 1, 1, i)
                add(2 * i, True)
            weigh(GROUPS // 2, 0, GROUPS // 4)
            add(GROUPS // 2 - 1, True)
            weigh(GROUPS // 2 + 1, 1, GROUPS // 4)
            weights(1)
            add(GROUPS // 2, False)
            with dve.Fori(GROUPS // 4 + 1, GROUPS // 2) as i:
                weigh(2 * i, 0, i)
                add(2 * i - 1, False)
                weigh(2 * i + 1, 1, i)
                add(2 * i, False)
            dve.wait_ge(xtok_in, 32)
            add(GROUPS - 1, False)
            for i in range(DENSE - 2, TB):
                finish(i)



def _layout(i):
    import numpy as np

    f = np.float32
    c = np.ascontiguousarray
    eye = np.eye(P, dtype=f)
    groups = np.kron(np.eye(P // GROUP, dtype=f), np.full((GROUP, GROUP), 1.0 / GROUP, f))
    belongs = np.zeros((NSTAT, 2 * CG, P), f)
    for n in range(2 * CG):
        belongs[n, n // 2, (n % 2) * GROUP:(n % 2 + 1) * GROUP] = 1.0
    for n in range(CG):
        belongs[2 * CG + n, CG + n] = 1.0
    size = np.full((NSTAT, 1, 1), GROUP, f)
    size[2 * CG:] = P
    stat = (belongs / size).transpose(2, 1, 0).reshape(P, 2 * CG * NSTAT)
    iota16 = np.broadcast_to(np.arange(TOPK, dtype=f), (P, TOPK))
    restart = np.ones((P, T), f)
    restart[:, ::CHUNK] = 0.0
    iota = np.broadcast_to(np.repeat(np.arange(P, dtype=f), 8), (P, P * 8))
    s, t = np.arange(P)[:, None], np.arange(P)[None, :]
    masks = []
    for level in range(LEVELS):
        n = CHUNK >> level
        masks.append((s // n == t // n) & (s % n < n // 2) & (t % n >= n // 2))
    masks.append(s == t)
    cols = lambda v, n: np.asarray(v, f).reshape(n, P).T
    w_in = np.asarray(i["w_in"])[0].reshape(KC, P, 6, CG, P)
    stream = w_in[:, :, [1, 0, 3, 2, 5]].transpose(2, 3, 1, 0, 4).reshape(5 * CG, P, D)
    w_v = w_in[:, :, 4].reshape(KC // 2, 2, P, HALF).transpose(0, 2, 1, 3).reshape(KC // 2, P, D)
    conv_w = np.asarray(i["conv_w"])[0].T.reshape(CG, P, TAPS).transpose(1, 0, 2).reshape(P, CG * TAPS)
    params = np.concatenate([
        conv_w, cols(i["conv_b"], CG),
        cols(i["conv_norm_g"], CG), cols(i["conv_norm_b"], CG), cols(i["hgrn_norm_g"], CG),
        cols(np.asarray(i["hgrn_lb_logits"])[0], CG), cols(np.asarray(i["hgrn_lb_logits"])[1], CG)], axis=1)
    return {
        "x": c(np.asarray(i["x"]).reshape(T, D)),
        "const_f": c(np.concatenate([eye, groups, stat, iota16], axis=1)),
        "const_b": c(np.concatenate([iota, restart], axis=1)),
        "const_m": c(np.concatenate(masks, axis=1).astype(np.int32)),
        "const_e": c(belongs.reshape(NSTAT, 2 * CG * P)),
        "params": c(params),
        "mix_g": c(np.broadcast_to(np.asarray(i["norm_mix_g"])[0], (P, D))),
        "ffn_g": c(np.broadcast_to(np.asarray(i["norm_ffn_g"])[0], (P, D))),
        "w_stream": c(stream),
        "w_v": c(w_v),
        "w_out": c(np.asarray(i["w_out"])[0]),
        "w_q": c(np.asarray(i["peer_w_query"])[0].reshape(KC, P, HP, P).transpose(2, 1, 0, 3).reshape(HP, P, D)),
        "keys": c(np.asarray(i["peer_sub_keys"])[0].reshape(HP, NK, P).transpose(2, 0, 1)),
        "u_t": c(np.asarray(i["peer_u"])[0].reshape(NK, NK, KC, P).transpose(1, 3, 2, 0).reshape(NK, P, D)),
        "u_rows": c(np.asarray(i["peer_u"])[0]),
        "v_t": c(np.asarray(i["peer_v"])[0].reshape(NK, NK, D).transpose(1, 0, 2)),
        "final_g": c(np.broadcast_to(np.asarray(i["final_norm_g"]), (P, D))),
    }


def kernel(**inputs):
    import numpy as np
    import concourse.bacc as bacc
    from concourse.bass_utils import run_bass_kernel_spmd as run

    nc = bacc.Bacc("TRN2", target_bir_lowering=False, num_devices=1)
    arrays = {f"in_{n}_dram": a for n, a in _layout(inputs).items()}
    args = [nc.dram_tensor(n, a.shape, mybir.dt.from_np(a.dtype), kind="ExternalInput").ap()
            for n, a in arrays.items()]
    args.append(nc.dram_tensor("out_0_dram", (T, D), F32, kind="ExternalOutput").ap())
    args.append(nc.dram_tensor("gates_dram", (TD // GT, P, NK * GT), F32, kind="Internal").ap())
    args.append(nc.dram_tensor("acts_dram", (NK, P, TD), F32, kind="Internal").ap())
    args.append(nc.dram_tensor("normed_dram", (GATHERED, P, D), F32, kind="Internal").ap())
    hybrid_block(nc, *args)
    r = run(nc, [arrays], core_ids=[0])
    return np.asarray(r.results[0]["out_0_dram"]).reshape(1, T, D)
```
